# Optimizing a Trainium2 kernel written in Bass

```python
import math
import jax
import jax.numpy as jnp
from jax import lax
import numpy as np

D_MODEL = 1024
BATCH = 1
SEQ = 128
DEPTH = 2
DEC_BATCH = 1
DEC_SEQ = 256
PAST_LEN = 128

GRID_W = 64
Q_BLOCK = 128
ROPE_THETA = 10000.0
RMS_EPS = 1e-6
LN_EPS = 1e-5

CONV_CH = D_MODEL // 2
CONV_WIDTH = 31
CONV_PAD = CONV_WIDTH // 2
HEAD_DIM = 64
GQA_HEADS = (D_MODEL // 2) // HEAD_DIM
GQA_KV_HEADS = 2
GQA_GROUP = GQA_HEADS // GQA_KV_HEADS
EVEN_SPLITS = [2 * CONV_CH, 2 * CONV_CH + GQA_HEADS * HEAD_DIM, 2 * CONV_CH + (GQA_HEADS + GQA_KV_HEADS) * HEAD_DIM]
EVEN_IN = 2 * CONV_CH + (GQA_HEADS + 2 * GQA_KV_HEADS) * HEAD_DIM
EVEN_OUT = CONV_CH + GQA_HEADS * HEAD_DIM

DIFF_HD = 64
DIFF_HEADS = (D_MODEL // 2) // (2 * DIFF_HD)
DIFF_W = DIFF_HEADS * 2 * DIFF_HD
LAMBDA_INIT = 0.8 - 0.6 * math.exp(-0.3 * 1)
MLA_HEADS = 8
MLA_NOPE = 64
MLA_ROPE = 32
MLA_QK = MLA_NOPE + MLA_ROPE
MLA_V = 64
MLA_Q_RANK = 256
MLA_KV_RANK = 128
ODD_SPLITS = [DIFF_W, 2 * DIFF_W, 3 * DIFF_W, 3 * DIFF_W + MLA_Q_RANK, 3 * DIFF_W + MLA_Q_RANK + MLA_KV_RANK]
ODD_IN = 3 * DIFF_W + MLA_Q_RANK + MLA_KV_RANK + MLA_ROPE
ODD_OUT = DIFF_W + MLA_HEADS * MLA_V

D_FF = 2816
N_EXPERTS = 8
MOE_TOP_K = 2
D_FF_EXPERT = 1408

kernel_name = "hybrid_diffusion_prefix_trunk_step"

def rms_norm(x, g):
    xf = x.astype(jnp.float32)
    y = xf * lax.rsqrt(jnp.mean(xf * xf, axis=-1, keepdims=True) + RMS_EPS)
    return (y * g.astype(jnp.float32)).astype(x.dtype)

def layer_norm(x, g, b):
    xf = x.astype(jnp.float32)
    mu = jnp.mean(xf, axis=-1, keepdims=True)
    var = jnp.mean(jnp.square(xf - mu), axis=-1, keepdims=True)
    y = (xf - mu) * lax.rsqrt(var + LN_EPS)
    return (y * g.astype(jnp.float32) + b.astype(jnp.float32)).astype(x.dtype)

def axial_rope_tables(n, rot_dim):
    rows = n // GRID_W
    row = jnp.repeat(jnp.arange(rows, dtype=jnp.int32), GRID_W).astype(jnp.float32)
    col = jnp.tile(jnp.arange(GRID_W, dtype=jnp.int32), rows).astype(jnp.float32)
    nf = rot_dim // 4
    inv = ROPE_THETA ** (-jnp.arange(nf, dtype=jnp.float32) / nf)
    ang = jnp.concatenate([row[:, None] * inv, col[:, None] * inv], axis=-1)
    return jnp.cos(ang), jnp.sin(ang)

def apply_rope(x, cos, sin):
    shape = (1, cos.shape[0]) + (1,) * (x.ndim - 3) + (cos.shape[1],)
    c = cos.reshape(shape).astype(x.dtype)
    s = sin.reshape(shape).astype(x.dtype)
    x1, x2 = jnp.split(x, 2, axis=-1)
    return jnp.concatenate([x1 * c - x2 * s, x2 * c + x1 * s], axis=-1)

def attend(q, k, v):
    B, Sq, Hk, G, dk = q.shape
    dv = v.shape[-1]
    nb = Sq // Q_BLOCK
    scale = dk ** -0.5
    qb = q.reshape(B, nb, Q_BLOCK, Hk, G, dk).transpose(1, 0, 2, 3, 4, 5)

    def one_block(qblk):
        s = jnp.einsum("bqhgd,bkhd->bhgqk", qblk, k).astype(jnp.float32) * scale
        p = jax.nn.softmax(s, axis=-1).astype(v.dtype)
        return jnp.einsum("bhgqk,bkhd->bqhgd", p, v)

    o = lax.map(one_block, qb)
    return o.transpose(1, 0, 2, 3, 4, 5).reshape(B, Sq, Hk, G, dv)

def conformer_conv(u, dw_w, dw_b, ln_g, ln_b):
    a, b = jnp.split(u, 2, axis=-1)
    g = a * jax.nn.sigmoid(b)
    y = lax.conv_general_dilated(g, dw_w[:, None, :].astype(g.dtype), (1,), [(CONV_PAD, CONV_PAD)],
                                 dimension_numbers=("NWC", "WIO", "NWC"), feature_group_count=CONV_CH)
    y = layer_norm(y + dw_b, ln_g, ln_b)
    return jax.nn.silu(y)

def mixer_even(h, p, ctx):
    w_in, dw_w, dw_b, ln_g, ln_b, q_g, k_g, w_out = p
    B, S, _ = h.shape
    z = h @ w_in
    u, q, k, v = jnp.split(z, EVEN_SPLITS, axis=-1)
    conv = conformer_conv(u, dw_w, dw_b, ln_g, ln_b)
    q = rms_norm(q.reshape(B, S, GQA_KV_HEADS, GQA_GROUP, HEAD_DIM), q_g)
    k = rms_norm(k.reshape(B, S, GQA_KV_HEADS, HEAD_DIM), k_g)
    v = v.reshape(B, S, GQA_KV_HEADS, HEAD_DIM)
    if ctx is None:
        state = (k, v)
        k_all, v_all = k, v
    else:
        state = None
        cos, sin = axial_rope_tables(S, HEAD_DIM)
        q = apply_rope(q, cos, sin)
        k = apply_rope(k, cos, sin)
        k_all = jnp.concatenate([k, ctx[0]], axis=1)
        v_all = jnp.concatenate([v, ctx[1]], axis=1)
    a = attend(q, k_all, v_all).reshape(B, S, GQA_HEADS * HEAD_DIM)
    return jnp.concatenate([conv, a], axis=-1) @ w_out, state

def mla_keys(ckv, kr, w_kvb, k_g, rope):
    B, S, _ = ckv.shape
    kv = (ckv @ w_kvb).reshape(B, S, MLA_HEADS, MLA_NOPE + MLA_V)
    k_nope, v = jnp.split(kv, [MLA_NOPE], axis=-1)
    k = jnp.concatenate([k_nope, jnp.broadcast_to(kr[:, :, None, :], (B, S, MLA_HEADS, MLA_ROPE))], axis=-1)
    k = rms_norm(k, k_g)
    if rope is not None:
        k = jnp.concatenate([k[..., :MLA_NOPE], apply_rope(k[..., MLA_NOPE:], rope[0], rope[1])], axis=-1)
    return k, v

def mixer_odd(h, p, ctx):
    (w_in, dq_g, dk_g, lq1, lk1, lq2, lk2, sub_g,
     qa_g, w_qb, kva_g, w_kvb, mq_g, mk_g, w_out) = p
    B, S, _ = h.shape
    z = h @ w_in
    dq, dk, dv, qa, kva, kr = jnp.split(z, ODD_SPLITS, axis=-1)
    dq = rms_norm(dq.reshape(B, S, DIFF_HEADS, 2, DIFF_HD), dq_g)
    dk = rms_norm(dk.reshape(B, S, DIFF_HEADS, 2, DIFF_HD), dk_g)
    dv = dv.reshape(B, S, DIFF_HEADS, 2 * DIFF_HD)
    ckv = rms_norm(kva, kva_g)
    q = rms_norm((rms_norm(qa, qa_g) @ w_qb).reshape(B, S, MLA_HEADS, MLA_QK), mq_g)
    if ctx is None:
        state = (dk, dv, ckv, kr)
        k_d, v_d = dk, dv
        k_m, v_m = mla_keys(ckv, kr, w_kvb, mk_g, None)
    else:
        state = None
        c_dk, c_dv, c_ckv, c_kr = ctx
        cos, sin = axial_rope_tables(S, DIFF_HD)
        dq = apply_rope(dq, cos, sin)
        dk = apply_rope(dk, cos, sin)
        cos_r, sin_r = axial_rope_tables(S, MLA_ROPE)
        q = jnp.concatenate([q[..., :MLA_NOPE], apply_rope(q[..., MLA_NOPE:], cos_r, sin_r)], axis=-1)
        k_lat, v_lat = mla_keys(ckv, kr, w_kvb, mk_g, (cos_r, sin_r))
        k_ctx, v_ctx = mla_keys(c_ckv, c_kr, w_kvb, mk_g, None)
        k_d = jnp.concatenate([dk, c_dk], axis=1)
        v_d = jnp.concatenate([dv, c_dv], axis=1)
        k_m = jnp.concatenate([k_lat, k_ctx], axis=1)
        v_m = jnp.concatenate([v_lat, v_ctx], axis=1)
    f32 = jnp.float32
    lam = (jnp.exp(jnp.sum(lq1.astype(f32) * lk1.astype(f32))) - jnp.exp(jnp.sum(lq2.astype(f32) * lk2.astype(f32)))
           + LAMBDA_INIT)
    o1 = attend(dq[:, :, :, 0:1], k_d[:, :, :, 0], v_d)
    o2 = attend(dq[:, :, :, 1:2], k_d[:, :, :, 1], v_d)
    od = rms_norm((o1 - lam.astype(o1.dtype) * o2)[:, :, :, 0], sub_g) * (1.0 - LAMBDA_INIT)
    om = attend(q[:, :, :, None], k_m, v_m)[:, :, :, 0]
    o = jnp.concatenate([od.reshape(B, S, DIFF_W), om.reshape(B, S, MLA_HEADS * MLA_V)], axis=-1)
    return o @ w_out, state

def swiglu(h, w1, w3, w2):
    return (jax.nn.silu(h @ w1) * (h @ w3)) @ w2

def moe_swiglu(h, router_w, w1, w3, w2):
    logits = (h @ router_w).astype(jnp.float32)
    top_v, top_i = lax.top_k(logits, MOE_TOP_K)
    gates = jax.nn.softmax(top_v, axis=-1)
    combine = jnp.sum(jax.nn.one_hot(top_i, N_EXPERTS, dtype=jnp.float32) * gates[..., None], axis=-2).astype(h.dtype)
    y = jnp.zeros_like(h)
    for e in range(N_EXPERTS):
        y = y + combine[..., e:e + 1] * swiglu(h, w1[e], w3[e], w2[e])
    return y

def run_layer(l, x, cond, shared, mix_p, ffn_p, ctx):
    ada_w, ada_b, n1_g, n2_g = shared
    m = jax.nn.silu(cond) @ ada_w + ada_b
    sh1, sc1, g1, sh2, sc2, g2 = jnp.split(m[:, None, :], 6, axis=-1)
    h = rms_norm(x, n1_g) * (1.0 + sc1) + sh1
    if l % 2 == 0:
        o, state = mixer_even(h, mix_p, ctx)
    else:
        o, state = mixer_odd(h, mix_p, ctx)
    x = x + g1 * o
    h = rms_norm(x, n2_g) * (1.0 + sc2) + sh2
    f = swiglu(h, *ffn_p) if l % 2 == 0 else moe_swiglu(h, *ffn_p)
    return x + g2 * f, state

def setup_inputs(seed: int = 0) -> dict:
    key = jax.random.key(seed)
    keys = iter(jax.random.split(key, 64))
    f32 = jnp.float32

    def nrm(shape, scale=1.0):
        return jax.random.normal(next(keys), shape, f32) * scale

    def gain(n):
        return 1.0 + nrm((n,), 0.02)

    D = D_MODEL
    return {
        "x_prompt": nrm((BATCH, SEQ, D)),
        "x_sample": nrm((DEC_BATCH, DEC_SEQ, D)),
        "cache_l0_gqa_k": nrm((DEC_BATCH, PAST_LEN, GQA_KV_HEADS, HEAD_DIM)),
        "cache_l0_gqa_v": nrm((DEC_BATCH, PAST_LEN, GQA_KV_HEADS, HEAD_DIM)),
        "cache_l1_diff_k": nrm((DEC_BATCH, PAST_LEN, DIFF_HEADS, 2, DIFF_HD)),
        "cache_l1_diff_v": nrm((DEC_BATCH, PAST_LEN, DIFF_HEADS, 2 * DIFF_HD)),
        "cache_l1_mla_ckv": nrm((DEC_BATCH, PAST_LEN, MLA_KV_RANK)),
        "cache_l1_mla_krope": nrm((DEC_BATCH, PAST_LEN, MLA_ROPE)),
        "c": nrm((DEC_BATCH, D)),
        "c_ctx": nrm((D,)),
        "l0_ada_w": nrm((D, 6 * D), 0.5 * D ** -0.5),
        "l0_ada_b": nrm((6 * D,), 0.02),
        "l0_norm1_g": gain(D),
        "l0_norm2_g": gain(D),
        "l0_w_in": nrm((D, EVEN_IN), D ** -0.5),
        "l0_conv_dw_w": nrm((CONV_WIDTH, CONV_CH), CONV_WIDTH ** -0.5),
        "l0_conv_dw_b": nrm((CONV_CH,), 0.02),
        "l0_conv_ln_g": gain(CONV_CH),
        "l0_conv_ln_b": nrm((CONV_CH,), 0.02),
        "l0_q_norm_g": gain(HEAD_DIM),
        "l0_k_norm_g": gain(HEAD_DIM),
        "l0_w_out": nrm((EVEN_OUT, D), EVEN_OUT ** -0.5),
        "l0_ffn_w1": nrm((D, D_FF), D ** -0.5),
        "l0_ffn_w3": nrm((D, D_FF), D ** -0.5),
        "l0_ffn_w2": nrm((D_FF, D), D_FF ** -0.5),
        "l1_ada_w": nrm((D, 6 * D), 0.5 * D ** -0.5),
        "l1_ada_b": nrm((6 * D,), 0.02),
        "l1_norm1_g": gain(D),
        "l1_norm2_g": gain(D),
        "l1_w_in": nrm((D, ODD_IN), D ** -0.5),
        "l1_diff_q_norm_g": gain(DIFF_HD),
        "l1_diff_k_norm_g": gain(DIFF_HD),
        "l1_lambda_q1": nrm((DIFF_HD,), 0.1),
        "l1_lambda_k1": nrm((DIFF_HD,), 0.1),
        "l1_lambda_q2": nrm((DIFF_HD,), 0.1),
        "l1_lambda_k2": nrm((DIFF_HD,), 0.1),
        "l1_diff_subln_g": gain(2 * DIFF_HD),
        "l1_mla_q_a_norm_g": gain(MLA_Q_RANK),
        "l1_mla_w_qb": nrm((MLA_Q_RANK, MLA_HEADS * MLA_QK), MLA_Q_RANK ** -0.5),
        "l1_mla_kv_a_norm_g": gain(MLA_KV_RANK),
        "l1_mla_w_kvb": nrm((MLA_KV_RANK, MLA_HEADS * (MLA_NOPE + MLA_V)), MLA_KV_RANK ** -0.5),
        "l1_mla_q_norm_g": gain(MLA_QK),
        "l1_mla_k_norm_g": gain(MLA_QK),
        "l1_w_out": nrm((ODD_OUT, D), ODD_OUT ** -0.5),
        "l1_router_w": nrm((D, N_EXPERTS), D ** -0.5),
        "l1_moe_w1": nrm((N_EXPERTS, D, D_FF_EXPERT), D ** -0.5),
        "l1_moe_w3": nrm((N_EXPERTS, D, D_FF_EXPERT), D ** -0.5),
        "l1_moe_w2": nrm((N_EXPERTS, D_FF_EXPERT, D), D_FF_EXPERT ** -0.5),
    }

def reference(x_prompt, x_sample, cache_l0_gqa_k, cache_l0_gqa_v, cache_l1_diff_k, cache_l1_diff_v,
              cache_l1_mla_ckv, cache_l1_mla_krope, c, c_ctx,
              l0_ada_w, l0_ada_b, l0_norm1_g, l0_norm2_g, l0_w_in, l0_conv_dw_w, l0_conv_dw_b,
              l0_conv_ln_g, l0_conv_ln_b, l0_q_norm_g, l0_k_norm_g, l0_w_out, l0_ffn_w1, l0_ffn_w3, l0_ffn_w2,
              l1_ada_w, l1_ada_b, l1_norm1_g, l1_norm2_g, l1_w_in, l1_diff_q_norm_g, l1_diff_k_norm_g,
              l1_lambda_q1, l1_lambda_k1, l1_lambda_q2, l1_lambda_k2, l1_diff_subln_g,
              l1_mla_q_a_norm_g, l1_mla_w_qb, l1_mla_kv_a_norm_g, l1_mla_w_kvb, l1_mla_q_norm_g, l1_mla_k_norm_g,
              l1_w_out, l1_router_w, l1_moe_w1, l1_moe_w3, l1_moe_w2):
    shared = [(l0_ada_w, l0_ada_b, l0_norm1_g, l0_norm2_g),
              (l1_ada_w, l1_ada_b, l1_norm1_g, l1_norm2_g)]
    mix = [(l0_w_in, l0_conv_dw_w, l0_conv_dw_b, l0_conv_ln_g, l0_conv_ln_b, l0_q_norm_g, l0_k_norm_g, l0_w_out),
           (l1_w_in, l1_diff_q_norm_g, l1_diff_k_norm_g, l1_lambda_q1, l1_lambda_k1, l1_lambda_q2, l1_lambda_k2,
            l1_diff_subln_g, l1_mla_q_a_norm_g, l1_mla_w_qb, l1_mla_kv_a_norm_g, l1_mla_w_kvb,
            l1_mla_q_norm_g, l1_mla_k_norm_g, l1_w_out)]
    ffn = [(l0_ffn_w1, l0_ffn_w3, l0_ffn_w2),
           (l1_router_w, l1_moe_w1, l1_moe_w3, l1_moe_w2)]
    caches = [(cache_l0_gqa_k, cache_l0_gqa_v),
              (cache_l1_diff_k, cache_l1_diff_v, cache_l1_mla_ckv, cache_l1_mla_krope)]
    cond_ctx = c_ctx[None, :]
    y_prompt = x_prompt
    y_sample = x_sample
    states = []
    for l in range(DEPTH):
        y_prompt, st = run_layer(l, y_prompt, cond_ctx, shared[l], mix[l], ffn[l], None)
        y_sample, _ = run_layer(l, y_sample, c, shared[l], mix[l], ffn[l], caches[l])
        states.append(st)
    (new_l0_gqa_k, new_l0_gqa_v), (new_l1_diff_k, new_l1_diff_v, new_l1_mla_ckv, new_l1_mla_krope) = states
    return (y_prompt, y_sample, new_l0_gqa_k, new_l0_gqa_v, new_l1_diff_k, new_l1_diff_v,
            new_l1_mla_ckv, new_l1_mla_krope)


_drawn_inputs = setup_inputs


def setup_inputs(seed=0):
    import zlib

    import numpy as np

    out = dict(_drawn_inputs(seed))
    spreads = {}
    factors = {'cache_l0_gqa_k': 5.147,
     'cache_l0_gqa_v': 4.378,
     'cache_l1_mla_ckv': 5.008,
     'cache_l1_mla_krope': 7.936,
     'l0_norm1_g': 3.031,
     'l0_norm2_g': 4.641,
     'l0_conv_dw_b': 8.0,
     'l0_conv_ln_g': 6.695,
     'l0_conv_ln_b': 8.0,
     'l0_q_norm_g': 8.0,
     'l0_k_norm_g': 2.918,
     'l1_norm1_g': 3.192,
     'l1_norm2_g': 3.707,
     'l1_diff_q_norm_g': 8.0,
     'l1_diff_k_norm_g': 3.618,
     'l1_lambda_q1': 3.909,
     'l1_lambda_k1': 4.899,
     'l1_lambda_q2': 3.802,
     'l1_diff_subln_g': 6.705,
     'l1_mla_q_a_norm_g': 8.0,
     'l1_mla_kv_a_norm_g': 2.695,
     'l1_mla_q_norm_g': 8.0,
     'l1_mla_k_norm_g': 8.0,
     'cache_l1_diff_k': 8.0,
     'cache_l1_diff_v': 8.0}
    for name, (base, spread) in spreads.items():
        noise = np.random.default_rng([zlib.crc32(name.encode()), seed]).standard_normal(out[name].shape)
        drawn = base * np.exp(spread * noise) if base else spread * noise
        out[name] = jnp.asarray(drawn.astype(out[name].dtype))
    for name, factor in factors.items():
        out[name] = (out[name] * factor).astype(out[name].dtype)
    return out
```

```python
import math
from contextlib import ExitStack

import numpy as np

import concourse.bass as bass
from concourse import mybir

F32 = mybir.dt.float32
F32R = mybir.dt.float32r
U32 = mybir.dt.uint32
I32 = mybir.dt.int32
ACT = mybir.ActivationFunctionType
ALU = mybir.AluOpType
AX = mybir.AxisListType

P = 128
D = 1024
KD = D // P
NT = 3
TOK = NT * P
NC = 512
CT = NC // P
CW = 31
PAD = CW // 2
CSEG = [(PAD, 0, P), (3 * PAD + P, P, 2 * P)]
CLEN = 4 * PAD + TOK
COUT = CLEN - 2 * PAD
HD = 64
DIFF_W = 512
MLA_H, NOPE, ROPE, VD, QR, KVR = 8, 64, 32, 64, 256, 128
QK = NOPE + ROPE
LAMBDA_INIT = 0.8 - 0.6 * math.exp(-0.3 * 1)
NE = 8
FE = 1408
FT = FE // P
FC = 4
FN = FE // FC
YC = 4
YN = D // YC
RMS_EPS = 1e-6
LN_EPS = 1e-5

R = 2
S = 2
SLOT = 3072
assert SLOT >= KD * FN == FT * YN
AHEAD = S - 1

HALVES = 6 * FC
HSLOTS = 4
HSLOT = R * SLOT // HSLOTS
HALF_K = [(0, 4), (4, 8)], [(0, 6), (6, 11)]
EXTRA = 5
JOB_A, JOB_B, JOB_T = 8, 20, 6
W2_AT = (4, 5, 9, 13)
ADD_AT = (6, 10, 14, 17)
assert HSLOT >= 6 * YN and HALVES % HSLOTS == 0

C_ID, C_LN = 0, 128
C_COS, C_SIN = 256, 384
C_COSR, C_SINR = 512, 576
C_SEL, C_SELB = 640, 642
C_IOTA, C_EPS = 898, 906
C_END = 908


def constants():
    c = np.zeros((P, C_END), np.float32)
    c[:, C_ID:C_ID + P] = np.eye(P, dtype=np.float32)
    c[:, C_LN:C_LN + P] = np.float32(1.0 / NC)
    n = 2 * P
    row = np.repeat(np.arange(n // 64), 64).astype(np.float32)
    col = np.tile(np.arange(64), n // 64).astype(np.float32)
    for rot, at_c, at_s in ((HD, C_COS, C_SIN), (ROPE, C_COSR, C_SINR)):
        nf = rot // 4
        inv = (np.float32(10000.0) ** (-np.arange(nf, dtype=np.float32) / np.float32(nf))).astype(np.float32)
        ang = np.concatenate([row[:, None] * inv, col[:, None] * inv], axis=-1).astype(np.float32)
        cos, sin = np.cos(ang), np.sin(ang)
        for t in range(2):
            a = slice(t * P, (t + 1) * P)
            c[:, at_c + t * rot:at_c + (t + 1) * rot] = np.concatenate([cos[a], cos[a]], axis=-1)
            c[:, at_s + t * rot:at_s + (t + 1) * rot] = np.concatenate([-sin[a], sin[a]], axis=-1)
    c[[0, 1, 4], C_SEL] = 1.0
    c[[2, 3, 4], C_SEL + 1] = 1.0
    c[[0, 1, 4], C_SELB:C_SELB + P] = 1.0
    c[[2, 3, 4], C_SELB + P:C_SELB + 2 * P] = 1.0
    c[:, C_IOTA:C_IOTA + NE] = np.arange(NE)
    c[:, C_EPS] = RMS_EPS
    c[:, C_EPS + 1] = LN_EPS
    return c


def job_constants():
    return np.concatenate([np.triu(np.ones((P, P))), np.ones((P, P)),
                           np.tile(np.arange(P), (P, 1))], axis=1).astype(np.float32)


def trunk_step(nc, A, out):
    ctx = ExitStack()
    with ctx:
        def sb(name, shape, dt=F32):
            return ctx.enter_context(nc.sbuf_tensor(name, shape, dt))

        def sem(name):
            return ctx.enter_context(nc.semaphore(name))

        x = sb("x", [P, NT, D])
        hTh = sb("hTh", [P, KD, TOK], F32R)
        hTl = sb("hTl", [P, KD, TOK], F32R)
        work = sb("work", [P, NT * FE])
        raw = sb("raw", [P, R * SLOT])
        Wh = sb("Wh", [P, S * SLOT], F32R)
        Wl = sb("Wl", [P, S * SLOT], F32R)
        gate_b = sb("gate_b", [P, 2, 2, D])
        cst = sb("cst", [P, C_END])
        hf = sb("hf", [P, 2, TOK])
        scr = sb("scr", [P, 1024])
        csil = sb("csil", [P, 2 * KD])
        chl = sb("chl", [P, KD, P], F32R)
        vecs = sb("vecs", [P, 60])
        dww = sb("dww", [P, CW * CT])
        mod = sb("mod", [P, 4, KD, 2])
        gains = sb("gains", [P, 1216])
        stats = sb("stats", [P, 160])
        comb = sb("comb", [P, NT, NE])
        comb_e = sb("comb_e", [P, NT])
        mx8 = sb("mx8", [P, NT, 8])
        ix8 = sb("ix8", [P, NT, 8], U32)
        ix8f = sb("ix8f", [P, NT, 8])
        rt = sb("rt", [P, 64])
        mask = sb("mask", [P, NT, NE])
        slot = sb("slot", [P, NT, NE + 1])
        slot_e = sb("slot_e", [P, NT])
        jobs = sb("jobs", [P, 112])
        jobs_i = sb("jobs_i", [P, 8], I32)
        marks = sb("marks", [P, 64])

        cckv = sb("cckv", [P, KVR])
        ckr = sb("ckr", [P, ROPE])

        def phase(*specs):
            with ExitStack() as own:
                return [own.enter_context(nc.sbuf_tensor(n, s, d)) for n, s, d in specs]

        stage, stage_w = phase(("stage", [P, P], F32), ("stage_w", [P, P], F32))
        (mrow,) = phase(("mrow", [P, 6 * D], F32))
        zq, cpad, yc, qT0, kT0, PT0, ck0, cv0 = phase(
            ("zq", [P, NT, 768], F32), ("cpad", [P, CT, CLEN], F32), ("yc", [P, CT, COUT], F32),
            ("qT0", [P, 4, TOK], F32), ("kT0", [P, 4 * P], F32), ("PT0", [P, 2, TOK], F32),
            ("ck0", [P, P], F32), ("cv0", [P, P], F32))
        gTh, gTl = phase(("gTh", [P, FT, TOK], F32R), ("gTl", [P, FT, TOK], F32R))
        zd, qT1, kT1, PT1, cdk, cdv = phase(
            ("zd", [P, NT, 3 * DIFF_W], F32), ("qT1", [P, 4, TOK], F32), ("kT1", [P, 4, 4 * P], F32),
            ("PT1", [P, 2, TOK], F32), ("cdk", [P, DIFF_W], F32), ("cdv", [P, DIFF_W], F32))
        kv, kT2, qT2 = phase(
            ("kv", [P, 4, 1024], F32), ("kT2", [P, 8, 4 * P], F32), ("qT2", [P, 8, TOK], F32))
        PT2 = hf
        toks_h, toks_l, mTh, mTl, yh, yl, pick, pickT, jcst = phase(
            ("toks_h", [P, NT, D], F32R), ("toks_l", [P, NT, D], F32R), ("mTh", [P, FT, P], F32R),
            ("mTl", [P, FT, P], F32R), ("yh", [P, 2, YN], F32R), ("yl", [P, 2, YN], F32R),
            ("pick", [P, NT, P], F32R), ("pickT", [P, TOK], F32R), ("jcst", [P, 3 * P], F32))

        xn = work[:, 0:NT * D].rearrange("p (t n) -> p t n", t=NT)
        gt = work[:, :].rearrange("p (t n) -> p t n", t=NT)
        zm = work[:, 0:NT * 416].rearrange("p (t n) -> p t n", t=NT)
        ktmp = work[:, 1248:2784].rearrange("p (b n) -> p b n", b=2)
        osb = work[:, 1248:1760]
        od = work[:, 1760:2016]
        Pb = work[:, 2784:3552].rearrange("p (b n) -> p b n", b=2)
        otok = work[:, 3552:4064]
        ysil = work[:, 0:CT * TOK].rearrange("p (c n) -> p c n", c=CT)
        ytmp = scr[:, 0:3 * YN].rearrange("p (b n) -> p b n", b=3)

        ident = cst[:, C_ID:C_ID + P]
        avg = cst[:, C_LN:C_LN + P]
        eps_rms = cst[:, C_EPS:C_EPS + 1]
        eps_ln = cst[:, C_EPS + 1:C_EPS + 2]
        G = {}
        at = 0
        for name, n in (("l0_q_norm_g", HD), ("l0_k_norm_g", HD), ("l1_diff_q_norm_g", HD),
                        ("l1_diff_k_norm_g", HD), ("l1_lambda_q1", HD), ("l1_lambda_k1", HD),
                        ("l1_lambda_q2", HD), ("l1_lambda_k2", HD), ("l1_diff_subln_g", P),
                        ("l1_mla_q_a_norm_g", QR), ("l1_mla_kv_a_norm_g", KVR),
                        ("l1_mla_q_norm_g", QK), ("l1_mla_k_norm_g", QK)):
            G[name] = gains[:, at:at + n]
            at += n
        V_N = {(0, 0): 16, (0, 1): 24, (1, 0): 32, (1, 1): 40}
        V_DWB, V_LNG, V_LNB = 48, 52, 56

        psA = [ctx.enter_context(nc.psum_tensor(f"psA{i}", [P, 512], F32)) for i in range(3)]
        psB = [ctx.enter_context(nc.psum_tensor(f"psB{i}", [P, 512], F32)) for i in range(3)]
        psT = [ctx.enter_context(nc.psum_tensor(f"psT{i}", [P, 512], F32)) for i in range(2)]

        def rows(w):
            return w.rearrange("(k p) n -> p k n", p=P)

        units = []

        def unit(kt, n, *pieces):
            units.append((pieces, kt, n))

        base = {}
        for l in range(2):
            ada = rows(A[f"l{l}_ada_w"])
            w_in, w_out = rows(A[f"l{l}_w_in"]), rows(A[f"l{l}_w_out"])
            base["ada", l] = len(units)
            for u in range(6 * D // YN):
                unit(KD, YN, (0, ada[:, :, u * YN:(u + 1) * YN]))
            base["in", l] = len(units)
            if l == 0:
                for j in range(CT):
                    unit(KD, 2 * P, (0, w_in[:, :, j * P:(j + 1) * P]),
                         (P, w_in[:, :, NC + j * P:NC + (j + 1) * P]))
                for j in range(3):
                    unit(KD, 256, (0, w_in[:, :, 2 * NC + j * 256:2 * NC + (j + 1) * 256]))
            else:
                for j in range(7):
                    unit(KD, 256, (0, w_in[:, :, j * 256:(j + 1) * 256]))
                unit(KD, 160, (0, w_in[:, :, 1792:1952]))
                qb, kvb = rows(A["l1_mla_w_qb"]), rows(A["l1_mla_w_kvb"])
                base["lat", l] = len(units)
                for j in range(2):
                    unit(2, 384, (0, qb[:, :, j * 384:(j + 1) * 384]))
                for j in range(2):
                    unit(1, 512, (0, kvb[:, :, j * 512:(j + 1) * 512]))
            base["out", l] = len(units)
            for j in range(YC):
                unit(KD, YN, (0, w_out[:, :, j * YN:(j + 1) * YN]))
            if l == 1:
                base["router"] = len(units)
                unit(KD, NE, (0, rows(A["l1_router_w"])))
            base["ffn", l] = len(units)
            for i in range(2 if l == 0 else 0):
                for j in range(3 * FC):
                    unit(KD if j < 2 * FC else FT, FN if j < 2 * FC else YN, (0, None))
        n_units = len(units)
        ffn_w = [
            (A["l0_ffn_w1"].rearrange("(k p) (e n) -> e p k n", p=P, e=2),
             A["l0_ffn_w3"].rearrange("(k p) (e n) -> e p k n", p=P, e=2),
             A["l0_ffn_w2"].rearrange("(e k p) n -> e p k n", p=P, e=2)),
            (A["l1_moe_w1"].rearrange("e (k p) n -> e p k n", p=P),
             A["l1_moe_w3"].rearrange("e (k p) n -> e p k n", p=P),
             A["l1_moe_w2"].rearrange("e (k p) n -> e p k n", p=P)),
        ]
        landed, count = [], [0] * R
        for u, (pieces, _, _) in enumerate(units):
            count[u % R] += 16 * len(pieces)
            landed.append(count[u % R])

        def raw_of(u):
            _, kt, n = units[u]
            at = u % R * SLOT
            return raw[:, at:at + kt * n]

        def hi_of(u):
            _, kt, n = units[u]
            at = u % S * SLOT
            return Wh[:, at:at + kt * n]

        def lo_of(u):
            _, kt, n = units[u]
            at = u % S * SLOT
            return Wl[:, at:at + kt * n]

        def by_k(view, u):
            return view.rearrange("p (k n) -> p k n", k=units[u][1])

        first = {}
        groups = {"A": 0, "B": 0, "T": 0}

        def takes(name, a=0, b=0, t=0):
            first[name] = dict(groups)
            groups["A"] += a
            groups["B"] += b
            groups["T"] += t

        takes("setup", t=2)
        for l in range(2):
            takes(("ada", l), b=24)
            takes(("mods", l), b=8, t=1)
            takes(("norm", l, 0), t=KD)
            if l == 0:
                takes("in0", a=CT, b=CT + 9)
                takes("prep0", t=4)
                takes("attend0", a=24, b=3, t=24 + NT)
                takes("lnorm", b=2)
            else:
                takes("in1", b=24)
                takes("prep1", t=7)
                takes("attend1", a=24, b=6, t=24 + NT)
                takes("latT", t=3)
                takes("lat", b=14)
                takes("prep2", t=14)
                takes("attend2", a=24, b=3, t=24 + NT)
            takes(("out", l), b=NT * YC)
            takes(("norm", l, 1), t=KD)
            if l == 1:
                takes("router", b=NT)
            if l == 0:
                takes(("ffn", l), a=12 * 2, b=24 * 2, t=FT * 2)
            else:
                takes("tables", b=1)
                takes("tokens", a=2 * NT, b=2 * NT)
                takes("jobs")

        raw_landed = [sem(f"raw_landed{i}") for i in range(R)]
        hi_ready = sem("hi_ready")
        lo_ready = sem("lo_ready")
        psA_full, psA_free = sem("psA_full"), sem("psA_free")
        psB_full, psB_free = sem("psB_full"), sem("psB_free")
        psT_full, psT_free = sem("psT_full"), sem("psT_free")
        const_in = sem("const_in")
        gains_in = sem("gains_in")
        cache_in = sem("cache_in")
        bias_in = sem("bias_in")
        x_in = sem("x_in")
        y_out = sem("y_out")
        state_out = sem("state_out")
        dve_chain = sem("dve_chain")
        act_chain = sem("act_chain")
        pool_chain = sem("pool_chain")
        c_silu = sem("c_silu")
        c_ready = sem("c_ready")
        sumsq = sem("sumsq")
        root = sem("root")
        ms_ready = sem("ms_ready")
        xn_ready = sem("xn_ready")
        hT_hi = sem("hT_hi")
        hT_lo = sem("hT_lo")
        z_ready = sem("z_ready")
        sig_ready = sem("sig_ready")
        bias_ready = sem("bias_ready")
        pv_done = sem("pv_done")
        o_ready = sem("o_ready")
        x_added = sem("x_added")
        ln_in = sem("ln_in")
        ln_out = sem("ln_out")
        ys_ready = sem("ys_ready")
        comb_ready = sem("comb_ready")
        logit_e = sem("logit_e")
        router_in = sem("router_in")
        lam_in = sem("lam_in")
        lam_e = sem("lam_e")
        gT_hi = sem("gT_hi")
        conv_chain = sem("conv_chain")

        half_landed = [sem(f"half_landed{i}") for i in range(HSLOTS)]
        half_hi = sem("half_hi")
        half_lo = sem("half_lo")
        half_used = sem("half_used")
        mask_ready = sem("mask_ready")
        table_ready = sem("table_ready")
        jcst_in = sem("jcst_in")
        place_ready = sem("place_ready")
        pick_ready = sem("pick_ready")
        pick_part = sem("pick_part")
        y_hi = sem("y_hi")

        def wait(eng, s, v):
            if not isinstance(v, int) or v > 0:
                eng.wait_ge(s, v)

        H, at = {}, 0
        for name, n in (("norm0", KD), ("att0", NT), ("conv", CT), ("norm1", KD), ("norm2", KD),
                        ("att1", NT), ("latT", 3), ("att2", NT), ("norm3", KD)):
            H[name] = at
            at += n

        last_group = {}
        for l in range(2):
            for u in range(24):
                last_group[base["ada", l] + u] = ("B", first["ada", l]["B"] + u)
            for j in range(YC):
                last_group[base["out", l] + j] = ("B", first["out", l]["B"] + NT * j + NT - 1)
            for i in range(2 if l == 0 else 0):
                f = first["ffn", l]
                for j in range(3 * FC):
                    if j < 2 * FC and j % 2 == 0:
                        g = ("A", f["A"] + 12 * i + NT * (j // 2) + NT - 1)
                    elif j < 2 * FC:
                        g = ("B", f["B"] + 24 * i + NT * (j // 2) + NT - 1)
                    else:
                        g = ("B", f["B"] + 24 * i + 12 + NT * (j - 2 * FC) + NT - 1)
                    last_group[base["ffn", l] + 12 * i + j] = g
        for j in range(CT):
            last_group[base["in", 0] + j] = ("B", first["in0"]["B"] + j)
        for j in range(3):
            last_group[base["in", 0] + CT + j] = ("B", first["in0"]["B"] + CT + NT * j + NT - 1)
        for j in range(8):
            last_group[base["in", 1] + j] = ("B", first["in1"]["B"] + NT * j + NT - 1)
        for j in range(2):
            last_group[base["lat", 1] + j] = ("B", first["lat"]["B"] + NT * j + NT - 1)
            last_group[base["lat", 1] + 2 + j] = ("B", first["lat"]["B"] + 2 * NT + 4 * j + 3)
        last_group[base["router"]] = ("B", first["router"]["B"] + NT - 1)
        full = {"A": psA_full, "B": psB_full}

        TGROUPS = {2: (0, 1), 4: (2, 3, 4), 6: (5, 6, 7), 8: (8, 9, 10)}

        def otile_at(t):
            return 8 * t + 12

        def tgroup(a, s):
            return first[f"attend{a}"]["T"] + s + sum(otile_at(t) <= s for t in range(NT - 1))

        def otgroup(a, t):
            f = first[f"attend{a}"]["T"]
            return f + otile_at(t) + t if t < NT - 1 else f + 8 * NT + NT - 1

        def ckvT(h):
            return h[:, 6:8, :].rearrange("p a b -> p (a b)")[:, 0:4 * P]

        def yv(c):
            return cpad[:, c, 0:TOK]

        def half_shape(h):
            (k0, k1), n = HALF_K[h >= 4 * FC][h % 2], (FN if h < 4 * FC else YN)
            return k0, k1, n

        def half_of(t, h):
            k0, k1, n = half_shape(h)
            at = h % HSLOTS * HSLOT
            return t[:, at:at + (k1 - k0) * n]

        def used_signal(h, n):
            j = h // 2
            if h % 2 == 0:
                return half_used, 3 * FC * n + j + 1
            if j >= 2 * FC:
                return psB_full, first["jobs"]["B"] + W2_AT[j - 2 * FC] + 1 + JOB_B * n
            if j % 2:
                return psB_full, first["jobs"]["B"] + j // 2 + 1 + JOB_B * n
            return psA_full, first["jobs"]["A"] + FC + j // 2 + 1 + JOB_A * n

        JT = {2: ((1, (0,)), (2, (1,))), 4: ((3, (2, 3, 4)),), 6: ((4, (5, 6, 7)),), 8: ((5, (8, 9, 10)),)}
        psAj, psBj = psA[0:2], psB + psA[2:3]
        ytj = scr[:, 0:4 * YN].rearrange("p (b n) -> p b n", b=4)
        picked = [h[:, :, 0:P] for h in (hTh, hTl)]
        gj = work[:, 0:FE]

        def over_jobs(eng, body):
            with eng.Fori(0, NE) as i:
                body(i, True)
            return further_jobs(eng, body)

        def further_jobs(eng, body):
            eng.wait_ge(table_ready, 1)
            more = eng.value_load(jobs_i[0:1, 0:1], min_val=0, max_val=EXTRA)
            with eng.Fori(0, EXTRA) as i:
                with eng.If(i < more):
                    body(i, False)
            return more

        qm = work[:, 1248:3552].rearrange("p (t n) -> p t n", t=NT)
        SS, RT, RC = 96, 112, 128

        def keys_of(t):
            return [0] if t == 0 else [1, 2, 3]

        def key_cols(t):
            return (0, P) if t == 0 else (P, 4 * P)

        def head0(s):
            t, h = divmod(s, 8)
            r = slice((h // 4) * HD, (h // 4 + 1) * HD)
            lo, hi = key_cols(t)
            return (qT0[r, h % 4, t * P:(t + 1) * P], kT0[r, lo:hi],
                    [(zq[:, k, 640:768] if k < 3 else cv0[:, :])[:, (h // 4) * HD:(h // 4 + 1) * HD]
                     for k in keys_of(t)])

        def head1(s):
            t, h = divmod(s, 8)
            r = slice((h % 2) * HD, (h % 2 + 1) * HD)
            lo, hi = key_cols(t)
            return (qT1[r, h // 2, t * P:(t + 1) * P], kT1[r, h // 2, lo:hi],
                    [(zd[:, k, 1024:1536] if k < 3 else cdv[:, :])[:, (h // 2) * P:(h // 2 + 1) * P]
                     for k in keys_of(t)])

        def head2(s):
            t, h = divmod(s, 8)
            lo, hi = key_cols(t)
            return (qT2[0:QK, h, t * P:(t + 1) * P], kT2[0:QK, h, lo:hi],
                    [kv[:, k, h * P + NOPE:(h + 1) * P] for k in keys_of(t)])

        ATT = [
            dict(per=8, n=HD, head=head0, PT=PT0, ft=4, no=0),
            dict(per=4, n=P, head=head1, PT=PT1, ft=0, no=1),
            dict(per=8, n=VD, head=head2, PT=PT2, ft=4, no=2),
        ]
        NS = 8 * NT

        def pv_signal(a, s):
            per = ATT[a]["per"]
            if s % per == per - 1:
                return psB_full, first[f"attend{a}"]["B"] + s // per + 1
            return pv_done, sum(NS - NS // ATT[b]["per"] for b in range(a)) + s - s // per + 1

        block = ctx.enter_context(nc.Block())

        @block.sync
        def _(sp):
            def load(u, i=0, j=0, view=None):
                _, kt, n = units[u + j]
                wait(sp, lo_ready, u + j + 12 * i - R + 1)
                dst = by_k(raw_of(u + j), u + j)
                if view is not None:
                    sp.dma_start(dst, view).then_inc(raw_landed[(u + j) % R], 16)
                    return
                pieces = units[u + j][0]
                for c, src in pieces:
                    sp.dma_start(dst[:, :, c:c + n // len(pieces)], src).then_inc(raw_landed[(u + j) % R], 16)

            def load_ffn(l, i):
                w1, w3, w2 = ffn_w[l]
                for j in range(3 * FC):
                    if j < 2 * FC:
                        c = j // 2
                        view = (w1, w3)[j % 2][i, :, :, c * FN:(c + 1) * FN]
                    else:
                        c = j - 2 * FC
                        view = w2[i, :, :, c * YN:(c + 1) * YN]
                    load(base["ffn", l], i, j, view)

            sp.dma_start(stage[0:KD, :], A["c_ctx"].rearrange("(k p) -> k p", p=P)).then_inc(const_in, 16)
            sp.dma_start(stage[KD:2 * KD, :], A["c"].rearrange("b (k p) -> (b k) p", p=P)).then_inc(const_in, 16)
            sp.dma_start(cst[:, :], A["consts"]).then_inc(const_in, 16)
            for (l, w), r in V_N.items():
                sp.dma_start(stage[r:r + KD, :],
                             A[f"l{l}_norm{w + 1}_g"].rearrange("(k p) -> k p", p=P)).then_inc(const_in, 16)
            for name, r in (("l0_conv_dw_b", V_DWB), ("l0_conv_ln_g", V_LNG), ("l0_conv_ln_b", V_LNB)):
                sp.dma_start(stage[r:r + CT, :], A[name].rearrange("(k p) -> k p", p=P)).then_inc(const_in, 16)
            sp.dma_start(stage_w[0:CW * CT, :],
                         A["l0_conv_dw_w"].rearrange("w (k p) -> (w k) p", p=P)).then_inc(const_in, 16)
            def load_half(e, h, n, wait_for=None):
                k0, k1, cols = half_shape(h)
                j = h // 2
                w1, w3, w2 = ffn_w[1]
                c = (j // 2 if j < 2 * FC else j - 2 * FC) * cols
                view = (w2 if j >= 2 * FC else (w1, w3)[j % 2])[e, :, k0:k1, c:c + cols]
                if wait_for is None and h != 4 * FC:
                    sp.wait_ge(half_lo, h + (2 if h == 4 * FC - 1 else 1) - HSLOTS + HALVES * n)
                sp.dma_start(half_of(raw, h).rearrange("p (k n) -> p k n", k=k1 - k0),
                             view).then_inc(half_landed[h % HSLOTS], 16)

            for u in range(base["ada", 0], base["ffn", 0]):
                load(u)
            with sp.Fori(0, 2) as i:
                load_ffn(0, i)
            for u in range(base["ada", 1], n_units):
                load(u)
            sp.wait_ge(lo_ready, n_units)
            for h in range(HSLOTS):
                load_half(0, h, 0, "split")

            def job(i, one_each):
                if one_each:
                    for h in range(HSLOTS, HALVES):
                        load_half(i, h, i)
                    for h in range(HSLOTS):
                        load_half(i + 1, h, i + 1)
                else:
                    e = sp.value_load(jobs_i[0:1, bass.ds(i + 1, 1)], min_val=0, max_val=NE - 1)
                    for h in range(HALVES):
                        load_half(e, h, i + NE)

            with sp.Fori(0, NE - 1) as i:
                job(i, True)
            for h in range(HSLOTS, HALVES):
                load_half(NE - 1, h, NE - 1)
            more = further_jobs(sp, job)
            sp.wait_ge(x_added, 12 * (2 + 2 + NE) + 12 * more)
            sp.dma_start(out[0][0], x[:, 0, :]).then_inc(y_out, 16)
            sp.dma_start(out[1][0].rearrange("(t p) n -> p t n", p=P), x[:, 1:NT, :]).then_inc(y_out, 16)
            sp.wait_ge(y_out, 32)
            sp.wait_ge(state_out, 16 * 6)

        @block.gpsimd
        def _(pool):
            pool.dma_start(x[:, 0, :], A["x_prompt"][0]).then_inc(x_in, 16)
            pool.dma_start(x[:, 1:NT, :], A["x_sample"][0].rearrange("(t p) n -> p t n", p=P)).then_inc(x_in, 16)
            for name, view in G.items():
                pool.dma_start(view, A[name].partition_broadcast(P)).then_inc(gains_in, 16)
            pool.dma_start(cckv[:, :], A["cache_l1_mla_ckv"][0]).then_inc(cache_in, 16)
            pool.dma_start(ckr[:, :], A["cache_l1_mla_krope"][0]).then_inc(cache_in, 16)

            def bias_row(l):
                wait(pool, psB_free, first["ada", l]["B"])
                pool.wait_ge(psT_full, first["ada", l]["T"])
                pool.dma_start(mrow[4:5, :], A[f"l{l}_ada_b"].rearrange("(a n) -> a n", a=1)).then_inc(bias_in, 16)

            def mods_done(l):
                pool.wait_ge(psB_free, first["mods", l]["B"] + 8)
                pool.wait_ge(psT_free, first["mods", l]["T"] + 1)

            def add(b, i=0):
                for j in range(YC):
                    for t in range(NT):
                        pool.wait_ge(psB_free, b + j * NT + t + 1 + 24 * i)
                        dst = x[:, t, j * YN:(j + 1) * YN]
                        pool.tensor_tensor(dst, dst, ytmp[:, t, :], ALU.add).then_inc(x_added, 1)

            bias_row(0)
            mods_done(0)
            pool.dma_start(ck0[:, :], A["cache_l0_gqa_k"].rearrange("b s h d -> (b s) (h d)")).then_inc(cache_in, 16)
            pool.dma_start(cv0[:, :], A["cache_l0_gqa_v"].rearrange("b s h d -> (b s) (h d)")).then_inc(cache_in, 16)
            pool.memset(cpad[:, :, :], 0.0).then_inc(pool_chain, 1)
            pool.wait_ge(z_ready, 1)
            pool.dma_start(out[2].rearrange("b s h d -> (b s) (h d)"), zq[:, 0, 512:640]).then_inc(state_out, 16)
            pool.dma_start(out[3].rearrange("b s h d -> (b s) (h d)"), zq[:, 0, 640:768]).then_inc(state_out, 16)
            add(first["out", 0]["B"])
            with pool.Fori(0, 2) as i:
                add(first["ffn", 0]["B"] + 12, i)
            bias_row(1)
            mods_done(1)
            pool.dma_start(cdk[:, :], A["cache_l1_diff_k"].rearrange("b s h j d -> (b s) (h j d)")).then_inc(cache_in, 16)
            pool.dma_start(cdv[:, :], A["cache_l1_diff_v"].rearrange("b s h d -> (b s) (h d)")).then_inc(cache_in, 16)
            pool.wait_ge(state_out, 32)
            pool.wait_ge(z_ready, 4)
            pool.dma_start(out[4].rearrange("b s h j d -> (b s) (h j d)"), zd[:, 0, 512:1024]).then_inc(state_out, 16)
            pool.dma_start(out[5].rearrange("b s h d -> (b s) (h d)"), zd[:, 0, 1024:1536]).then_inc(state_out, 16)
            pool.wait_ge(state_out, 64)
            pool.wait_ge(z_ready, 7)
            pool.dma_start(out[6][0], zm[:, 0, QR:QR + KVR]).then_inc(state_out, 16)
            pool.dma_start(out[7][0], zm[:, 0, QR + KVR:416]).then_inc(state_out, 16)
            add(first["out", 1]["B"])
            pool.dma_start(jcst[:, :], A["job_consts"]).then_inc(jcst_in, 16)

            def job(i, one_each):
                n = i if one_each else i + NE
                for c in range(YC):
                    for t in range(NT):
                        b = first["jobs"]["B"] + ADD_AT[c] + t
                        pool.wait_ge(psB_free, b + 1 + JOB_B * n)
                        dst = x[:, t, c * YN:(c + 1) * YN]
                        pool.tensor_tensor(dst, dst, ytj[:, (NT * c + t) % 4, :], ALU.add).then_inc(x_added, 1)

            over_jobs(pool, job)

        @block.scalar
        def _(act):
            chain = [0]

            def link(ins):
                chain[0] += 1
                ins.then_inc(act_chain, 1)
                act.wait_ge(act_chain, chain[0])

            def split_hi(u, i=0, per=12):
                act.wait_ge(raw_landed[u % R], landed[u] + 16 * (per // R) * i)
                if u >= S:
                    group, g = last_group[u - S]
                    grows = 6 if per == 6 else 12 if group == "A" else 24
                    act.wait_ge(full[group], g + 1 + grows * i)
                elif not isinstance(i, int):
                    act.wait_ge(psB_full, last_group[u - S + per][1] + 1 + per * (i - 1))
                act.copy(hi_of(u), raw_of(u)).then_inc(hi_ready, 1)

            def step(u):
                if u + AHEAD < n_units:
                    split_hi(u + AHEAD)

            roots = [0]

            def square_root(o, i, scale, eps):
                roots[0] += 1
                act.wait_ge(ms_ready, roots[0])
                act.activation(o, i, ACT.Sqrt, scale=scale, bias=eps).then_inc(root, 1)

            def ada(l):
                u0 = base["ada", l] + AHEAD
                for j in range(6):
                    split_hi(u0 + j)
                with act.Fori(1, 3) as i:
                    for j in range(6):
                        split_hi(u0 + j, i, 6)
                for j in range(6):
                    split_hi(u0 + 18 + j)

            norms = [0]

            def norm():
                n = norms[0]
                act.wait_ge(x_in, 32)
                wait(act, x_added, [0, 12, 36, 48][n])
                for t in range(NT):
                    link(act.activation(scr[:, 0:D], x[:, t, :], ACT.Square, accum_out=stats[:, t:t + 1]))
                act.activation(stats[:, 4:7], stats[:, 0:3], ACT.Sqrt, scale=1.0 / D,
                               bias=eps_rms).then_inc(sumsq, 1)
                for f in range(KD):
                    act.wait_ge(psT_free, first["norm", n // 2, n % 2]["T"] + f + 1)
                    act.copy(hTh[:, f, :], hf[:, f % 2, :]).then_inc(hT_hi, 1)
                norms[0] += 1

            def o_split(a, t):
                k = otgroup(a, t)
                act.wait_ge(psT_full, k + 1)
                act.copy(hTh[:, ATT[a]["ft"]:ATT[a]["ft"] + 4, t * P:(t + 1) * P],
                         psT[k % 2][:, :].rearrange("p (f n) -> p f n", f=4)).then_inc(hT_hi, 1)

            def attend(a):
                f = first[f"attend{a}"]
                for s in range(NS):
                    n = P * len(keys_of(s // 8))
                    g = f["A"] + s
                    act.wait_ge(bias_ready, NS * a + s + 1)
                    if s >= 2:
                        act.wait_ge(psT_full, tgroup(a, s - 2) + 1)
                    act.activation(Pb[:, s % 2, 0:n], psA[g % 3][:, 0:n], ACT.Exp, scale=-1.0,
                                   bias=stats[:, 32 + s:33 + s],
                                   accum_out=stats[:, 64 + s:65 + s]).then_inc(psA_free, 1)
                    if a == 1 and s % 4 == 1 and s > 4:
                        square_root(stats[:, 12:14], stats[:, 10:12], 1.0 / P, eps_rms)
                    if s in (otile_at(0), otile_at(1)):
                        o_split(a, s // 8 - 1)
                if a == 1:
                    square_root(stats[:, 12:14], stats[:, 10:12], 1.0 / P, eps_rms)
                o_split(a, NT - 1)

            def ffn(l):
                u0, f, k = base["ffn", l], first["ffn", l], (2 if l == 0 else NE)
                act.wait_ge(state_out, 32)
                with act.Fori(0, k) as i:
                    for j in range(3 * FC):
                        if j + AHEAD < 3 * FC:
                            split_hi(u0 + j + AHEAD, i)
                        elif l == 0:
                            split_hi(u0 + j + AHEAD, i)
                        else:
                            with act.If(i < k - 1):
                                split_hi(u0 + j + AHEAD, i)
                        if j < 2 * FC and j % 2 == 0:
                            for t in range(NT):
                                g = f["A"] + NT * (j // 2) + t
                                act.wait_ge(psA_full, g + 1 + 12 * i)
                                act.activation(gt[:, t, j // 2 * FN:(j // 2 + 1) * FN], psA[g % 3][:, 0:FN],
                                               ACT.Silu).then_inc(psA_free, 1)
                        for q in TGROUPS.get(j, ()):
                            act.wait_ge(psT_full, f["T"] + q + 1 + FT * i)
                            act.copy(gTh[:, q, :], psT[q % 2][:, 0:TOK]).then_inc(gT_hi, 1)

            def qk_root(hd, heads):
                square_root(stats[:, RT:RT + heads], stats[:, SS:SS + heads], 1.0 / hd, eps_rms)

            act.wait_ge(const_in, 16 * 11)
            act.wait_ge(psT_free, 1)
            act.activation(csil[:, :], vecs[:, 0:2 * KD], ACT.Silu).then_inc(c_silu, 1)
            for u in range(AHEAD):
                split_hi(u)

            ada(0)
            norm()
            for j in range(CT):
                step(base["in", 0] + j)
                g = first["in0"]["A"] + j
                act.wait_ge(psA_full, g + 1)
                if j == 0:
                    act.wait_ge(hT_lo, H["norm0"] + KD)
                if j >= 2:
                    act.wait_ge(psB_free, first["in0"]["B"] + j - 1)
                act.activation(hf[:, j % 2, :], psA[g % 3][:, 0:TOK], ACT.Sigmoid).then_inc(psA_free, 1)
            for j in range(3):
                step(base["in", 0] + CT + j)
            for t in range(NT):
                qk_root(HD, 10)
            attend(0)
            square_root(hf[:, 1, :], hf[:, 0, :], 1.0, eps_ln)
            for c in range(CT):
                act.wait_ge(ln_out, c + 1)
                link(act.activation(ysil[:, c, :], yv(c), ACT.Silu, scale=vecs[:, V_LNG + c:V_LNG + c + 1],
                                    bias=vecs[:, V_LNB + c:V_LNB + c + 1]))
                act.copy(hTh[:, c, :], ysil[:, c, :]).then_inc(hT_hi, 1)
            for j in range(YC):
                step(base["out", 0] + j)
            norm()
            ffn(0)

            ada(1)
            norm()
            act.wait_ge(lam_in, 1)
            act.activation(stats[:, 90:92], stats[:, 88:90], ACT.Exp).then_inc(lam_e, 1)
            for j in range(8):
                step(base["in", 1] + j)
            for t in range(NT):
                qk_root(HD, 16)
            attend(1)
            qk_root(QR, NT)
            qk_root(KVR, NT)
            for q in range(3):
                k = first["latT"]["T"] + q
                act.wait_ge(psT_full, k + 1)
                dst = hTh[:, 4 + q, :] if q < 2 else ckvT(hTh)
                act.copy(dst, psT[k % 2][:, 0:TOK if q < 2 else 4 * P]).then_inc(hT_hi, 1)
            for j in range(4):
                step(base["lat", 1] + j)
            for t in range(NT + 4):
                qk_root(QK, MLA_H)
            attend(2)
            for j in range(YC):
                step(base["out", 1] + j)
            norm()
            step(base["router"])
            act.wait_ge(router_in, 1)
            act.activation(rt[:, 4:7], rt[:, 0:3], ACT.Exp).then_inc(logit_e, 1)
            for q in range(2 * NT):
                g = first["tokens"]["A"] + q
                act.wait_ge(psA_full, g + 1)
                act.copy(toks_h[:, q // 2, q % 2 * 512:(q % 2 + 1) * 512], psA[g % 3][:, :]).then_inc(psA_free, 1)

            def split_half(h, n):
                k0, k1, cols = half_shape(h)
                act.wait_ge(half_landed[h % HSLOTS], 16 * (h // HSLOTS + 1) + 16 * (HALVES // HSLOTS) * n)
                act.copy(half_of(Wh, h), half_of(raw, h)).then_inc(half_hi, 1)

            def gathered(n):
                for q in range(4):
                    act.wait_ge(psA_full, first["jobs"]["A"] + q + 1 + JOB_A * n)
                    act.copy(picked[q // 2][:, q % 2 * 4:q % 2 * 4 + 4, :],
                             psAj[q % 2][:, :].rearrange("p (f n) -> p f n", f=4)).then_inc(psA_free, 1)

            def job(i, one_each):
                n = i if one_each else i + NE
                f = first["jobs"]
                if not one_each:
                    act.wait_ge(psB_full, f["B"] + JOB_B * n)
                    for h in range(HSLOTS - 1):
                        split_half(h, n)
                    gathered(n)
                for h in range(HALVES):
                    j = h // 2
                    ahead = h + HSLOTS - 1
                    if ahead < HALVES:
                        act.wait_ge(*used_signal(h - 1, n) if h else used_signal(HALVES - 1, n - 1))
                        split_half(ahead, n)
                    elif one_each:
                        with act.If(i < NE - 1):
                            act.wait_ge(*used_signal(h - 1, n))
                            split_half(ahead - HALVES, n + 1)
                    if h == 4 * FC:
                        transposed(j, n)
                        if one_each:
                            with act.If(i < NE - 1):
                                gathered(n + 1)
                    if h % 2 == 0:
                        continue
                    if j < 2 * FC and j % 2 == 0:
                        g = FC + j // 2
                        act.wait_ge(psA_full, f["A"] + g + 1 + JOB_A * n)
                        act.activation(gj[:, j // 2 * FN:(j // 2 + 1) * FN], psAj[g % 2][:, 0:FN],
                                       ACT.Silu).then_inc(psA_free, 1)
                        transposed(j, n)
                    elif j >= 2 * FC:
                        c = j - 2 * FC
                        act.wait_ge(psB_full, f["B"] + W2_AT[c] + 1 + JOB_B * n)
                        act.copy(yh[:, c % 2, :], psBj[W2_AT[c] % 4][:, 0:YN]).then_inc(y_hi, 1)

            def transposed(j, n):
                for g, tiles in JT.get(j, ()):
                    act.wait_ge(psT_full, first["jobs"]["T"] + g + 1 + JOB_T * n)
                    act.copy(mTh[:, tiles[0]:tiles[-1] + 1, :],
                             psT[g % 2][:, 0:P * len(tiles)].rearrange("p (f n) -> p f n", f=len(tiles))
                             ).then_inc(gT_hi, 1)

            for h in range(HSLOTS - 1):
                split_half(h, 0)
            gathered(0)
            over_jobs(act, job)

        @block.tensor
        def _(pe):
            def free_a(g, i=0, per=12):
                if g >= 3:
                    pe.wait_ge(psA_free, g - 2 + per * i)

            def free_b(g, i=0, per=24):
                if g >= 3:
                    pe.wait_ge(psB_free, g - 2 + per * i)

            def free_t(g):
                if g >= 2:
                    pe.wait_ge(psT_free, g - 1)

            def split_products(o, pairs):
                n = len(pairs)
                for k, (sh, sl, mh, ml) in enumerate(pairs):
                    pe.matmul(o, sh, mh, start=(k == 0), stop=False)
                    pe.matmul(o, sh, ml, start=False, stop=False)
                    last = pe.matmul(o, sl, mh, start=False, stop=(k == n - 1))
                return last

            def rows_times(o, u, stat, t, cols=None):
                _, kt, n = units[u]
                wh, wl = by_k(hi_of(u), u), by_k(lo_of(u), u)
                return split_products(o[:, 0:n], [
                    (stat[0][:, k, t * P:(t + 1) * P], stat[1][:, k, t * P:(t + 1) * P], wh[:, k, :], wl[:, k, :])
                    for k in range(kt)])

            def unit_b(u, b0, stat, tiles=NT):
                pe.wait_ge(lo_ready, u + 1)
                for t in range(tiles):
                    g = b0 + t
                    free_b(g)
                    rows_times(psB[g % 3], u, stat, t).then_inc(psB_full, 1)

            def ada(l):
                u0, b0 = base["ada", l], first["ada", l]["B"]

                def one(j, i=0):
                    u, g = u0 + j, b0 + j
                    pe.wait_ge(lo_ready, u + 1 + 6 * i)
                    free_b(g, i, 6)
                    wh, wl = by_k(hi_of(u), u), by_k(lo_of(u), u)
                    for k in range(KD):
                        pe.matmul(psB[g % 3][:, 0:YN], chl[:, k, :], wh[:, k, :], start=(k == 0), stop=False)
                        last = pe.matmul(psB[g % 3][:, 0:YN], chl[:, k, :], wl[:, k, :], start=False,
                                         stop=(k == KD - 1))
                    last.then_inc(psB_full, 1)

                for j in range(6):
                    one(j)
                with pe.Fori(1, 4) as i:
                    for j in range(6):
                        one(j, i)

            def mods(l):
                f = first["mods", l]
                pe.wait_ge(psB_free, f["B"])
                pe.wait_ge(bias_in, 16 * (l + 1))
                g = f["T"]
                free_t(g)
                chunks = [*range(0, 2 * KD), *range(3 * KD, 5 * KD)]
                for n, c in enumerate(chunks):
                    last = pe.matmul(psT[g % 2][:, 2 * n:2 * n + 2], mrow[0:5, c * P:(c + 1) * P],
                                     cst[0:5, C_SEL:C_SEL + 2], start=True, stop=True)
                last.then_inc(psT_full, 1)
                for n in range(8):
                    gate, cond, half = n // 4, n // 2 % 2, n % 2
                    g = f["B"] + n
                    free_b(g)
                    c0 = (3 * gate + 2) * D + half * 512
                    pe.matmul(psB[g % 3][:, :], cst[0:5, C_SELB + cond * P:C_SELB + (cond + 1) * P],
                              mrow[0:5, c0:c0 + 512], start=True, stop=True).then_inc(psB_full, 1)

            norms = [0]

            def norm(l, w):
                g0 = first["norm", l, w]["T"]
                pe.wait_ge(xn_ready, norms[0] + 1)
                for f in range(KD):
                    free_t(g0 + f)
                    for t in range(NT):
                        last = pe.transpose(psT[(g0 + f) % 2][:, t * P:(t + 1) * P], xn[:, t, f * P:(f + 1) * P],
                                            ident)
                    last.then_inc(psT_full, 1)
                norms[0] += 1

            def attend(a):
                cfg, f = ATT[a], first[f"attend{a}"]
                for i in range(NS + 2):
                    if i < NS:
                        g = f["A"] + i
                        free_a(g)
                        q, k, _ = cfg["head"](i)
                        pe.matmul(psA[g % 3][:, 0:P * len(keys_of(i // 8))], q, k,
                                  start=True, stop=True).then_inc(psA_full, 1)
                    if 1 <= i <= NS:
                        s = i - 1
                        g = tgroup(a, s)
                        pe.wait_ge(psA_free, f["A"] + s + 1)
                        free_t(g)
                        for k in range(len(keys_of(s // 8))):
                            last = pe.transpose(psT[g % 2][:, k * P:(k + 1) * P],
                                                Pb[:, s % 2, k * P:(k + 1) * P], ident)
                        last.then_inc(psT_full, 1)
                    if i >= 2:
                        s = i - 2
                        g = f["B"] + s // cfg["per"]
                        if s % cfg["per"] == 0:
                            free_b(g)
                        pe.wait_ge(psT_free, tgroup(a, s) + 1)
                        c = s % cfg["per"] * cfg["n"]
                        vs = cfg["head"](s)[2]
                        for k, v in enumerate(vs):
                            last = pe.matmul(psB[g % 3][:, c:c + cfg["n"]], cfg["PT"][:, s % 2, k * P:(k + 1) * P],
                                             v, start=(k == 0), stop=(k == len(vs) - 1))
                        last.then_inc(pv_signal(a, s)[0], 1)
                    if i in (otile_at(0), otile_at(1)):
                        o_transpose(a, i // 8 - 1)
                o_transpose(a, NT - 1)

            def o_transpose(a, t):
                g = otgroup(a, t)
                pe.wait_ge(o_ready, NT * a + t + 1)
                free_t(g)
                for k in range(4):
                    last = pe.transpose(psT[g % 2][:, k * P:(k + 1) * P], otok[:, k * P:(k + 1) * P], ident)
                last.then_inc(psT_full, 1)

            def out_projection(l):
                pe.wait_ge(hT_lo, H["att0" if l == 0 else "att2"] + (NT + CT if l == 0 else NT))
                for j in range(YC):
                    unit_b(base["out", l] + j, first["out", l]["B"] + NT * j, (hTh, hTl))

            def ffn(l):
                u0, f, k = base["ffn", l], first["ffn", l], (2 if l == 0 else NE)

                def transposes(j, i):
                    pe.wait_ge(psB_free, f["B"] + NT * (j // 2) + 24 * i)
                    for q in TGROUPS[j]:
                        pe.wait_ge(psT_free, f["T"] + (q if q < 2 else q - 1) + FT * i)
                        for t in range(NT):
                            last = pe.transpose(psT[q % 2][:, t * P:(t + 1) * P],
                                                gt[:, t, q * P:(q + 1) * P], ident)
                        last.then_inc(psT_full, 1)

                with pe.Fori(0, k) as i:
                    for j in range(3 * FC):
                        u = u0 + j
                        if j == 2 * FC:
                            transposes(j, i)
                            pe.wait_ge(psT_free, f["T"] + FT + FT * i)
                        pe.wait_ge(lo_ready, u + 1 + 12 * i)
                        for t in range(NT):
                            if j < 2 * FC and j % 2 == 0:
                                g = f["A"] + NT * (j // 2) + t
                                free_a(g, i)
                                rows_times(psA[g % 3], u, (hTh, hTl), t).then_inc(psA_full, 1)
                            else:
                                g = f["B"] + NT * (j // 2 if j < 2 * FC else j - FC) + t
                                free_b(g, i)
                                rows_times(psB[g % 3], u, (hTh, hTl) if j < 2 * FC else (gTh, gTl),
                                           t).then_inc(psB_full, 1)
                        if j in TGROUPS and j < 2 * FC:
                            transposes(j, i)

            pe.wait_ge(const_in, 16 * 11)
            pe.transpose(psT[0][:, 0:60], stage[0:60, :], ident[0:60, 0:60]).then_inc(psT_full, 1)
            pe.transpose(psT[1][:, 0:CW * CT], stage_w[0:CW * CT, :],
                         ident[0:CW * CT, 0:CW * CT]).then_inc(psT_full, 1)
            pe.wait_ge(c_ready, 1)
            ada(0)
            mods(0)
            norm(0, 0)
            pe.wait_ge(hT_lo, H["norm0"] + KD)
            for j in range(CT):
                u = base["in", 0] + j
                pe.wait_ge(lo_ready, u + 1)
                wh, wl = by_k(hi_of(u), u), by_k(lo_of(u), u)
                ga, gb = first["in0"]["A"] + j, first["in0"]["B"] + j
                free_a(ga)
                c = slice(P, 2 * P)
                split_products(psA[ga % 3][:, 0:TOK], [
                    (wh[:, k, c], wl[:, k, c], hTh[:, k, :], hTl[:, k, :]) for k in range(KD)
                ]).then_inc(psA_full, 1)
                free_b(gb)
                c = slice(0, P)
                split_products(psB[gb % 3][:, 0:TOK], [
                    (wh[:, k, c], wl[:, k, c], hTh[:, k, :], hTl[:, k, :]) for k in range(KD)
                ]).then_inc(psB_full, 1)
            for j in range(3):
                unit_b(base["in", 0] + CT + j, first["in0"]["B"] + CT + NT * j, (hTh, hTl))
            g0 = first["prep0"]["T"]
            for t in range(NT):
                pe.wait_ge(z_ready, t + 1)
                free_t(g0 + t)
                for j in range(4):
                    last = pe.transpose(psT[(g0 + t) % 2][:, j * P:(j + 1) * P], zq[:, t, j * P:(j + 1) * P], ident)
                last.then_inc(psT_full, 1)
            pe.wait_ge(cache_in, 64)
            free_t(g0 + 3)
            for t in range(4):
                src = zq[:, t, 512:640] if t < 3 else ck0[:, :]
                last = pe.transpose(psT[(g0 + 3) % 2][:, t * P:(t + 1) * P], src, ident)
            last.then_inc(psT_full, 1)
            pe.wait_ge(psT_free, g0 + 4)
            attend(0)
            for n in range(2):
                g = first["lnorm"]["B"] + n
                pe.wait_ge(ln_in, n + 1)
                free_b(g)
                src = yc if n == 0 else cpad
                for c in range(CT):
                    last = pe.matmul(psB[g % 3][:, 0:COUT], avg, src[:, c, 0:COUT], start=(c == 0),
                                     stop=(c == CT - 1))
                last.then_inc(psB_full, 1)
            out_projection(0)
            norm(0, 1)
            pe.wait_ge(hT_lo, H["norm1"] + KD)
            ffn(0)

            ada(1)
            mods(1)
            norm(1, 0)
            pe.wait_ge(hT_lo, H["norm2"] + KD)
            for j in range(8):
                unit_b(base["in", 1] + j, first["in1"]["B"] + NT * j, (hTh, hTl))
            g0 = first["prep1"]["T"]
            pe.wait_ge(cache_in, 96)
            for n in range(7):
                t = n // 2
                if n % 2 == 0 and t < NT:
                    pe.wait_ge(z_ready, 3 + t + 1)
                free_t(g0 + n)
                for j in range(4):
                    if n == 6:
                        src = cdk[:, j * P:(j + 1) * P]
                    else:
                        src = zd[:, t, n % 2 * DIFF_W + j * P:n % 2 * DIFF_W + (j + 1) * P]
                    last = pe.transpose(psT[(g0 + n) % 2][:, j * P:(j + 1) * P], src, ident)
                last.then_inc(psT_full, 1)
            pe.wait_ge(psT_free, g0 + 7)
            attend(1)
            g0 = first["latT"]["T"]
            pe.wait_ge(z_ready, 7)
            for q in range(3):
                free_t(g0 + q)
                for t in range(3 if q < 2 else 4):
                    src = cckv[:, :] if t == 3 else zm[:, t, q * P:(q + 1) * P]
                    last = pe.transpose(psT[(g0 + q) % 2][:, t * P:(t + 1) * P], src, ident)
                last.then_inc(psT_full, 1)
            pe.wait_ge(hT_lo, H["latT"] + 3)
            for j in range(2):
                unit_b(base["lat", 1] + j, first["lat"]["B"] + NT * j, (hTh[:, 4:6, :], hTl[:, 4:6, :]))
            ck = [ckvT(h).rearrange("p (a b) -> p a b", a=1) for h in (hTh, hTl)]
            for j in range(2):
                unit_b(base["lat", 1] + 2 + j, first["lat"]["B"] + 2 * NT + 4 * j, ck, 4)
            g0 = first["prep2"]["T"]
            for n in range(14):
                t = n // 2 if n < 6 else n // 2 - 3
                pe.wait_ge(z_ready, 7 + n // 2 + 1)
                free_t(g0 + n)
                for j in range(4):
                    h = n % 2 * 4 + j
                    src = qm[:, t, h * QK:(h + 1) * QK] if n < 6 else ktmp[:, t % 2, h * QK:(h + 1) * QK]
                    last = pe.transpose(psT[(g0 + n) % 2][0:QK, j * P:(j + 1) * P], src, ident)
                last.then_inc(psT_full, 1)
            pe.wait_ge(psT_free, g0 + 14)
            attend(2)
            out_projection(1)
            norm(1, 1)
            pe.wait_ge(hT_lo, H["norm3"] + KD)
            unit_b(base["router"], first["router"]["B"], (hTh, hTl))
            for part, banks, full_sem, free in ((hTh, psA, psA_full, free_a), (hTl, psB, psB_full, free_b)):
                g0 = first["tokens"]["A" if part is hTh else "B"]
                for q in range(2 * NT):
                    if part is hTl and q == 0:
                        g = first["tables"]["B"]
                        pe.wait_ge(mask_ready, 1)
                        pe.wait_ge(jcst_in, 16)
                        free(g)
                        for t in range(NT):
                            for r in range(t + 1):
                                pe.matmul(psB[g % 3][:, t * NE:(t + 1) * NE], jcst[:, P:2 * P] if r < t else
                                          jcst[:, 0:P], mask[:, r, :], start=(r == 0), stop=(r == t))
                        for t in range(NT):
                            last = pe.matmul(psB[g % 3][:, NT * NE:(NT + 1) * NE], jcst[:, P:2 * P], mask[:, t, :],
                                             start=(t == 0), stop=(t == NT - 1))
                        last.then_inc(psB_full, 1)
                    g = g0 + q
                    free(g)
                    for k in range(4):
                        last = pe.transpose(banks[g % 3][:, k * P:(k + 1) * P],
                                            part[:, q % 2 * 4 + k, q // 2 * P:(q // 2 + 1) * P].bitcast(F32), ident)
                    last.then_inc(full_sem, 1)
            f = first["jobs"]
            pe.wait_ge(psA_free, f["A"])
            pe.wait_ge(psB_free, f["B"])
            pe.wait_ge(psT_free, f["T"])

            def gather(n):
                pe.wait_ge(pick_ready, n + 1)
                for q in range(4):
                    pe.wait_ge(psA_free, f["A"] + q - 1 + JOB_A * n)
                    src = (toks_h, toks_l)[q // 2]
                    for k in range(4):
                        c = (q % 2 * 4 + k) * P
                        for t in range(NT):
                            last = pe.matmul(psAj[q % 2][:, k * P:(k + 1) * P], src[:, t, c:c + P], pick[:, t, :],
                                             start=(t == 0), stop=(t == NT - 1))
                    last.then_inc(psA_full, 1)

            def turn(j, n):
                pe.wait_ge(psB_free, f["B"] + j // 2 + JOB_B * n)
                for g, tiles in JT.get(j, ()):
                    pe.wait_ge(psT_free, f["T"] + g - 1 + JOB_T * n)
                    for k, q in enumerate(tiles):
                        last = pe.transpose(psT[g % 2][:, k * P:(k + 1) * P], gj[:, q * P:(q + 1) * P], ident)
                    last.then_inc(psT_full, 1)

            def half_products(h, n, bank, free_sem, free_at, full_sem, stat):
                k0, k1, cols = half_shape(h)
                wh, wl = (half_of(w, h).rearrange("p (k n) -> p k n", k=k1 - k0) for w in (Wh, Wl))
                pe.wait_ge(half_lo, h + 1 + HALVES * n)
                if h % 2 == 0:
                    pe.wait_ge(free_sem, free_at)
                o = bank[:, 0:cols]
                for k in range(k0, k1):
                    pe.matmul(o, stat[0][:, k, :], wh[:, k - k0, :], start=(k == 0), stop=False)
                    pe.matmul(o, stat[0][:, k, :], wl[:, k - k0, :], start=False, stop=False)
                    last = pe.matmul(o, stat[1][:, k, :], wh[:, k - k0, :], start=False,
                                     stop=(h % 2 == 1 and k == k1 - 1))
                last.then_inc(full_sem if h % 2 else half_used, 1)

            def give_back(c, n):
                pe.wait_ge(psB_free, f["B"] + W2_AT[c] + 1 + JOB_B * n)
                for t in range(NT):
                    b = ADD_AT[c] + t
                    pe.wait_ge(psB_free, f["B"] + b - 3 + JOB_B * n)
                    o, at = psBj[b % 4][:, 0:YN], pickT[:, t * P:(t + 1) * P]
                    pe.matmul(o, at, yh[:, c % 2, :], start=True, stop=False)
                    pe.matmul(o, at, yl[:, c % 2, :], start=False, stop=True).then_inc(psB_full, 1)

            def job(i, one_each):
                n = i if one_each else i + NE
                if not one_each:
                    gather(n)
                pe.wait_ge(psA_free, f["A"] + FC + JOB_A * n)
                for h in range(HALVES):
                    j = h // 2
                    if j >= 2 * FC:
                        if h <= 4 * FC + 1:
                            pe.wait_ge(psT_free, f["T"] + JOB_T - 1 + h - 4 * FC + JOB_T * n)
                        b = W2_AT[j - 2 * FC]
                        half_products(h, n, psBj[b % 4], psB_free, f["B"] + b - 3 + JOB_B * n, psB_full, (mTh, mTl))
                    elif j % 2:
                        b = j // 2
                        half_products(h, n, psBj[b % 4], psB_free, f["B"] + b - 3 + JOB_B * n, psB_full, picked)
                    else:
                        a = FC + j // 2
                        half_products(h, n, psAj[a % 2], psA_free, f["A"] + a - 1 + JOB_A * n, psA_full, picked)
                    if h == 1:
                        pe.wait_ge(psT_free, f["T"] - 1 + JOB_T * n)
                        for t in range(NT):
                            last = pe.transpose(psT[0][:, t * P:(t + 1) * P], pick[:, t, :].bitcast(F32), ident)
                        last.then_inc(psT_full, 1)
                    if h % 2 and j < 2 * FC and j in JT:
                        turn(j, n)
                    if h == 4 * FC:
                        turn(j, n)
                        if one_each:
                            with pe.If(i < NE - 1):
                                gather(n + 1)
                    if h % 2 and j > 2 * FC:
                        give_back(j - 2 * FC - 1, n)
                give_back(YC - 1, n)

            gather(0)
            over_jobs(pe, job)

        @block.vector
        def _(dve):
            chain = [0]

            def link(ins):
                chain[0] += 1
                ins.then_inc(dve_chain, 1)
                dve.wait_ge(dve_chain, chain[0])

            def split_lo(u, i=0, per=12):
                dve.wait_ge(hi_ready, u + 1 + per * i)
                dve.tensor_tensor(lo_of(u), raw_of(u), hi_of(u).bitcast(F32), ALU.subtract).then_inc(lo_ready, 1)

            def step(u):
                if u + AHEAD < n_units:
                    split_lo(u + AHEAD)

            asked, lows = [0], [0]

            def ask_root(ins):
                ins.then_inc(ms_ready, 1)
                asked[0] += 1
                dve.wait_ge(root, asked[0])

            def low(dst, src, hi):
                lows[0] += 1
                dve.wait_ge(hT_hi, lows[0])
                dve.tensor_tensor(dst, src, hi.bitcast(F32), ALU.subtract).then_inc(hT_lo, 1)

            def ada(l):
                u0, b0 = base["ada", l], first["ada", l]["B"]

                def rows_out(j, i=0):
                    g = b0 + j
                    dve.wait_ge(psB_full, g + 1 + 6 * i)
                    dve.tensor_copy(mrow[0:4, bass.ds((j + 6 * i) * YN, YN)] if not isinstance(i, int)
                                    else mrow[0:4, (j + 6 * i) * YN:(j + 6 * i + 1) * YN],
                                    psB[g % 3][0:4, 0:YN]).then_inc(psB_free, 1)

                for j in range(6):
                    split_lo(u0 + AHEAD + j)
                    rows_out(j)
                with dve.Fori(1, 3) as i:
                    for j in range(6):
                        split_lo(u0 + AHEAD + j, i, 6)
                        rows_out(j, i)
                for j in range(6):
                    split_lo(u0 + AHEAD + 18 + j)
                    rows_out(j, 3)

            def mods(l):
                f = first["mods", l]
                g = f["T"]
                dve.wait_ge(psT_full, g + 1)
                v = psT[g % 2][:, 0:8 * KD].rearrange("p (k f c) -> p k f c", k=4, f=KD)
                for k in (1, 3):
                    gain = vecs[:, V_N[l, k // 2]:V_N[l, k // 2] + KD]
                    for c in range(2):
                        link(dve.scalar_tensor_tensor(out=mod[:, k, :, c], in0=v[:, k, :, c], scalar=1.0, in1=gain,
                                                      op0=ALU.add, op1=ALU.mult))
                link(dve.tensor_copy(mod[:, 0, :, :], v[:, 0, :, :]))
                dve.tensor_copy(mod[:, 2, :, :], v[:, 2, :, :]).then_inc(psT_free, 1)
                for n in range(8):
                    gate, cond, half = n // 4, n // 2 % 2, n % 2
                    g = f["B"] + n
                    dve.wait_ge(psB_full, g + 1)
                    dve.tensor_copy(gate_b[:, gate, cond, half * 512:(half + 1) * 512],
                                    psB[g % 3][:, :]).then_inc(psB_free, 1)

            norms = [0]

            def norm(l, w):
                n, g0 = norms[0], first["norm", l, w]["T"]
                norms[0] += 1
                if n == 3:
                    dve.wait_ge(state_out, 96)
                dve.wait_ge(sumsq, n + 1)
                dve.wait_ge(psT_free, first["mods", l]["T"] + 1)
                link(dve.reciprocal(stats[:, 28:31], stats[:, 4:7]))
                for t in range(NT):
                    ins = dve.tensor_scalar(xn[:, t, :], x[:, t, :], stats[:, 28 + t:29 + t], None, ALU.mult)
                    if t < NT - 1:
                        link(ins)
                ins.then_inc(xn_ready, 1)
                for f in range(KD + 1):
                    if f < KD:
                        g = g0 + f
                        dve.wait_ge(psT_full, g + 1)
                        if f >= 2:
                            dve.wait_ge(hT_lo, lows[0])
                        for c, (a, b) in enumerate(((0, P), (P, TOK))):
                            ins = dve.tensor_scalar(hf[:, f % 2, a:b], psT[g % 2][:, a:b],
                                                    mod[:, 2 * w + 1, f, c:c + 1], mod[:, 2 * w, f, c:c + 1],
                                                    ALU.mult, ALU.add)
                            if c == 0:
                                link(ins)
                        ins.then_inc(psT_free, 1)
                    if f > 0:
                        low(hTl[:, f - 1, :], hf[:, (f - 1) % 2, :], hTh[:, f - 1, :])

            def rms_heads(z, heads, hd):
                sq = scr[:, 0:heads * hd].rearrange("p (h d) -> p h d", h=heads)
                link(dve.tensor_tensor(sq, z, z, ALU.mult))
                ask_root(dve.tensor_reduce(stats[:, SS:SS + heads], sq, AX.X, ALU.add))
                link(dve.reciprocal(stats[:, RC:RC + heads], stats[:, RT:RT + heads]))

            def scaled(z, heads, hd, at, gain, factor=1.0):
                r = stats[:, RC + at:RC + at + heads].unsqueeze(2).to_broadcast([P, heads, hd])
                link(dve.scalar_tensor_tensor(out=z, in0=z, scalar=factor, in1=r, op0=ALU.mult, op1=ALU.mult))
                link(dve.tensor_tensor(z, z, gain.unsqueeze(1).to_broadcast([P, heads, hd]), ALU.mult))

            def rope(z, heads, w, t, at_c, at_s):
                cos = cst[:, at_c + (t - 1) * w:at_c + t * w].unsqueeze(1).to_broadcast([P, heads, w])
                sin = cst[:, at_s + (t - 1) * w:at_s + t * w].unsqueeze(1).to_broadcast([P, heads, w])
                rot = scr[:, 0:heads * w].rearrange("p (h d) -> p h d", h=heads)
                h = w // 2
                link(dve.tensor_tensor(rot[:, :, 0:h], z[:, :, h:w], sin[:, :, 0:h], ALU.mult))
                link(dve.tensor_tensor(rot[:, :, h:w], z[:, :, 0:h], sin[:, :, h:w], ALU.mult))
                link(dve.tensor_tensor(z, z, cos, ALU.mult))
                return dve.tensor_tensor(z, z, rot, ALU.add)

            marked = [-1]

            def nothing():
                marked[0] += 1
                return dve.memset(marks[:, marked[0]:marked[0] + 1], 0.0)

            def columns_out(u, g, dst):
                dve.wait_ge(psB_full, g + 1)
                dve.tensor_copy(dst, psB[g % 3][:, 0:units[u][2]]).then_inc(psB_free, 1)

            taps = [0]

            def tap():
                n = taps[0]
                if n >= CW * CT:
                    return
                taps[0] += 1
                w, c = divmod(n, CT)
                src, k = cpad[:, c, w:w + COUT], dww[:, n:n + 1]
                if w == 0:
                    ins = dve.tensor_scalar(yc[:, c, :], src, k, vecs[:, V_DWB + c:V_DWB + c + 1], ALU.mult, ALU.add)
                else:
                    dve.wait_ge(conv_chain, n - CT + 1)
                    ins = dve.scalar_tensor_tensor(out=yc[:, c, :], in0=src, scalar=k, in1=yc[:, c, :],
                                                   op0=ALU.mult, op1=ALU.add)
                ins.then_inc(conv_chain, 1)

            def attend(a):
                cfg, f = ATT[a], first[f"attend{a}"]
                per = cfg["per"]
                for i in range(NS + 2):
                    if i < NS:
                        n = P * len(keys_of(i // 8))
                        g = f["A"] + i
                        dve.wait_ge(psA_full, g + 1)
                        dve.tensor_reduce(stats[:, 32 + i:33 + i], psA[g % 3][:, 0:n], AX.X,
                                          ALU.min).then_inc(bias_ready, 1)
                    if a == 0:
                        for _ in range(5):
                            tap()
                    if 1 <= i <= NS:
                        s = i - 1
                        n = P * len(keys_of(s // 8))
                        g = tgroup(a, s)
                        dve.wait_ge(psT_full, g + 1)
                        if s >= 2:
                            dve.wait_ge(*pv_signal(a, s - 2))
                        dve.tensor_copy(cfg["PT"][:, s % 2, 0:n], psT[g % 2][:, 0:n]).then_inc(psT_free, 1)
                    if i >= 2 and (i - 2) % per == per - 1:
                        rows_ready(a, (i - 2) // per)
                    if i in (otile_at(0), otile_at(1)):
                        o_low(a, i // 8 - 1)
                o_low(a, NT - 1)

            def o_low(a, t):
                k = otgroup(a, t)
                c = slice(cfg_ft(a), cfg_ft(a) + 4)
                lows[0] += 1
                dve.wait_ge(hT_hi, lows[0])
                link(dve.tensor_tensor(hTl[:, c, t * P:(t + 1) * P],
                                       psT[k % 2][:, :].rearrange("p (f n) -> p f n", f=4),
                                       hTh[:, c, t * P:(t + 1) * P].bitcast(F32), ALU.subtract))
                nothing().then_inc(psT_free, 1)
                nothing().then_inc(hT_lo, 1)

            def cfg_ft(a):
                return ATT[a]["ft"]

            def rows_ready(a, m):
                cfg, f = ATT[a], first[f"attend{a}"]
                per, n = cfg["per"], cfg["n"]
                t = m * per // 8
                g = f["B"] + m
                dve.wait_ge(psB_full, g + 1)
                dve.wait_ge(psA_free, f["A"] + (m + 1) * per)
                link(dve.reciprocal(stats[:, 16:16 + per], stats[:, 64 + m * per:64 + (m + 1) * per]))
                r = stats[:, 16:16 + per].unsqueeze(2).to_broadcast([P, per, n])
                src = psB[g % 3][:, :].rearrange("p (h d) -> p h d", h=per)
                if NT * a + t >= 1 and (a != 1 or m % 2 == 0):
                    pa, pt = divmod(NT * a + t - 1, NT)
                    dve.wait_ge(psT_full, otgroup(pa, pt) + 1)
                if a != 1:
                    dve.tensor_tensor(otok.rearrange("p (h d) -> p h d", h=per), src, r, ALU.mult).then_inc(psB_free, 1)
                    dve.wait_ge(psB_free, g + 1)
                    nothing().then_inc(o_ready, 1)
                    return
                o4 = osb.rearrange("p (h j d) -> p h j d", h=2, j=2)
                dve.tensor_tensor(osb.rearrange("p (h d) -> p h d", h=per), src, r, ALU.mult).then_inc(psB_free, 1)
                dve.wait_ge(psB_free, g + 1)
                o2 = od.rearrange("p (h d) -> p h d", h=2)
                link(dve.scalar_tensor_tensor(out=o2, in0=o4[:, :, 1, :], scalar=stats[:, 92:93], in1=o4[:, :, 0, :],
                                              op0=ALU.mult, op1=ALU.add))
                sq = scr[:, 0:256].rearrange("p (h d) -> p h d", h=2)
                link(dve.tensor_tensor(sq, o2, o2, ALU.mult))
                ask_root(dve.tensor_reduce(stats[:, 10:12], sq, AX.X, ALU.add))
                link(dve.reciprocal(stats[:, 14:16], stats[:, 12:14]))
                link(dve.scalar_tensor_tensor(out=o2, in0=o2, scalar=1.0 - LAMBDA_INIT,
                                              in1=stats[:, 14:16].unsqueeze(2).to_broadcast([P, 2, P]),
                                              op0=ALU.mult, op1=ALU.mult))
                half = m % 2
                ins = dve.tensor_tensor(otok[:, half * 256:(half + 1) * 256].rearrange("p (h d) -> p h d", h=2), o2,
                                        G["l1_diff_subln_g"].unsqueeze(1).to_broadcast([P, 2, P]), ALU.mult)
                if half == 1:
                    ins.then_inc(o_ready, 1)
                else:
                    link(ins)

            def gated(g, t, j, gate, y0, i=0, weight=None):
                n = y0 + NT * j + t
                if n - 2 > 0:
                    dve.wait_ge(x_added, n - 2 + 12 * i)
                dve.wait_ge(psB_full, g + 1 + 24 * i)
                gb = gate_b[:, gate, 0 if t == 0 else 1, j * YN:(j + 1) * YN]
                if weight is None:
                    ins = dve.tensor_tensor(ytmp[:, t, :], psB[g % 3][:, 0:YN], gb, ALU.mult)
                else:
                    ins = dve.scalar_tensor_tensor(out=ytmp[:, t, :], in0=psB[g % 3][:, 0:YN], scalar=weight, in1=gb,
                                                   op0=ALU.mult, op1=ALU.mult)
                ins.then_inc(psB_free, 1)

            def out_projection(l, y0):
                for j in range(YC):
                    step(base["out", l] + j)
                    for t in range(NT):
                        gated(first["out", l]["B"] + NT * j + t, t, j, 0, y0)

            def ffn(l, y0, h0):
                u0, f, k = base["ffn", l], first["ffn", l], (2 if l == 0 else NE)
                with dve.Fori(0, k) as i:
                    if l == 1:
                        dve.wait_ge(psB_free, f["B"] + 24 * i)
                        dve.tensor_copy(comb_e[:, :], comb[:, :, bass.ds(i, 1)].rearrange("p t e -> p (t e)")
                                        ).then_inc(comb_ready, 1)
                        dve.wait_ge(comb_ready, i + 1)
                    for j in range(3 * FC):
                        if j + AHEAD < 3 * FC or l == 0:
                            split_lo(u0 + j + AHEAD, i)
                        else:
                            with dve.If(i < k - 1):
                                split_lo(u0 + j + AHEAD, i)
                        if j < 2 * FC and j % 2:
                            c = j // 2
                            for t in range(NT):
                                g = f["B"] + NT * c + t
                                dve.wait_ge(psA_free, f["A"] + NT * c + t + 1 + 12 * i)
                                dve.wait_ge(psB_full, g + 1 + 24 * i)
                                dst = gt[:, t, c * FN:(c + 1) * FN]
                                dve.tensor_tensor(dst, dst, psB[g % 3][:, 0:FN], ALU.mult).then_inc(psB_free, 1)
                        for q in TGROUPS.get(j, ()):
                            dve.wait_ge(gT_hi, h0 + q + 1 + FT * i)
                            dve.tensor_tensor(gTl[:, q, :], psT[q % 2][:, 0:TOK], gTh[:, q, :].bitcast(F32),
                                              ALU.subtract).then_inc(psT_free, 1)
                        if j >= 2 * FC:
                            for t in range(NT):
                                gated(f["B"] + 12 + NT * (j - 2 * FC) + t, t, j - 2 * FC, 1, y0, i,
                                      comb_e[:, t:t + 1])

            link(dve.memset(chl[:, :, :].bitcast(F32), 0.0))
            link(dve.memset(comb_e[:, :], 1.0))
            dve.wait_ge(psT_full, 2)
            dve.tensor_copy(vecs[:, :], psT[0][:, 0:60]).then_inc(psT_free, 1)
            dve.tensor_copy(dww[:, :], psT[1][:, 0:CW * CT]).then_inc(psT_free, 1)
            dve.wait_ge(c_silu, 1)
            for c in range(2):
                cs = csil[:, c * KD:(c + 1) * KD]
                link(dve.tensor_copy(chl[:, :, 2 * c], cs))
                ins = dve.tensor_tensor(chl[:, :, 2 * c + 1], cs, chl[:, :, 2 * c].bitcast(F32), ALU.subtract)
                if c == 0:
                    link(ins)
            ins.then_inc(c_ready, 1)
            for u in range(AHEAD):
                split_lo(u)

            ada(0)
            mods(0)
            norm(0, 0)
            dve.wait_ge(pool_chain, 1)
            for j in range(CT):
                step(base["in", 0] + j)
                g = first["in0"]["B"] + j
                dve.wait_ge(psA_free, first["in0"]["A"] + j + 1)
                dve.wait_ge(psB_full, g + 1)
                for at, tok, n in CSEG:
                    ins = dve.tensor_tensor(cpad[:, j, at:at + n], psB[g % 3][:, tok:tok + n],
                                            hf[:, j % 2, tok:tok + n], ALU.mult)
                    if tok == 0:
                        link(ins)
                ins.then_inc(psB_free, 1)
            for j in range(3):
                u = base["in", 0] + CT + j
                step(u)
                for t in range(NT):
                    g = first["in0"]["B"] + CT + NT * j + t
                    if j < 2:
                        dve.wait_ge(psB_full, g + 1)
                        dve.tensor_copy(zq[:, t, 0:512].rearrange("p (h k d) -> p h k d", h=4, k=2)[:, :, j, :],
                                        psB[g % 3][:, 0:256].rearrange("p (h d) -> p h d", h=4)).then_inc(psB_free, 1)
                    else:
                        columns_out(u, g, zq[:, t, 512:768])
            dve.wait_ge(psB_free, first["in0"]["B"] + CT + 9)
            dve.wait_ge(gains_in, 16 * len(G))
            g0 = first["prep0"]["T"]
            for t in range(NT):
                z = zq[:, t, 0:640].rearrange("p (h d) -> p h d", h=10)
                rms_heads(z, 10, HD)
                scaled(z[:, 0:8, :], 8, HD, 0, G["l0_q_norm_g"], -(HD ** -0.5))
                scaled(z[:, 8:10, :], 2, HD, 8, G["l0_k_norm_g"])
                (rope(z, 10, HD, t, C_COS, C_SIN) if t else nothing()).then_inc(z_ready, 1)
                dve.wait_ge(z_ready, t + 1)
                dve.wait_ge(psT_full, g0 + t + 1)
                dve.tensor_copy(qT0[:, :, t * P:(t + 1) * P],
                                psT[(g0 + t) % 2][:, :].rearrange("p (f n) -> p f n", f=4)).then_inc(psT_free, 1)
            dve.wait_ge(psT_full, g0 + 4)
            dve.tensor_copy(kT0[:, :], psT[(g0 + 3) % 2][:, :]).then_inc(psT_free, 1)
            attend(0)
            while taps[0] < CW * CT:
                tap()
            dve.wait_ge(conv_chain, CW * CT)
            nothing().then_inc(ln_in, 1)
            g = first["lnorm"]["B"]
            dve.wait_ge(psB_full, g + 1)
            for c in range(CT):
                ins = dve.tensor_tensor(yc[:, c, :], yc[:, c, :], psB[g % 3][:, 0:COUT], ALU.subtract)
                if c < CT - 1:
                    link(ins)
            ins.then_inc(psB_free, 1)
            dve.wait_ge(psB_free, g + 1)
            for c in range(CT):
                ins = dve.tensor_tensor(cpad[:, c, 0:COUT], yc[:, c, :], yc[:, c, :], ALU.mult)
                if c < CT - 1:
                    link(ins)
            ins.then_inc(ln_in, 1)
            g += 1
            dve.wait_ge(psB_full, g + 1)
            link(dve.tensor_copy(hf[:, 0, 0:P], psB[g % 3][:, 0:P]))
            dve.tensor_copy(hf[:, 0, P:TOK], psB[g % 3][:, 2 * PAD + P:COUT]).then_inc(psB_free, 1)
            dve.wait_ge(psB_free, g + 1)
            ask_root(nothing())
            link(dve.reciprocal(hf[:, 0, :], hf[:, 1, :]))
            for c in range(CT):
                link(dve.tensor_tensor(yv(c)[:, 0:P], yc[:, c, 0:P], hf[:, 0, 0:P], ALU.mult))
                dve.tensor_tensor(yv(c)[:, P:TOK], yc[:, c, 2 * PAD + P:COUT], hf[:, 0, P:TOK],
                                  ALU.mult).then_inc(ln_out, 1)
            for c in range(CT):
                low(hTl[:, c, :], ysil[:, c, :], hTh[:, c, :])
            out_projection(0, 0)
            norm(0, 1)
            dve.wait_ge(state_out, 32)
            ffn(0, 12, 0)

            ada(1)
            mods(1)
            dve.wait_ge(x_added, 36)
            for n, (q, k) in enumerate((("l1_lambda_q1", "l1_lambda_k1"), ("l1_lambda_q2", "l1_lambda_k2"))):
                link(dve.tensor_tensor(hf[:, 0, 0:HD], G[q], G[k], ALU.mult))
                ins = dve.tensor_reduce(stats[:, 88 + n:89 + n], hf[:, 0, 0:HD], AX.X, ALU.add)
                if n == 0:
                    link(ins)
            ins.then_inc(lam_in, 1)
            norm(1, 0)
            for j in range(8):
                u = base["in", 1] + j
                step(u)
                for t in range(NT):
                    dst = zd[:, t, j * 256:(j + 1) * 256] if j < 6 else (
                        zm[:, t, 0:256] if j == 6 else zm[:, t, 256:416])
                    columns_out(u, first["in1"]["B"] + NT * j + t, dst)
            dve.wait_ge(psB_free, first["in1"]["B"] + 24)
            dve.wait_ge(lam_e, 1)
            link(dve.tensor_tensor(stats[:, 93:94], stats[:, 91:92], stats[:, 90:91], ALU.subtract))
            link(dve.tensor_scalar(stats[:, 92:93], stats[:, 93:94], -LAMBDA_INIT, None, ALU.add))
            g0 = first["prep1"]["T"]
            for n in range(7):
                t = n // 2
                if n % 2 == 0 and t < NT:
                    z = zd[:, t, 0:2 * DIFF_W].rearrange("p (h d) -> p h d", h=16)
                    rms_heads(z, 16, HD)
                    scaled(z[:, 0:8, :], 8, HD, 0, G["l1_diff_q_norm_g"], -(HD ** -0.5))
                    scaled(z[:, 8:16, :], 8, HD, 8, G["l1_diff_k_norm_g"])
                    (rope(z, 16, HD, t, C_COS, C_SIN) if t else nothing()).then_inc(z_ready, 1)
                    dve.wait_ge(z_ready, NT + t + 1)
                dve.wait_ge(psT_full, g0 + n + 1)
                dst = qT1 if n % 2 == 0 and t < NT else kT1
                dve.tensor_copy(dst[:, :, t * P:(t + 1) * P],
                                psT[(g0 + n) % 2][:, :].rearrange("p (f n) -> p f n", f=4)).then_inc(psT_free, 1)
            attend(1)
            dve.wait_ge(psB_free, first["in1"]["B"] + 24)
            for at, n, name in ((0, QR, "l1_mla_q_a_norm_g"), (QR, KVR, "l1_mla_kv_a_norm_g")):
                z = zm[:, :, at:at + n]
                rms_heads(z, NT, n)
                scaled(z, NT, n, 0, G[name])
            nothing().then_inc(z_ready, 1)
            g0 = first["latT"]["T"]
            for q in range(3):
                g = g0 + q
                n = TOK if q < 2 else 4 * P
                dst, hi = ((hTl[:, 4 + q, :], hTh[:, 4 + q, :]) if q < 2 else (ckvT(hTl), ckvT(hTh)))
                lows[0] += 1
                dve.wait_ge(hT_hi, lows[0])
                link(dve.tensor_tensor(dst, psT[g % 2][:, 0:n], hi.bitcast(F32), ALU.subtract))
                nothing().then_inc(psT_free, 1)
                nothing().then_inc(hT_lo, 1)
            dve.wait_ge(state_out, 64)
            b0 = first["lat"]["B"]
            for j in range(4):
                u = base["lat", 1] + j
                step(u)
                for t in range(NT if j < 2 else 4):
                    if j < 2:
                        columns_out(u, b0 + NT * j + t, qm[:, t, j * 384:(j + 1) * 384])
                    else:
                        columns_out(u, b0 + 2 * NT + 4 * (j - 2) + t, kv[:, t, (j - 2) * 512:(j - 1) * 512])
            dve.wait_ge(psB_free, b0 + 14)
            g0 = first["prep2"]["T"]
            for m in range(7):
                t = m if m < NT else m - NT
                if m < NT:
                    z = qm[:, t, :].rearrange("p (h d) -> p h d", h=MLA_H)
                    name, factor = "l1_mla_q_norm_g", -(QK ** -0.5)
                else:
                    z = ktmp[:, t % 2, :].rearrange("p (h d) -> p h d", h=MLA_H)
                    name, factor = "l1_mla_k_norm_g", 1.0
                    kr = zm[:, t, QR + KVR:416] if t < NT else ckr[:, :]
                    link(dve.tensor_copy(z[:, :, 0:NOPE],
                                         kv[:, t, :].rearrange("p (h d) -> p h d", h=MLA_H)[:, :, 0:NOPE]))
                    link(dve.tensor_copy(z[:, :, NOPE:QK], kr.unsqueeze(1).to_broadcast([P, MLA_H, ROPE])))
                rms_heads(z, MLA_H, QK)
                scaled(z, MLA_H, QK, 0, G[name], factor)
                (rope(z[:, :, NOPE:QK], MLA_H, ROPE, t, C_COSR, C_SINR) if t in (1, 2) else nothing()
                 ).then_inc(z_ready, 1)
                dve.wait_ge(z_ready, 7 + m + 1)
                for half in range(2):
                    g = g0 + 2 * m + half
                    dve.wait_ge(psT_full, g + 1)
                    dst = (qT2 if m < NT else kT2)[0:QK, 4 * half:4 * half + 4, t * P:(t + 1) * P]
                    dve.tensor_copy(dst, psT[g % 2][0:QK, :].rearrange("p (f n) -> p f n", f=4)).then_inc(psT_free, 1)
            attend(2)
            out_projection(1, 36)
            norm(1, 1)
            step(base["router"])
            g = first["router"]["B"]
            dve.wait_ge(psB_full, g + NT)
            for t in range(NT):
                b = psB[(g + t) % 3][:, 0:NE]
                link(dve.max(mx8[:, t, :], b))
                dve.max_index(ix8[:, t, :], mx8[:, t, :], b).then_inc(psB_free, 1)
            dve.wait_ge(psB_free, g + NT)
            link(dve.tensor_copy(ix8f[:, :, :], ix8[:, :, :]))
            dve.tensor_tensor(rt[:, 0:3], mx8[:, :, 1], mx8[:, :, 0], ALU.subtract).then_inc(router_in, 1)
            dve.wait_ge(logit_e, 1)
            link(dve.tensor_scalar(rt[:, 8:11], rt[:, 4:7], 1.0, None, ALU.add))
            link(dve.reciprocal(rt[:, 12:15], rt[:, 8:11]))
            link(dve.tensor_tensor(rt[:, 16:19], rt[:, 12:15], rt[:, 4:7], ALU.mult))
            iota = cst[:, C_IOTA:C_IOTA + NE]
            for t in range(NT):
                link(dve.tensor_scalar(rt[:, 40:48], iota, ix8f[:, t, 0:1], None, ALU.is_equal))
                link(dve.scalar_tensor_tensor(out=mask[:, t, :], in0=iota, scalar=ix8f[:, t, 1:2], in1=rt[:, 40:48],
                                              op0=ALU.is_equal, op1=ALU.add))
                link(dve.tensor_scalar(rt[:, 24:32], rt[:, 40:48], rt[:, 12 + t:13 + t], None, ALU.mult))
                link(dve.tensor_scalar(rt[:, 32:40], iota, ix8f[:, t, 1:2], rt[:, 16 + t:17 + t],
                                       ALU.is_equal, ALU.mult))
                link(dve.tensor_tensor(comb[:, t, :], rt[:, 24:32], rt[:, 32:40], ALU.add))
            nothing().then_inc(mask_ready, 1)
            g = first["tables"]["B"]
            dve.wait_ge(psB_full, g + 1)
            all_places = slot[:, :, 0:NE]
            link(dve.tensor_tensor(all_places, psB[g % 3][:, 0:NT * NE].rearrange("p (t e) -> p t e", t=NT),
                                   mask[:, :, :], ALU.mult))
            link(dve.tensor_scalar(all_places, all_places, -1.0, None, ALU.add))
            dve.tensor_copy(jobs[:, 0:NE], psB[g % 3][:, NT * NE:(NT + 1) * NE]).then_inc(psB_free, 1)
            dve.wait_ge(psB_free, g + 1)
            link(dve.tensor_scalar(jobs[:, 8:16], jobs[:, 0:8], P + 0.5, None, ALU.is_gt))
            link(dve.scalar_tensor_tensor(out=jobs[:, 16:24], in0=jobs[:, 0:8], scalar=2 * P + 0.5,
                                          in1=jobs[:, 8:16], op0=ALU.is_gt, op1=ALU.add))
            for e in range(1, NE):
                link(dve.tensor_tensor(jobs[:, 16 + e:17 + e], jobs[:, 15 + e:16 + e], jobs[:, 16 + e:17 + e],
                                       ALU.add))
            run = jobs[:, 16:24].unsqueeze(1).to_broadcast([P, EXTRA, NE])
            below = jobs[:, 24:24 + EXTRA * NE].rearrange("p (j e) -> p j e", j=EXTRA)
            link(dve.tensor_tensor(below, run, iota[:, 0:EXTRA].unsqueeze(2).to_broadcast([P, EXTRA, NE]),
                                   ALU.is_le))
            link(dve.tensor_copy(jobs[:, 64:65], jobs[:, 23:24]))
            link(dve.tensor_reduce(jobs[:, 65:65 + EXTRA], below, AX.X, ALU.add))
            link(dve.tensor_scalar(jobs[:, 65:65 + EXTRA], jobs[:, 65:65 + EXTRA], NE - 1.0, None, ALU.min))
            link(dve.tensor_tensor(below, below, run, ALU.mult))
            link(dve.tensor_reduce(jobs[:, 72:72 + EXTRA], below, AX.X, ALU.max))
            link(dve.tensor_tensor(jobs[:, 80:80 + EXTRA], iota[:, 0:EXTRA], jobs[:, 72:72 + EXTRA], ALU.subtract))
            link(dve.tensor_scalar(jobs[:, 88:88 + EXTRA], jobs[:, 80:80 + EXTRA], float(P), float(P),
                                   ALU.mult, ALU.add))
            dve.tensor_copy(jobs_i[:, 0:1 + EXTRA], jobs[:, 64:65 + EXTRA]).then_inc(table_ready, 1)
            for q in range(2 * NT):
                g = first["tokens"]["B"] + q
                dve.wait_ge(psB_full, g + 1)
                dve.tensor_copy(toks_l[:, q // 2, q % 2 * 512:(q % 2 + 1) * 512], psB[g % 3][:, :]).then_inc(psB_free, 1)
            f = first["jobs"]

            def choose(e, n, start):
                if isinstance(e, int):
                    src = slot[:, :, e]
                else:
                    src = slot[:, :, bass.ds(e, 1)].rearrange("p t e -> p (t e)")
                dve.tensor_scalar(slot_e[:, :], src, start, None, ALU.subtract).then_inc(place_ready, 1)
                dve.wait_ge(place_ready, n + 1)
                for t in range(NT):
                    ins = dve.tensor_scalar(pick[:, t, :], jcst[:, 2 * P:3 * P], slot_e[:, t:t + 1], None,
                                            ALU.is_equal)
                    ins.then_inc(pick_part if t < NT - 1 else pick_ready, 1)

            def split_half(h, n):
                dve.wait_ge(half_hi, h + 1 + HALVES * n)
                dve.tensor_tensor(half_of(Wl, h), half_of(raw, h), half_of(Wh, h).bitcast(F32),
                                  ALU.subtract).then_inc(half_lo, 1)

            def turned(j, n):
                for g, tiles in JT.get(j, ()):
                    k = len(tiles)
                    dve.wait_ge(gT_hi, 2 * FT + g + (JOB_T - 1) * n)
                    c = slice(tiles[0], tiles[-1] + 1)
                    dve.tensor_tensor(mTl[:, c, :], psT[g % 2][:, 0:P * k].rearrange("p (f n) -> p f n", f=k),
                                      mTh[:, c, :].bitcast(F32), ALU.subtract).then_inc(psT_free, 1)

            def given_back(c, n):
                for t in range(NT):
                    b = ADD_AT[c] + t
                    dve.wait_ge(x_added, 48 + NT * c + t - 3 + 12 * n)
                    dve.wait_ge(psB_full, f["B"] + b + 1 + JOB_B * n)
                    dve.scalar_tensor_tensor(out=ytj[:, (NT * c + t) % 4, :], in0=psBj[b % 4][:, 0:YN],
                                             scalar=comb_e[:, t:t + 1],
                                             in1=gate_b[:, 1, 0 if t == 0 else 1, c * YN:(c + 1) * YN],
                                             op0=ALU.mult, op1=ALU.mult).then_inc(psB_free, 1)

            def job(i, one_each):
                n = i if one_each else i + NE
                if one_each:
                    e = i
                else:
                    e = dve.value_load(jobs_i[0:1, bass.ds(i + 1, 1)], min_val=0, max_val=NE - 1)
                    for h in range(HSLOTS - 1):
                        split_half(h, n)
                    choose(e, n, jobs[:, bass.ds(i + 88, 1)])
                dve.wait_ge(psB_free, f["B"] + JOB_B * n)
                dve.tensor_copy(comb_e[:, :], comb[:, :, bass.ds(e, 1)].rearrange("p t e -> p (t e)")
                                ).then_inc(comb_ready, 1)
                dve.wait_ge(comb_ready, n + 1)
                for h in range(HALVES):
                    j = h // 2
                    ahead = h + HSLOTS - 1
                    if ahead < HALVES:
                        split_half(ahead, n)
                    elif one_each:
                        with dve.If(i < NE - 1):
                            split_half(ahead - HALVES, n + 1)
                    if h == 1:
                        dve.wait_ge(psT_full, f["T"] + 1 + JOB_T * n)
                        dve.tensor_copy(pickT[:, :], psT[0][:, 0:TOK]).then_inc(psT_free, 1)
                    if h == 8 and one_each:
                        with dve.If(i < NE - 1):
                            dve.wait_ge(pick_ready, n + 1)
                            choose(i + 1, n + 1, 0.0)
                    if h == 4 * FC:
                        turned(j, n)
                    if h % 2 == 0:
                        continue
                    if j < 2 * FC and j % 2:
                        c = j // 2
                        dve.wait_ge(psA_free, f["A"] + FC + c + 1 + JOB_A * n)
                        dve.wait_ge(psB_full, f["B"] + c + 1 + JOB_B * n)
                        dst = gj[:, c * FN:(c + 1) * FN]
                        dve.tensor_tensor(dst, dst, psBj[c % 4][:, 0:FN], ALU.mult).then_inc(psB_free, 1)
                    elif j < 2 * FC:
                        turned(j, n)
                    else:
                        c = j - 2 * FC
                        dve.wait_ge(y_hi, c + 1 + YC * n)
                        dve.tensor_tensor(yl[:, c % 2, :], psBj[W2_AT[c] % 4][:, 0:YN], yh[:, c % 2, :].bitcast(F32),
                                          ALU.subtract).then_inc(psB_free, 1)
                        if c > 0:
                            given_back(c - 1, n)
                given_back(YC - 1, n)

            for h in range(HSLOTS - 1):
                split_half(h, 0)
            dve.wait_ge(jcst_in, 16)
            choose(0, 0, 0.0)
            over_jobs(dve, job)


_OUTS = [(1, P, D), (1, 2 * P, D), (1, P, 2, HD), (1, P, 2, HD), (1, P, 4, 2, HD), (1, P, 4, 2 * HD),
         (1, P, KVR), (1, P, ROPE)]


def kernel(**inputs):
    import concourse.bacc as _bacc
    from concourse.bass_utils import run_bass_kernel_spmd as _run

    nc = _bacc.Bacc("TRN2", target_bir_lowering=False, num_devices=1)
    arrays = {f"in_{n}": np.ascontiguousarray(a) for n, a in inputs.items()}
    arrays["in_consts"] = constants()
    arrays["in_job_consts"] = job_constants()
    A = {n[3:]: nc.dram_tensor(n, a.shape, mybir.dt.from_np(a.dtype), kind="ExternalInput").ap()
         for n, a in arrays.items()}
    out = [nc.dram_tensor(f"out_{i}", s, F32, kind="ExternalOutput").ap() for i, s in enumerate(_OUTS)]
    trunk_step(nc, A, out)
    r = _run(nc, [arrays], core_ids=[0])
    return tuple(r.results[0][f"out_{i}"] for i in range(len(_OUTS)))
```

```python
import math
from contextlib import ExitStack

import numpy as np

import concourse.bass as bass
from concourse import mybir

F32 = mybir.dt.float32
F32R = mybir.dt.float32r
U32 = mybir.dt.uint32
I32 = mybir.dt.int32
ACT = mybir.ActivationFunctionType
ALU = mybir.AluOpType
AX = mybir.AxisListType

P = 128
D = 1024
KD = D // P
NT = 3
TOK = NT * P
NC = 512
CT = NC // P
CW = 31
PAD = CW // 2
CSEG = [(PAD, 0, P), (3 * PAD + P, P, 2 * P)]
CLEN = 4 * PAD + TOK
COUT = CLEN - 2 * PAD
CT_V = 2
HD = 64
DIFF_W = 512
MLA_H, NOPE, ROPE, VD, QR, KVR = 8, 64, 32, 64, 256, 128
QK = NOPE + ROPE
LAMBDA_INIT = 0.8 - 0.6 * math.exp(-0.3 * 1)
NE = 8
FE = 1408
FT = FE // P
FC = 4
FN = FE // FC
YC = 4
YN = D // YC
RMS_EPS = 1e-6
LN_EPS = 1e-5

R = 2
R_SMALL = 3
S = 2
SLOT = 3072
assert SLOT >= KD * FN == FT * YN
AHEAD = S - 1

HALVES = 6 * FC
HSLOTS = 4
HSLOT = R * SLOT // HSLOTS
HALF_K = [(0, 4), (4, 8)], [(0, 6), (6, 11)]
GATHER_AT = [4 * FC - 1, 4 * FC, 4 * FC + 2, 4 * FC + 4]
EXTRA = 5
JOB_A, JOB_B, JOB_T = 4, 16, 6
JOB_GROUPS = [("u", 0), ("u", 1), ("u", 2), ("u", 3), ("d", 0), ("d", 1), ("b", 0), ("b", 0), ("d", 2),
              ("b", 1), ("b", 1), ("d", 3), ("b", 2), ("b", 2), ("b", 3), ("b", 3)]
JOB_BANK = [0, 1, 2, 3, 0, 1, 2, 3, 0, 2, 3, 1, 2, 3, 0, 1]
W2_AT = [JOB_GROUPS.index(("d", c)) for c in range(YC)]
ADD_AT = [JOB_GROUPS.index(("b", c)) for c in range(YC)]
JOB_V = FC + YC
BACKS = 3 * YC
assert len(JOB_GROUPS) == JOB_B
assert HSLOT >= 6 * YN and HALVES % HSLOTS == 0

C_ID, C_LN = 0, 128
C_COS, C_SIN = 256, 384
C_COSR, C_SINR = 512, 576
C_SEL, C_SELB = 640, 642
C_IOTA, C_EPS = 898, 906
C_END = 908


def constants():
    c = np.zeros((P, C_END), np.float32)
    c[:, C_ID:C_ID + P] = np.eye(P, dtype=np.float32)
    c[:, C_LN:C_LN + P] = np.float32(1.0 / NC)
    n = 2 * P
    row = np.repeat(np.arange(n // 64), 64).astype(np.float32)
    col = np.tile(np.arange(64), n // 64).astype(np.float32)
    for rot, at_c, at_s in ((HD, C_COS, C_SIN), (ROPE, C_COSR, C_SINR)):
        nf = rot // 4
        inv = (np.float32(10000.0) ** (-np.arange(nf, dtype=np.float32) / np.float32(nf))).astype(np.float32)
        ang = np.concatenate([row[:, None] * inv, col[:, None] * inv], axis=-1).astype(np.float32)
        cos, sin = np.cos(ang), np.sin(ang)
        for t in range(2):
            a = slice(t * P, (t + 1) * P)
            c[:, at_c + t * rot:at_c + (t + 1) * rot] = np.concatenate([cos[a], cos[a]], axis=-1)
            c[:, at_s + t * rot:at_s + (t + 1) * rot] = np.concatenate([-sin[a], sin[a]], axis=-1)
    c[[0, 1, 4], C_SEL] = 1.0
    c[[2, 3, 4], C_SEL + 1] = 1.0
    c[[0, 1, 4], C_SELB:C_SELB + P] = 1.0
    c[[2, 3, 4], C_SELB + P:C_SELB + 2 * P] = 1.0
    c[:, C_IOTA:C_IOTA + NE] = np.arange(NE)
    c[:, C_EPS] = RMS_EPS
    c[:, C_EPS + 1] = LN_EPS
    return c


def job_constants():
    return np.concatenate([np.triu(np.ones((P, P))), np.ones((P, P)),
                           np.tile(np.arange(P), (P, 1))], axis=1).astype(np.float32)


def trunk_step(nc, A, out):
    ctx = ExitStack()
    with ctx:
        def sb(name, shape, dt=F32):
            return ctx.enter_context(nc.sbuf_tensor(name, shape, dt))

        def sem(name):
            return ctx.enter_context(nc.semaphore(name))

        x = sb("x", [P, NT, D])
        hTh = sb("hTh", [P, KD, TOK], F32R)
        hTl = sb("hTl", [P, KD, TOK], F32R)
        work = sb("work", [P, NT * FE])
        raw = sb("raw", [P, R * SLOT])
        Wh = sb("Wh", [P, S * SLOT], F32R)
        Wl = sb("Wl", [P, S * SLOT], F32R)
        gate_b = sb("gate_b", [P, 2, 2, D])
        cst = sb("cst", [P, C_END])
        hf = sb("hf", [P, 2, TOK])
        scr = sb("scr", [P, 1024])
        csil = sb("csil", [P, 2 * KD])
        chl = sb("chl", [P, KD, P], F32R)
        vecs = sb("vecs", [P, 60])
        dww = sb("dww", [P, CW * CT])
        mod = sb("mod", [P, 4, KD, 2])
        gains = sb("gains", [P, 1216])
        stats = sb("stats", [P, 160])
        comb = sb("comb", [P, NT, NE])
        comb_e = sb("comb_e", [P, NT])
        mx8 = sb("mx8", [P, NT, 8])
        ix8 = sb("ix8", [P, NT, 8], U32)
        ix8f = sb("ix8f", [P, NT, 8])
        rt = sb("rt", [P, 64])
        mask = sb("mask", [P, NT, NE])
        slot = sb("slot", [P, NT, NE + 2])
        slot_e = sb("slot_e", [P, 2, NT])
        jobs = sb("jobs", [P, 112])
        jobs_i = sb("jobs_i", [P, 8], I32)
        marks = sb("marks", [P, 64])

        cckv = sb("cckv", [P, KVR])
        ckr = sb("ckr", [P, ROPE])

        def phase(*specs):
            with ExitStack() as own:
                return [own.enter_context(nc.sbuf_tensor(n, s, d)) for n, s, d in specs]

        stage, stage_w = phase(("stage", [P, P], F32), ("stage_w", [P, P], F32))
        (mrow,) = phase(("mrow", [P, 6 * D], F32))
        zq, cpad, yc, qT0, kT0, PT0, ck0, cv0 = phase(
            ("zq", [P, NT, 768], F32), ("cpad", [P, CT, CLEN], F32), ("yc", [P, CT, COUT], F32),
            ("qT0", [P, 4, TOK], F32), ("kT0", [P, 4 * P], F32), ("PT0", [P, 2, TOK], F32),
            ("ck0", [P, P], F32), ("cv0", [P, P], F32))
        gTh, gTl = phase(("gTh", [P, FT, TOK], F32R), ("gTl", [P, FT, TOK], F32R))
        zd, qT1, kT1, PT1, cdk, cdv = phase(
            ("zd", [P, NT, 3 * DIFF_W], F32), ("qT1", [P, 4, TOK], F32), ("kT1", [P, 4, 4 * P], F32),
            ("PT1", [P, 2, TOK], F32), ("cdk", [P, DIFF_W], F32), ("cdv", [P, DIFF_W], F32))
        kv, kT2, qT2 = phase(
            ("kv", [P, 4, 1024], F32), ("kT2", [P, 8, 4 * P], F32), ("qT2", [P, 8, TOK], F32))
        PT2 = hf
        toks_h, toks_l, mTh, mTl, yh, yl, pick, pickT = phase(
            ("toks_h", [P, NT, D], F32R), ("toks_l", [P, NT, D], F32R), ("mTh", [P, FT, P], F32R),
            ("mTl", [P, FT, P], F32R), ("yh", [P, 2, YN], F32R), ("yl", [P, 2, YN], F32R),
            ("pick", [P, NT, 2 * P], F32R), ("pickT", [P, TOK], F32R))
        jcst = hf[:, 0, 0:3 * P]

        xn = work[:, 0:NT * D].rearrange("p (t n) -> p t n", t=NT)
        gt = work[:, :].rearrange("p (t n) -> p t n", t=NT)
        zm = work[:, 0:NT * 416].rearrange("p (t n) -> p t n", t=NT)
        ktmp = work[:, 1248:2784].rearrange("p (b n) -> p b n", b=2)
        osb = work[:, 1248:1760]
        od = work[:, 1760:2016]
        Pb = work[:, 2784:3552].rearrange("p (b n) -> p b n", b=2)
        otok = work[:, 3552:4064]
        ysil = work[:, 0:CT * TOK].rearrange("p (c n) -> p c n", c=CT)
        ytmp = scr[:, 0:3 * YN].rearrange("p (b n) -> p b n", b=3)

        ident = cst[:, C_ID:C_ID + P]
        avg = cst[:, C_LN:C_LN + P]
        eps_rms = cst[:, C_EPS:C_EPS + 1]
        eps_ln = cst[:, C_EPS + 1:C_EPS + 2]
        G = {}
        at = 0
        for name, n in (("l0_q_norm_g", HD), ("l0_k_norm_g", HD), ("l1_diff_q_norm_g", HD),
                        ("l1_diff_k_norm_g", HD), ("l1_lambda_q1", HD), ("l1_lambda_k1", HD),
                        ("l1_lambda_q2", HD), ("l1_lambda_k2", HD), ("l1_diff_subln_g", P),
                        ("l1_mla_q_a_norm_g", QR), ("l1_mla_kv_a_norm_g", KVR),
                        ("l1_mla_q_norm_g", QK), ("l1_mla_k_norm_g", QK)):
            G[name] = gains[:, at:at + n]
            at += n
        V_N = {(0, 0): 16, (0, 1): 24, (1, 0): 32, (1, 1): 40}
        V_DWB, V_LNG, V_LNB = 48, 52, 56

        psA = [ctx.enter_context(nc.psum_tensor(f"psA{i}", [P, 512], F32)) for i in range(3)]
        psB = [ctx.enter_context(nc.psum_tensor(f"psB{i}", [P, 512], F32)) for i in range(3)]
        psT = [ctx.enter_context(nc.psum_tensor(f"psT{i}", [P, 512], F32)) for i in range(2)]

        def rows(w):
            return w.rearrange("(k p) n -> p k n", p=P)

        units = []

        def unit(kt, n, *pieces):
            units.append((pieces, kt, n))

        base = {}
        for l in range(2):
            ada = rows(A[f"l{l}_ada_w"])
            w_in, w_out = rows(A[f"l{l}_w_in"]), rows(A[f"l{l}_w_out"])
            base["ada", l] = len(units)
            for u in range(6 * D // YN):
                unit(KD, YN, (0, ada[:, :, u * YN:(u + 1) * YN]))
            base["in", l] = len(units)
            if l == 0:
                for j in range(CT):
                    unit(KD, 2 * P, (0, w_in[:, :, j * P:(j + 1) * P]),
                         (P, w_in[:, :, NC + j * P:NC + (j + 1) * P]))
                for j in range(3):
                    unit(KD, 256, (0, w_in[:, :, 2 * NC + j * 256:2 * NC + (j + 1) * 256]))
            else:
                for j in range(7):
                    unit(KD, 256, (0, w_in[:, :, j * 256:(j + 1) * 256]))
                unit(KD, 256, (0, w_in[:, :, 1696:1952]))
                qb, kvb = rows(A["l1_mla_w_qb"]), rows(A["l1_mla_w_kvb"])
                base["lat", l] = len(units)
                for j in range(2):
                    unit(2, 384, (0, qb[:, :, j * 384:(j + 1) * 384]))
                for j in range(2):
                    unit(1, 512, (0, kvb[:, :, j * 512:(j + 1) * 512]))
            base["out", l] = len(units)
            for j in range(YC):
                unit(KD, YN, (0, w_out[:, :, j * YN:(j + 1) * YN]))
            if l == 1:
                base["router"] = len(units)
                unit(KD, NE, (0, rows(A["l1_router_w"])))
            base["ffn", l] = len(units)
            for i in range(2 if l == 0 else 0):
                for j in range(3 * FC):
                    unit(KD if j < 2 * FC else FT, FN if j < 2 * FC else YN, (0, None))
        n_units = len(units)
        ffn_w = [
            (A["l0_ffn_w1"].rearrange("(k p) (e n) -> e p k n", p=P, e=2),
             A["l0_ffn_w3"].rearrange("(k p) (e n) -> e p k n", p=P, e=2),
             A["l0_ffn_w2"].rearrange("(e k p) n -> e p k n", p=P, e=2)),
            (A["l1_moe_w1"].rearrange("e (k p) n -> e p k n", p=P),
             A["l1_moe_w3"].rearrange("e (k p) n -> e p k n", p=P),
             A["l1_moe_w2"].rearrange("e (k p) n -> e p k n", p=P)),
        ]
        rings = []
        for u in range(n_units):
            if base["ffn", 0] <= u < base["ada", 1]:
                k = (u - base["ffn", 0]) % R
                rings.append((k, k * SLOT, R))
            else:
                k = (u - base["ffn", 0] if u < base["ffn", 0] else base["ada", 1] - u) % R_SMALL
                rings.append((k, k * (R * SLOT // R_SMALL), R_SMALL))
        landed, count = [], [0] * R_SMALL
        for u, (pieces, _, _) in enumerate(units):
            count[rings[u][0]] += 16 * len(pieces)
            landed.append(count[rings[u][0]])

        def raw_of(u):
            _, kt, n = units[u]
            at = rings[u][1]
            return raw[:, at:at + kt * n]

        def hi_of(u):
            _, kt, n = units[u]
            at = u % S * SLOT
            return Wh[:, at:at + kt * n]

        def lo_of(u):
            _, kt, n = units[u]
            at = u % S * SLOT
            return Wl[:, at:at + kt * n]

        def by_k(view, u):
            return view.rearrange("p (k n) -> p k n", k=units[u][1])

        first = {}
        groups = {"A": 0, "B": 0, "T": 0}

        def takes(name, a=0, b=0, t=0):
            first[name] = dict(groups)
            groups["A"] += a
            groups["B"] += b
            groups["T"] += t

        takes("setup", t=2)
        for l in range(2):
            takes(("ada", l), b=24)
            takes(("mods", l), b=8, t=1)
            takes(("norm", l, 0), t=KD)
            if l == 0:
                takes("in0", a=CT, b=CT + 9)
                takes("prep0", t=4)
                takes("attend0", a=24, b=3, t=24 + NT)
                takes("lnorm", b=2)
            else:
                takes("in1", b=24)
                takes("prep1", t=7)
                takes("attend1", a=24, b=6, t=24 + NT)
                takes("latT", t=3)
                takes("lat", b=14)
                takes("prep2", t=14)
                takes("attend2", a=24, b=3, t=24 + NT)
            takes(("out", l), b=NT * YC)
            takes(("norm", l, 1), t=KD)
            if l == 1:
                takes("router", b=NT)
            if l == 0:
                takes(("ffn", l), a=12 * 2, b=24 * 2, t=FT * 2)
            else:
                takes("tables", b=1)
                takes("tokens", a=2 * NT, b=2 * NT)
                takes("jobs")

        raw_landed = [sem(f"raw_landed{i}") for i in range(R_SMALL)]
        hi_ready = sem("hi_ready")
        lo_ready = sem("lo_ready")
        psA_full, psA_free = sem("psA_full"), sem("psA_free")
        psB_full, psB_free = sem("psB_full"), sem("psB_free")
        psT_full, psT_free = sem("psT_full"), sem("psT_free")
        const_in = sem("const_in")
        gains_in = sem("gains_in")
        cache_in = sem("cache_in")
        bias_in = sem("bias_in")
        x_in = sem("x_in")
        y_out = sem("y_out")
        state_out = sem("state_out")
        dve_chain = sem("dve_chain")
        act_chain = sem("act_chain")
        pool_chain = sem("pool_chain")
        c_silu = sem("c_silu")
        c_ready = sem("c_ready")
        sumsq = sem("sumsq")
        root = sem("root")
        ms_ready = sem("ms_ready")
        xn_ready = sem("xn_ready")
        hT_hi = sem("hT_hi")
        hT_lo = sem("hT_lo")
        mod_part = sem("mod_part")
        z_ready = sem("z_ready")
        sig_ready = sem("sig_ready")
        bias_ready = sem("bias_ready")
        pv_done = sem("pv_done")
        o_ready = sem("o_ready")
        x_added = sem("x_added")
        ln_in = sem("ln_in")
        ln_out = sem("ln_out")
        ys_ready = sem("ys_ready")
        comb_ready = sem("comb_ready")
        back_free = sem("back_free")
        gather_full = sem("gather_full")
        gather_free = sem("gather_free")
        y_added = sem("y_added")
        x_done_p = sem("x_done_p")
        x_done_q = sem("x_done_q")
        logit_e = sem("logit_e")
        router_in = sem("router_in")
        lam_in = sem("lam_in")
        lam_e = sem("lam_e")
        gT_hi = sem("gT_hi")
        conv_chain = sem("conv_chain")
        tap_made = sem("tap_made")
        conv_chain_p = sem("conv_chain_p")

        half_landed = [sem(f"half_landed{i}") for i in range(HSLOTS)]
        half_hi = sem("half_hi")
        half_lo = sem("half_lo")
        half_used = sem("half_used")
        mask_ready = sem("mask_ready")
        table_ready = sem("table_ready")
        jcst_in = sem("jcst_in")
        place_ready = sem("place_ready")
        pick_ready = sem("pick_ready")
        pick_part = sem("pick_part")
        y_hi = sem("y_hi")

        def wait(eng, s, v):
            if not isinstance(v, int) or v > 0:
                eng.wait_ge(s, v)

        H, at = {}, 0
        for name, n in (("norm0", KD), ("att0", NT), ("conv", CT), ("norm1", KD), ("norm2", KD),
                        ("att1", NT), ("latT", 3), ("att2", NT), ("norm3", KD)):
            H[name] = at
            at += n

        last_group = {}
        for l in range(2):
            for u in range(24):
                last_group[base["ada", l] + u] = ("B", first["ada", l]["B"] + u)
            for j in range(YC):
                last_group[base["out", l] + j] = ("B", first["out", l]["B"] + NT * j + NT - 1)
            for i in range(2 if l == 0 else 0):
                f = first["ffn", l]
                for j in range(3 * FC):
                    if j < 2 * FC and j % 2 == 0:
                        g = ("A", f["A"] + 12 * i + NT * (j // 2) + NT - 1)
                    elif j < 2 * FC:
                        g = ("B", f["B"] + 24 * i + NT * (j // 2) + NT - 1)
                    else:
                        g = ("B", f["B"] + 24 * i + 12 + NT * (j - 2 * FC) + NT - 1)
                    last_group[base["ffn", l] + 12 * i + j] = g
        for j in range(CT):
            last_group[base["in", 0] + j] = ("B", first["in0"]["B"] + j)
        for j in range(3):
            last_group[base["in", 0] + CT + j] = ("B", first["in0"]["B"] + CT + NT * j + NT - 1)
        for j in range(8):
            last_group[base["in", 1] + j] = ("B", first["in1"]["B"] + NT * j + NT - 1)
        for j in range(2):
            last_group[base["lat", 1] + j] = ("B", first["lat"]["B"] + NT * j + NT - 1)
            last_group[base["lat", 1] + 2 + j] = ("B", first["lat"]["B"] + 2 * NT + 4 * j + 3)
        last_group[base["router"]] = ("B", first["router"]["B"] + NT - 1)
        full = {"A": psA_full, "B": psB_full}

        TGROUPS = {2: (0, 1), 4: (2, 3, 4), 6: (5, 6, 7), 8: (8, 9, 10)}

        def otile_at(t):
            return 8 * t + 12

        def tgroup(a, s):
            return first[f"attend{a}"]["T"] + s + sum(otile_at(t) <= s for t in range(NT - 1))

        def otgroup(a, t):
            f = first[f"attend{a}"]["T"]
            return f + otile_at(t) + t if t < NT - 1 else f + 8 * NT + NT - 1

        def ckvT(h):
            return h[:, 6:8, :].rearrange("p a b -> p (a b)")[:, 0:4 * P]

        def yv(c):
            return cpad[:, c, 0:TOK]

        def half_shape(h):
            (k0, k1), n = HALF_K[h >= 4 * FC][h % 2], (FN if h < 4 * FC else YN)
            return k0, k1, n

        def half_of(t, h):
            k0, k1, n = half_shape(h)
            at = h % HSLOTS * HSLOT
            return t[:, at:at + (k1 - k0) * n]

        def used_signal(h, n):
            j = h // 2
            if h % 2 == 0:
                return half_used, 3 * FC * n + j + 1
            if j >= 2 * FC:
                return psB_full, first["jobs"]["B"] + W2_AT[j - 2 * FC] + 1 + JOB_B * n
            if j % 2:
                return psB_full, first["jobs"]["B"] + j // 2 + 1 + JOB_B * n
            return psA_full, first["jobs"]["A"] + j // 2 + 1 + JOB_A * n

        JT = {2: ((1, (0,)), (2, (1,))), 4: ((3, (2, 3, 4)),), 6: ((4, (5, 6, 7)),), 8: ((5, (8, 9, 10)),)}
        psAj, psBj = psA[0:2], psB + psA[2:3]

        def job_bank(b):
            return psBj[JOB_BANK[b]]

        def returned(t):
            return slice((t == 2) * YN, (t == 2) * YN + YN)

        yp = scr[:, 0:D]
        yq = work[:, FE:FE + 2 * D].rearrange("p (t n) -> p t n", t=2)
        ytj = work[:, FE + 2 * D:FE + 2 * D + NT * YN].rearrange("p (t n) -> p t n", t=NT)

        def y_rows(t, c):
            cols = slice(c * YN, (c + 1) * YN)
            return yp[:, cols] if t == 0 else yq[:, t - 1, cols]
        picked = [h[:, :, 0:2 * P] for h in (hTh, hTl)]
        gj = work[:, 0:FE]

        def job_number(i, p):
            return 2 * i + p if p is not None else i + NE

        def gather_number(i, p):
            return i if p is not None else i + NE // 2

        def of_pieces(pieces):
            return [2 * k + r for k in pieces for r in range(2)]

        def chosen(p):
            return slice((p or 0) * P, (p or 0) * P + P)

        def over_jobs(eng, body):
            with eng.Fori(0, NE // 2) as i:
                for p in range(2):
                    body(i, p)
            return further_jobs(eng, body)

        def further_jobs(eng, body):
            eng.wait_ge(table_ready, 1)
            more = eng.value_load(jobs_i[0:1, 0:1], min_val=0, max_val=EXTRA)
            with eng.Fori(0, EXTRA) as i:
                with eng.If(i < more):
                    body(i, None)
            return more

        qm = work[:, 1248:3552].rearrange("p (t n) -> p t n", t=NT)
        SS, RT, RC = 96, 112, 128

        def keys_of(t):
            return [0] if t == 0 else [1, 2, 3]

        def key_cols(t):
            return (0, P) if t == 0 else (P, 4 * P)

        def head0(s):
            t, h = divmod(s, 8)
            r = slice((h // 4) * HD, (h // 4 + 1) * HD)
            lo, hi = key_cols(t)
            return (qT0[r, h % 4, t * P:(t + 1) * P], kT0[r, lo:hi],
                    [(zq[:, k, 640:768] if k < 3 else cv0[:, :])[:, (h // 4) * HD:(h // 4 + 1) * HD]
                     for k in keys_of(t)])

        def head1(s):
            t, h = divmod(s, 8)
            r = slice((h % 2) * HD, (h % 2 + 1) * HD)
            lo, hi = key_cols(t)
            return (qT1[r, h // 2, t * P:(t + 1) * P], kT1[r, h // 2, lo:hi],
                    [(zd[:, k, 1024:1536] if k < 3 else cdv[:, :])[:, (h // 2) * P:(h // 2 + 1) * P]
                     for k in keys_of(t)])

        def head2(s):
            t, h = divmod(s, 8)
            lo, hi = key_cols(t)
            return (qT2[0:QK, h, t * P:(t + 1) * P], kT2[0:QK, h, lo:hi],
                    [kv[:, k, h * P + NOPE:(h + 1) * P] for k in keys_of(t)])

        ATT = [
            dict(per=8, n=HD, head=head0, PT=PT0, ft=4, no=0),
            dict(per=4, n=P, head=head1, PT=PT1, ft=0, no=1),
            dict(per=8, n=VD, head=head2, PT=PT2, ft=4, no=2),
        ]
        NS = 8 * NT

        def pv_signal(a, s):
            per = ATT[a]["per"]
            if s % per == per - 1:
                return psB_full, first[f"attend{a}"]["B"] + s // per + 1
            return pv_done, sum(NS - NS // ATT[b]["per"] for b in range(a)) + s - s // per + 1

        def tap_product(n):
            return work[:, n % 3 * COUT:n % 3 * COUT + COUT]

        block = ctx.enter_context(nc.Block())

        @block.sync
        def _(sp):
            def load(u, i=0, j=0, view=None):
                _, kt, n = units[u + j]
                slot, _, ring = rings[u + j]
                behind = u + j - base["ada", 1] in (0, 1, 2)
                wait(sp, lo_ready, u + j + 12 * i - (1 if behind else ring - 1))
                dst = by_k(raw_of(u + j), u + j)
                if view is not None:
                    sp.dma_start(dst, view).then_inc(raw_landed[slot], 16)
                    return
                pieces = units[u + j][0]
                for c, src in pieces:
                    sp.dma_start(dst[:, :, c:c + n // len(pieces)], src).then_inc(raw_landed[slot], 16)

            def load_ffn(l, i):
                w1, w3, w2 = ffn_w[l]
                for j in range(3 * FC):
                    if j < 2 * FC:
                        c = j // 2
                        view = (w1, w3)[j % 2][i, :, :, c * FN:(c + 1) * FN]
                    else:
                        c = j - 2 * FC
                        view = w2[i, :, :, c * YN:(c + 1) * YN]
                    load(base["ffn", l], i, j, view)

            sp.dma_start(stage[0:KD, :], A["c_ctx"].rearrange("(k p) -> k p", p=P)).then_inc(const_in, 16)
            sp.dma_start(stage[KD:2 * KD, :], A["c"].rearrange("b (k p) -> (b k) p", p=P)).then_inc(const_in, 16)
            sp.dma_start(cst[:, :], A["consts"]).then_inc(const_in, 16)
            for (l, w), r in V_N.items():
                sp.dma_start(stage[r:r + KD, :],
                             A[f"l{l}_norm{w + 1}_g"].rearrange("(k p) -> k p", p=P)).then_inc(const_in, 16)
            for name, r in (("l0_conv_dw_b", V_DWB), ("l0_conv_ln_g", V_LNG), ("l0_conv_ln_b", V_LNB)):
                sp.dma_start(stage[r:r + CT, :], A[name].rearrange("(k p) -> k p", p=P)).then_inc(const_in, 16)
            sp.dma_start(stage_w[0:CW * CT, :],
                         A["l0_conv_dw_w"].rearrange("w (k p) -> (w k) p", p=P)).then_inc(const_in, 16)
            def load_half(e, h, n, wait_for=None):
                k0, k1, cols = half_shape(h)
                j = h // 2
                w1, w3, w2 = ffn_w[1]
                c = (j // 2 if j < 2 * FC else j - 2 * FC) * cols
                view = (w2 if j >= 2 * FC else (w1, w3)[j % 2])[e, :, k0:k1, c:c + cols]
                if wait_for is None and h != 4 * FC:
                    sp.wait_ge(half_lo, h + (2 if h == 4 * FC - 1 else 1) - HSLOTS + HALVES * n)
                sp.dma_start(half_of(raw, h).rearrange("p (k n) -> p k n", k=k1 - k0),
                             view).then_inc(half_landed[h % HSLOTS], 16)

            for u in range(base["ada", 0], base["ffn", 0]):
                load(u)
            with sp.Fori(0, 2) as i:
                load_ffn(0, i)
            for u in range(base["ada", 1], n_units):
                load(u)
            sp.wait_ge(lo_ready, n_units)
            for h in range(HSLOTS):
                load_half(0, h, 0, "split")

            def job(i, one_each):
                if one_each:
                    for h in range(HSLOTS, HALVES):
                        load_half(i, h, i)
                    for h in range(HSLOTS):
                        load_half(i + 1, h, i + 1)
                else:
                    e = sp.value_load(jobs_i[0:1, bass.ds(i + 1, 1)], min_val=0, max_val=NE - 1)
                    for h in range(HALVES):
                        load_half(e, h, i + NE)

            with sp.Fori(0, NE - 1) as i:
                job(i, True)
            for h in range(HSLOTS, HALVES):
                load_half(NE - 1, h, NE - 1)
            further_jobs(sp, job)
            sp.wait_ge(x_done_p, YC)
            sp.dma_start(out[0][0], x[:, 0, :]).then_inc(y_out, 16)
            sp.wait_ge(x_done_q, YC)
            sp.dma_start(out[1][0].rearrange("(t p) n -> p t n", p=P), x[:, 1:NT, :]).then_inc(y_out, 16)
            sp.wait_ge(y_out, 32)
            sp.wait_ge(state_out, 16 * 6)

        @block.gpsimd
        def _(pool):
            pool.dma_start(x[:, 0, :], A["x_prompt"][0]).then_inc(x_in, 16)
            pool.dma_start(x[:, 1:NT, :], A["x_sample"][0].rearrange("(t p) n -> p t n", p=P)).then_inc(x_in, 16)
            for name, view in G.items():
                pool.dma_start(view, A[name].partition_broadcast(P)).then_inc(gains_in, 16)
            pool.dma_start(cckv[:, :], A["cache_l1_mla_ckv"][0]).then_inc(cache_in, 16)
            pool.dma_start(ckr[:, :], A["cache_l1_mla_krope"][0]).then_inc(cache_in, 16)

            def bias_row(l):
                wait(pool, psB_free, first["ada", l]["B"])
                pool.wait_ge(psT_full, first["ada", l]["T"])
                pool.dma_start(mrow[4:5, :], A[f"l{l}_ada_b"].rearrange("(a n) -> a n", a=1)).then_inc(bias_in, 16)

            def mods_done(l):
                pool.wait_ge(psB_free, first["mods", l]["B"] + 8)
                pool.wait_ge(psT_free, first["mods", l]["T"] + 1)

            def add(b, i=0):
                for j in range(YC):
                    for t in range(NT):
                        pool.wait_ge(psB_free, b + j * NT + t + 1 + 24 * i)
                        dst = x[:, t, j * YN:(j + 1) * YN]
                        pool.tensor_tensor(dst, dst, ytmp[:, t, :], ALU.add).then_inc(x_added, 1)

            bias_row(0)
            mods_done(0)
            pool.dma_start(ck0[:, :], A["cache_l0_gqa_k"].rearrange("b s h d -> (b s) (h d)")).then_inc(cache_in, 16)
            pool.dma_start(cv0[:, :], A["cache_l0_gqa_v"].rearrange("b s h d -> (b s) (h d)")).then_inc(cache_in, 16)
            pool.memset(cpad[:, :, :], 0.0).then_inc(pool_chain, 1)
            pool.wait_ge(z_ready, 1)
            pool.dma_start(out[2].rearrange("b s h d -> (b s) (h d)"), zq[:, 0, 512:640]).then_inc(state_out, 16)
            pool.dma_start(out[3].rearrange("b s h d -> (b s) (h d)"), zq[:, 0, 640:768]).then_inc(state_out, 16)
            for n in range(CT - CT_V, CW * (CT - CT_V)):
                w, c = divmod(n, CT - CT_V)
                k = n - (CT - CT_V)
                dst = yc[:, CT_V + c, :]
                pool.wait_ge(tap_made, n + 1)
                wait(pool, conv_chain_p, k - (CT - CT_V) + 1)
                pool.tensor_tensor(dst, dst, tap_product(n), ALU.add).then_inc(conv_chain_p, 1)
            add(first["out", 0]["B"])
            with pool.Fori(0, 2) as i:
                add(first["ffn", 0]["B"] + 12, i)
            bias_row(1)
            mods_done(1)
            pool.dma_start(cdk[:, :], A["cache_l1_diff_k"].rearrange("b s h j d -> (b s) (h j d)")).then_inc(cache_in, 16)
            pool.dma_start(cdv[:, :], A["cache_l1_diff_v"].rearrange("b s h d -> (b s) (h d)")).then_inc(cache_in, 16)
            pool.wait_ge(state_out, 32)
            pool.wait_ge(z_ready, 4)
            pool.dma_start(out[4].rearrange("b s h j d -> (b s) (h j d)"), zd[:, 0, 512:1024]).then_inc(state_out, 16)
            pool.dma_start(out[5].rearrange("b s h d -> (b s) (h d)"), zd[:, 0, 1024:1536]).then_inc(state_out, 16)
            pool.wait_ge(state_out, 64)
            pool.wait_ge(z_ready, 7)
            pool.dma_start(out[6][0], zm[:, 0, QR:QR + KVR]).then_inc(state_out, 16)
            pool.dma_start(out[7][0], zm[:, 0, QR + KVR:416]).then_inc(state_out, 16)
            add(first["out", 1]["B"])
            pool.wait_ge(hT_lo, H["norm3"] + KD)
            pool.dma_start(jcst[:, :], A["job_consts"]).then_inc(jcst_in, 16)

            def job(i, p):
                n = job_number(i, p)
                for c in range(YC):
                    for t in range(NT):
                        pool.wait_ge(back_free, BACKS * n + BACKS + NT * c + t + 1)
                        pool.tensor_tensor(y_rows(t, c), y_rows(t, c), ytj[:, t, :], ALU.add).then_inc(y_added, 1)

            pool.memset(yp, 0.0).then_inc(y_added, 1)
            pool.memset(yq[:, 0, :], 0.0).then_inc(y_added, 1)
            pool.memset(yq[:, 1, :], 0.0).then_inc(y_added, 1)
            more = over_jobs(pool, job)
            for c in range(YC):
                pool.wait_ge(y_added, BACKS * (NE - 1) + 6 + NT * c + BACKS * more)
                pool.tensor_tensor(y_rows(0, c), y_rows(0, c), gate_b[:, 1, 0, c * YN:(c + 1) * YN],
                                   ALU.mult).then_inc(pool_chain, 1)
                pool.wait_ge(pool_chain, 2 + c)
                dst = x[:, 0, c * YN:(c + 1) * YN]
                pool.tensor_tensor(dst, dst, y_rows(0, c), ALU.add).then_inc(x_done_p, 1)

        @block.scalar
        def _(act):
            chain = [0]

            def link(ins):
                chain[0] += 1
                ins.then_inc(act_chain, 1)
                act.wait_ge(act_chain, chain[0])

            def split_hi(u, i=0, per=12):
                act.wait_ge(raw_landed[rings[u][0]], landed[u] + 16 * (per // rings[u][2]) * i)
                if u >= S:
                    group, g = last_group[u - S]
                    grows = 6 if per == 6 else 12 if group == "A" else 24
                    act.wait_ge(full[group], g + 1 + grows * i)
                elif not isinstance(i, int):
                    act.wait_ge(psB_full, last_group[u - S + per][1] + 1 + per * (i - 1))
                act.copy(hi_of(u), raw_of(u)).then_inc(hi_ready, 1)

            def step(u):
                if u + AHEAD < n_units:
                    split_hi(u + AHEAD)

            roots = [0]

            def square_root(o, i, scale, eps):
                roots[0] += 1
                act.wait_ge(ms_ready, roots[0])
                act.activation(o, i, ACT.Sqrt, scale=scale, bias=eps).then_inc(root, 1)

            def ada(l):
                u0 = base["ada", l] + AHEAD
                for j in range(6):
                    split_hi(u0 + j)
                with act.Fori(1, 3) as i:
                    for j in range(6):
                        split_hi(u0 + j, i, 6)
                for j in range(6):
                    split_hi(u0 + 18 + j)

            norms = [0]

            def norm():
                n = norms[0]
                act.wait_ge(x_in, 32)
                wait(act, x_added, [0, 12, 36, 48][n])
                for t in range(NT):
                    link(act.activation(scr[:, 0:D], x[:, t, :], ACT.Square, accum_out=stats[:, t:t + 1]))
                act.activation(stats[:, 4:7], stats[:, 0:3], ACT.Sqrt, scale=1.0 / D,
                               bias=eps_rms).then_inc(sumsq, 1)
                l, w = divmod(n, 2)
                for f in range(KD):
                    g = first["norm", l, w]["T"] + f
                    act.wait_ge(psT_full, g + 1)
                    if f >= 2:
                        act.wait_ge(hT_lo, H[f"norm{n}"] + f - 1)
                    for c, (a, b) in enumerate(((0, P), (P, TOK))):
                        act.activation(hf[:, f % 2, a:b], psT[g % 2][:, a:b], ACT.Identity,
                                       scale=mod[:, 2 * w + 1, f, c:c + 1], bias=mod[:, 2 * w, f, c:c + 1]
                                       ).then_inc(psT_free if c else mod_part, 1)
                norms[0] += 1

            def o_split(a, t):
                k = otgroup(a, t)
                act.wait_ge(psT_full, k + 1)
                act.copy(hTh[:, ATT[a]["ft"]:ATT[a]["ft"] + 4, t * P:(t + 1) * P],
                         psT[k % 2][:, :].rearrange("p (f n) -> p f n", f=4)).then_inc(hT_hi, 1)

            taps = [0]

            def tap():
                n = taps[0]
                if n >= CW * (CT - CT_V):
                    return
                taps[0] += 1
                w, c = divmod(n, CT - CT_V)
                src, k = cpad[:, CT_V + c, w:w + COUT], dww[:, w * CT + CT_V + c:w * CT + CT_V + c + 1]
                if w == 0:
                    act.activation(yc[:, CT_V + c, :], src, ACT.Identity, scale=k,
                                   bias=vecs[:, V_DWB + CT_V + c:V_DWB + CT_V + c + 1]).then_inc(tap_made, 1)
                    return
                wait(act, conv_chain_p, n - 3 - (CT - CT_V) + 1)
                act.mul(tap_product(n), src, k).then_inc(tap_made, 1)

            def attend(a):
                f = first[f"attend{a}"]
                for s in range(NS):
                    n = P * len(keys_of(s // 8))
                    g = f["A"] + s
                    act.wait_ge(bias_ready, NS * a + s + 1)
                    if s >= 2:
                        act.wait_ge(psT_full, tgroup(a, s - 2) + 1)
                    act.activation(Pb[:, s % 2, 0:n], psA[g % 3][:, 0:n], ACT.Exp, scale=-1.0,
                                   bias=stats[:, 32 + s:33 + s],
                                   accum_out=stats[:, 64 + s:65 + s]).then_inc(psA_free, 1)
                    if a == 0:
                        for _ in range(3):
                            tap()
                    if a == 1 and s % 4 == 1 and s > 4:
                        square_root(stats[:, 12:14], stats[:, 10:12], 1.0 / P, eps_rms)
                    if s in (otile_at(0), otile_at(1)):
                        o_split(a, s // 8 - 1)
                if a == 1:
                    square_root(stats[:, 12:14], stats[:, 10:12], 1.0 / P, eps_rms)
                o_split(a, NT - 1)

            def ffn(l):
                u0, f, k = base["ffn", l], first["ffn", l], (2 if l == 0 else NE)
                act.wait_ge(state_out, 32)
                with act.Fori(0, k) as i:
                    for j in range(3 * FC):
                        if j + AHEAD < 3 * FC:
                            split_hi(u0 + j + AHEAD, i)
                        elif l == 0:
                            split_hi(u0 + j + AHEAD, i)
                        else:
                            with act.If(i < k - 1):
                                split_hi(u0 + j + AHEAD, i)
                        if j < 2 * FC and j % 2 == 0:
                            for t in range(NT):
                                g = f["A"] + NT * (j // 2) + t
                                act.wait_ge(psA_full, g + 1 + 12 * i)
                                act.activation(gt[:, t, j // 2 * FN:(j // 2 + 1) * FN], psA[g % 3][:, 0:FN],
                                               ACT.Silu).then_inc(psA_free, 1)
                        for q in TGROUPS.get(j, ()):
                            act.wait_ge(psT_full, f["T"] + q + 1 + FT * i)
                            act.copy(gTh[:, q, :], psT[q % 2][:, 0:TOK]).then_inc(gT_hi, 1)

            def qk_root(hd, heads):
                square_root(stats[:, RT:RT + heads], stats[:, SS:SS + heads], 1.0 / hd, eps_rms)

            act.wait_ge(const_in, 16 * 11)
            act.wait_ge(psT_free, 1)
            act.activation(csil[:, :], vecs[:, 0:2 * KD], ACT.Silu).then_inc(c_silu, 1)
            for u in range(AHEAD):
                split_hi(u)

            ada(0)
            norm()
            for j in range(CT):
                step(base["in", 0] + j)
                g = first["in0"]["A"] + j
                act.wait_ge(psA_full, g + 1)
                if j == 0:
                    act.wait_ge(hT_lo, H["norm0"] + KD)
                if j >= 2:
                    act.wait_ge(psB_free, first["in0"]["B"] + j - 1)
                act.activation(hf[:, j % 2, :], psA[g % 3][:, 0:TOK], ACT.Sigmoid).then_inc(psA_free, 1)
            for j in range(3):
                step(base["in", 0] + CT + j)
            def transposed_in(g, dst):
                act.wait_ge(psT_full, g + 1)
                act.copy(dst, psT[g % 2][0:dst.shape[0], :].rearrange("p (f n) -> p f n", f=4)).then_inc(psT_free, 1)

            g0 = first["prep0"]["T"]
            for t in range(NT):
                qk_root(HD, 10)
                transposed_in(g0 + t, qT0[:, :, t * P:(t + 1) * P])
            transposed_in(g0 + NT, kT0[:, :].rearrange("p (f n) -> p f n", f=4))
            attend(0)
            square_root(hf[:, 1, :], hf[:, 0, :], 1.0, eps_ln)
            for c in range(CT):
                act.wait_ge(ln_out, c + 1)
                link(act.activation(ysil[:, c, :], yv(c), ACT.Silu, scale=vecs[:, V_LNG + c:V_LNG + c + 1],
                                    bias=vecs[:, V_LNB + c:V_LNB + c + 1]))
                act.copy(hTh[:, c, :], ysil[:, c, :]).then_inc(hT_hi, 1)
            for j in range(YC):
                step(base["out", 0] + j)
            norm()
            ffn(0)

            ada(1)
            norm()
            act.wait_ge(lam_in, 1)
            act.activation(stats[:, 90:92], stats[:, 88:90], ACT.Exp).then_inc(lam_e, 1)
            for j in range(8):
                step(base["in", 1] + j)
            g0 = first["prep1"]["T"]
            for n in range(7):
                t = n // 2
                if n % 2 == 0 and t < NT:
                    qk_root(HD, 16)
                transposed_in(g0 + n, (qT1 if n % 2 == 0 and t < NT else kT1)[:, :, t * P:(t + 1) * P])
            attend(1)
            qk_root(QR, NT)
            qk_root(KVR, NT)
            for q in range(3):
                k = first["latT"]["T"] + q
                act.wait_ge(psT_full, k + 1)
                dst = hTh[:, 4 + q, :] if q < 2 else ckvT(hTh)
                act.copy(dst, psT[k % 2][:, 0:TOK if q < 2 else 4 * P]).then_inc(hT_hi, 1)
            for j in range(4):
                step(base["lat", 1] + j)
            g0 = first["prep2"]["T"]
            for m in range(NT + 4):
                qk_root(QK, MLA_H)
                t = m if m < NT else m - NT
                for half in range(2):
                    transposed_in(g0 + 2 * m + half,
                                  (qT2 if m < NT else kT2)[0:QK, 4 * half:4 * half + 4, t * P:(t + 1) * P])
            attend(2)
            for j in range(YC):
                step(base["out", 1] + j)
            norm()
            step(base["router"])
            act.wait_ge(router_in, 1)
            act.activation(rt[:, 4:7], rt[:, 0:3], ACT.Exp).then_inc(logit_e, 1)
            for q in range(2 * NT):
                g = first["tokens"]["A"] + q
                act.wait_ge(psA_full, g + 1)
                act.copy(toks_h[:, q // 2, q % 2 * 512:(q % 2 + 1) * 512], psA[g % 3][:, :]).then_inc(psA_free, 1)

            def split_half(h, n):
                k0, k1, cols = half_shape(h)
                act.wait_ge(half_landed[h % HSLOTS], 16 * (h // HSLOTS + 1) + 16 * (HALVES // HSLOTS) * n)
                act.copy(half_of(Wh, h), half_of(raw, h)).then_inc(half_hi, 1)

            def gathered(m, pieces=range(4)):
                for q in of_pieces(pieces):
                    act.wait_ge(gather_full, q + 1 + KD * m)
                    act.copy(picked[q // 4][:, q % 4 * 2:q % 4 * 2 + 2, :],
                             psAj[q % 2][:, :].rearrange("p (f n) -> p f n", f=2)).then_inc(gather_free, 1)

            def job(i, p):
                n = job_number(i, p)
                f = first["jobs"]
                if p is None:
                    act.wait_ge(psB_full, f["B"] + JOB_B * n)
                    for h in range(HSLOTS - 1):
                        split_half(h, n)
                    gathered(gather_number(i, p))
                for h in range(HALVES):
                    j = h // 2
                    ahead = h + HSLOTS - 1
                    if ahead < HALVES:
                        act.wait_ge(*used_signal(h - 1, n) if h else used_signal(HALVES - 1, n - 1))
                        split_half(ahead, n)
                    elif p == 0:
                        act.wait_ge(*used_signal(h - 1, n))
                        split_half(ahead - HALVES, n + 1)
                    elif p == 1:
                        with act.If(i < NE // 2 - 1):
                            act.wait_ge(*used_signal(h - 1, n))
                            split_half(ahead - HALVES, n + 1)
                    if h == 4 * FC:
                        transposed(j, n)
                    if h in GATHER_AT and p == 1:
                        with act.If(i < NE // 2 - 1):
                            gathered(i + 1, [GATHER_AT.index(h)])
                    if h % 2 == 0:
                        continue
                    if j < 2 * FC and j % 2 == 0:
                        g = j // 2
                        act.wait_ge(psA_full, f["A"] + g + 1 + JOB_A * n)
                        act.activation(gj[:, j // 2 * FN:(j // 2 + 1) * FN], psAj[g % 2][:, 0:FN],
                                       ACT.Silu).then_inc(psA_free, 1)
                        transposed(j, n)
                    elif j >= 2 * FC:
                        c = j - 2 * FC
                        act.wait_ge(psB_full, f["B"] + W2_AT[c] + 1 + JOB_B * n)
                        act.copy(yh[:, c % 2, :], job_bank(W2_AT[c])[:, 0:YN]).then_inc(y_hi, 1)
                        if c == 0:
                            act.wait_ge(comb_ready, n + 1)
                        else:
                            given_back(c - 1, n)
                given_back(YC - 1, n)

            def given_back(c, n):
                for t in range(NT):
                    b = ADD_AT[c] + (t > 0)
                    act.wait_ge(y_added, BACKS * n + NT * c + t + 1)
                    act.wait_ge(psB_full, first["jobs"]["B"] + b + 1 + JOB_B * n)
                    act.activation(ytj[:, t, :], job_bank(b)[:, returned(t)], ACT.Identity,
                                   scale=comb_e[:, t:t + 1]).then_inc(back_free, 1)

            def transposed(j, n):
                for g, tiles in JT.get(j, ()):
                    act.wait_ge(psT_full, first["jobs"]["T"] + g + 1 + JOB_T * n)
                    act.copy(mTh[:, tiles[0]:tiles[-1] + 1, :],
                             psT[g % 2][:, 0:P * len(tiles)].rearrange("p (f n) -> p f n", f=len(tiles))
                             ).then_inc(gT_hi, 1)

            for h in range(HSLOTS - 1):
                split_half(h, 0)
            act.copy(marks[0:1, 63:64], cst[0:1, 0:1]).then_inc(back_free, BACKS)
            gathered(0)
            over_jobs(act, job)

        @block.tensor
        def _(pe):
            def free_a(g, i=0, per=12):
                if g >= 3:
                    pe.wait_ge(psA_free, g - 2 + per * i)

            def free_b(g, i=0, per=24):
                if g >= 3:
                    pe.wait_ge(psB_free, g - 2 + per * i)

            def free_t(g):
                if g >= 2:
                    pe.wait_ge(psT_free, g - 1)

            def split_products(o, pairs):
                n = len(pairs)
                for k, (sh, sl, mh, ml) in enumerate(pairs):
                    pe.matmul(o, sh, mh, start=(k == 0), stop=False)
                    pe.matmul(o, sh, ml, start=False, stop=False)
                    last = pe.matmul(o, sl, mh, start=False, stop=(k == n - 1))
                return last

            def rows_times(o, u, stat, t, cols=None):
                _, kt, n = units[u]
                wh, wl = by_k(hi_of(u), u), by_k(lo_of(u), u)
                return split_products(o[:, 0:n], [
                    (stat[0][:, k, t * P:(t + 1) * P], stat[1][:, k, t * P:(t + 1) * P], wh[:, k, :], wl[:, k, :])
                    for k in range(kt)])

            def unit_b(u, b0, stat, tiles=NT):
                pe.wait_ge(lo_ready, u + 1)
                for t in range(tiles):
                    g = b0 + t
                    free_b(g)
                    rows_times(psB[g % 3], u, stat, t).then_inc(psB_full, 1)

            def ada(l):
                u0, b0 = base["ada", l], first["ada", l]["B"]

                def one(j, i=0):
                    u, g = u0 + j, b0 + j
                    pe.wait_ge(lo_ready, u + 1 + 6 * i)
                    free_b(g, i, 6)
                    wh, wl = by_k(hi_of(u), u), by_k(lo_of(u), u)
                    for k in range(KD):
                        pe.matmul(psB[g % 3][:, 0:YN], chl[:, k, :], wh[:, k, :], start=(k == 0), stop=False)
                        last = pe.matmul(psB[g % 3][:, 0:YN], chl[:, k, :], wl[:, k, :], start=False,
                                         stop=(k == KD - 1))
                    last.then_inc(psB_full, 1)

                for j in range(6):
                    one(j)
                with pe.Fori(1, 4) as i:
                    for j in range(6):
                        one(j, i)

            def mods(l):
                f = first["mods", l]
                pe.wait_ge(psB_free, f["B"])
                pe.wait_ge(bias_in, 16 * (l + 1))
                g = f["T"]
                free_t(g)
                chunks = [*range(0, 2 * KD), *range(3 * KD, 5 * KD)]
                for n, c in enumerate(chunks):
                    last = pe.matmul(psT[g % 2][:, 2 * n:2 * n + 2], mrow[0:5, c * P:(c + 1) * P],
                                     cst[0:5, C_SEL:C_SEL + 2], start=True, stop=True)
                last.then_inc(psT_full, 1)
                for n in range(8):
                    gate, cond, half = n // 4, n // 2 % 2, n % 2
                    g = f["B"] + n
                    free_b(g)
                    c0 = (3 * gate + 2) * D + half * 512
                    pe.matmul(psB[g % 3][:, :], cst[0:5, C_SELB + cond * P:C_SELB + (cond + 1) * P],
                              mrow[0:5, c0:c0 + 512], start=True, stop=True).then_inc(psB_full, 1)

            norms = [0]

            def norm(l, w, u=None, b0=None):
                g0 = first["norm", l, w]["T"]
                pe.wait_ge(xn_ready, norms[0] + 1)

                def products(k):
                    if k == 0:
                        pe.wait_ge(lo_ready, u + 1)
                        for t in range(NT):
                            free_b(b0 + t)
                    pe.wait_ge(hT_lo, H[f"norm{norms[0]}"] + k + 1)
                    wh, wl, n = by_k(hi_of(u), u)[:, k, :], by_k(lo_of(u), u)[:, k, :], units[u][2]
                    for t in range(NT):
                        o = psB[(b0 + t) % 3][:, 0:n]
                        sh, sl = (h[:, k, t * P:(t + 1) * P] for h in (hTh, hTl))
                        pe.matmul(o, sh, wh, start=(k == 0), stop=False)
                        pe.matmul(o, sh, wl, start=False, stop=False)
                        last = pe.matmul(o, sl, wh, start=False, stop=(k == KD - 1))
                        if k == KD - 1:
                            last.then_inc(psB_full, 1)

                for f in range(KD):
                    free_t(g0 + f)
                    for t in range(NT):
                        last = pe.transpose(psT[(g0 + f) % 2][:, t * P:(t + 1) * P], xn[:, t, f * P:(f + 1) * P],
                                            ident)
                    last.then_inc(psT_full, 1)
                    if u is not None and f >= 2:
                        products(f - 2)
                if u is not None:
                    products(KD - 2)
                    products(KD - 1)
                norms[0] += 1

            def attend(a):
                cfg, f = ATT[a], first[f"attend{a}"]
                for i in range(NS + 2):
                    if i < NS:
                        g = f["A"] + i
                        free_a(g)
                        q, k, _ = cfg["head"](i)
                        pe.matmul(psA[g % 3][:, 0:P * len(keys_of(i // 8))], q, k,
                                  start=True, stop=True).then_inc(psA_full, 1)
                    if 1 <= i <= NS:
                        s = i - 1
                        g = tgroup(a, s)
                        pe.wait_ge(psA_free, f["A"] + s + 1)
                        free_t(g)
                        for k in range(len(keys_of(s // 8))):
                            last = pe.transpose(psT[g % 2][:, k * P:(k + 1) * P],
                                                Pb[:, s % 2, k * P:(k + 1) * P], ident)
                        last.then_inc(psT_full, 1)
                    if i >= 2:
                        s = i - 2
                        g = f["B"] + s // cfg["per"]
                        if s % cfg["per"] == 0:
                            free_b(g)
                        pe.wait_ge(psT_free, tgroup(a, s) + 1)
                        c = s % cfg["per"] * cfg["n"]
                        vs = cfg["head"](s)[2]
                        for k, v in enumerate(vs):
                            last = pe.matmul(psB[g % 3][:, c:c + cfg["n"]], cfg["PT"][:, s % 2, k * P:(k + 1) * P],
                                             v, start=(k == 0), stop=(k == len(vs) - 1))
                        last.then_inc(pv_signal(a, s)[0], 1)
                    if i in (otile_at(0), otile_at(1)):
                        o_transpose(a, i // 8 - 1)
                o_transpose(a, NT - 1)

            def o_transpose(a, t):
                g = otgroup(a, t)
                pe.wait_ge(o_ready, NT * a + t + 1)
                free_t(g)
                for k in range(4):
                    last = pe.transpose(psT[g % 2][:, k * P:(k + 1) * P], otok[:, k * P:(k + 1) * P], ident)
                last.then_inc(psT_full, 1)

            def out_projection(l):
                pe.wait_ge(hT_lo, H["att0" if l == 0 else "att2"] + (NT + CT if l == 0 else NT))
                for j in range(YC):
                    unit_b(base["out", l] + j, first["out", l]["B"] + NT * j, (hTh, hTl))

            def ffn(l):
                u0, f, k = base["ffn", l], first["ffn", l], (2 if l == 0 else NE)

                def transposes(j, i):
                    pe.wait_ge(psB_free, f["B"] + NT * (j // 2) + 24 * i)
                    for q in TGROUPS[j]:
                        pe.wait_ge(psT_free, f["T"] + (q if q < 2 else q - 1) + FT * i)
                        for t in range(NT):
                            last = pe.transpose(psT[q % 2][:, t * P:(t + 1) * P],
                                                gt[:, t, q * P:(q + 1) * P], ident)
                        last.then_inc(psT_full, 1)

                with pe.Fori(0, k) as i:
                    for j in range(3 * FC):
                        u = u0 + j
                        if j == 2 * FC:
                            transposes(j, i)
                            pe.wait_ge(psT_free, f["T"] + FT + FT * i)
                        pe.wait_ge(lo_ready, u + 1 + 12 * i)
                        for t in range(NT):
                            if j < 2 * FC and j % 2 == 0:
                                g = f["A"] + NT * (j // 2) + t
                                free_a(g, i)
                                rows_times(psA[g % 3], u, (hTh, hTl), t).then_inc(psA_full, 1)
                            else:
                                g = f["B"] + NT * (j // 2 if j < 2 * FC else j - FC) + t
                                free_b(g, i)
                                rows_times(psB[g % 3], u, (hTh, hTl) if j < 2 * FC else (gTh, gTl),
                                           t).then_inc(psB_full, 1)
                        if j in TGROUPS and j < 2 * FC:
                            transposes(j, i)

            pe.wait_ge(const_in, 16 * 11)
            pe.transpose(psT[0][:, 0:60], stage[0:60, :], ident[0:60, 0:60]).then_inc(psT_full, 1)
            pe.transpose(psT[1][:, 0:CW * CT], stage_w[0:CW * CT, :],
                         ident[0:CW * CT, 0:CW * CT]).then_inc(psT_full, 1)
            pe.wait_ge(c_ready, 1)
            ada(0)
            mods(0)
            norm(0, 0)
            pe.wait_ge(hT_lo, H["norm0"] + KD)
            for j in range(CT):
                u = base["in", 0] + j
                pe.wait_ge(lo_ready, u + 1)
                wh, wl = by_k(hi_of(u), u), by_k(lo_of(u), u)
                ga, gb = first["in0"]["A"] + j, first["in0"]["B"] + j
                free_a(ga)
                c = slice(P, 2 * P)
                split_products(psA[ga % 3][:, 0:TOK], [
                    (wh[:, k, c], wl[:, k, c], hTh[:, k, :], hTl[:, k, :]) for k in range(KD)
                ]).then_inc(psA_full, 1)
                free_b(gb)
                c = slice(0, P)
                split_products(psB[gb % 3][:, 0:TOK], [
                    (wh[:, k, c], wl[:, k, c], hTh[:, k, :], hTl[:, k, :]) for k in range(KD)
                ]).then_inc(psB_full, 1)
            for j in range(3):
                unit_b(base["in", 0] + CT + j, first["in0"]["B"] + CT + NT * j, (hTh, hTl))
            g0 = first["prep0"]["T"]
            for t in range(NT):
                pe.wait_ge(z_ready, t + 1)
                free_t(g0 + t)
                for j in range(4):
                    last = pe.transpose(psT[(g0 + t) % 2][:, j * P:(j + 1) * P], zq[:, t, j * P:(j + 1) * P], ident)
                last.then_inc(psT_full, 1)
            pe.wait_ge(cache_in, 64)
            free_t(g0 + 3)
            for t in range(4):
                src = zq[:, t, 512:640] if t < 3 else ck0[:, :]
                last = pe.transpose(psT[(g0 + 3) % 2][:, t * P:(t + 1) * P], src, ident)
            last.then_inc(psT_full, 1)
            pe.wait_ge(psT_free, g0 + 4)
            attend(0)
            for n in range(2):
                g = first["lnorm"]["B"] + n
                pe.wait_ge(ln_in, n + 1)
                free_b(g)
                src = yc if n == 0 else cpad
                for c in range(CT):
                    last = pe.matmul(psB[g % 3][:, 0:COUT], avg, src[:, c, 0:COUT], start=(c == 0),
                                     stop=(c == CT - 1))
                last.then_inc(psB_full, 1)
            out_projection(0)
            norm(0, 1)
            pe.wait_ge(hT_lo, H["norm1"] + KD)
            ffn(0)

            ada(1)
            mods(1)
            norm(1, 0, base["in", 1], first["in1"]["B"])
            for j in range(1, 8):
                unit_b(base["in", 1] + j, first["in1"]["B"] + NT * j, (hTh, hTl))
            g0 = first["prep1"]["T"]
            pe.wait_ge(cache_in, 96)
            for n in range(7):
                t = n // 2
                if n % 2 == 0 and t < NT:
                    pe.wait_ge(z_ready, 3 + t + 1)
                free_t(g0 + n)
                for j in range(4):
                    if n == 6:
                        src = cdk[:, j * P:(j + 1) * P]
                    else:
                        src = zd[:, t, n % 2 * DIFF_W + j * P:n % 2 * DIFF_W + (j + 1) * P]
                    last = pe.transpose(psT[(g0 + n) % 2][:, j * P:(j + 1) * P], src, ident)
                last.then_inc(psT_full, 1)
            pe.wait_ge(psT_free, g0 + 7)
            attend(1)
            g0 = first["latT"]["T"]
            pe.wait_ge(z_ready, 7)
            for q in range(3):
                free_t(g0 + q)
                for t in range(3 if q < 2 else 4):
                    src = cckv[:, :] if t == 3 else zm[:, t, q * P:(q + 1) * P]
                    last = pe.transpose(psT[(g0 + q) % 2][:, t * P:(t + 1) * P], src, ident)
                last.then_inc(psT_full, 1)
            pe.wait_ge(hT_lo, H["latT"] + 3)
            for j in range(2):
                unit_b(base["lat", 1] + j, first["lat"]["B"] + NT * j, (hTh[:, 4:6, :], hTl[:, 4:6, :]))
            ck = [ckvT(h).rearrange("p (a b) -> p a b", a=1) for h in (hTh, hTl)]
            for j in range(2):
                unit_b(base["lat", 1] + 2 + j, first["lat"]["B"] + 2 * NT + 4 * j, ck, 4)
            g0 = first["prep2"]["T"]
            for n in range(14):
                t = n // 2 if n < 6 else n // 2 - 3
                pe.wait_ge(z_ready, 7 + n // 2 + 1)
                free_t(g0 + n)
                for j in range(4):
                    h = n % 2 * 4 + j
                    src = qm[:, t, h * QK:(h + 1) * QK] if n < 6 else ktmp[:, t % 2, h * QK:(h + 1) * QK]
                    last = pe.transpose(psT[(g0 + n) % 2][0:QK, j * P:(j + 1) * P], src, ident)
                last.then_inc(psT_full, 1)
            pe.wait_ge(psT_free, g0 + 14)
            attend(2)
            out_projection(1)
            norm(1, 1, base["router"], first["router"]["B"])
            for part, banks, full_sem, free in ((hTh, psA, psA_full, free_a), (hTl, psB, psB_full, free_b)):
                g0 = first["tokens"]["A" if part is hTh else "B"]
                for q in range(2 * NT):
                    if part is hTl and q == 0:
                        g = first["tables"]["B"]
                        pe.wait_ge(mask_ready, 1)
                        pe.wait_ge(jcst_in, 16)
                        free(g)
                        for t in range(NT):
                            for r in range(t + 1):
                                pe.matmul(psB[g % 3][:, t * NE:(t + 1) * NE], jcst[:, P:2 * P] if r < t else
                                          jcst[:, 0:P], mask[:, r, :], start=(r == 0), stop=(r == t))
                        for t in range(NT):
                            last = pe.matmul(psB[g % 3][:, NT * NE:(NT + 1) * NE], jcst[:, P:2 * P], mask[:, t, :],
                                             start=(t == 0), stop=(t == NT - 1))
                        last.then_inc(psB_full, 1)
                    g = g0 + q
                    free(g)
                    for k in range(4):
                        last = pe.transpose(banks[g % 3][:, k * P:(k + 1) * P],
                                            part[:, q % 2 * 4 + k, q // 2 * P:(q // 2 + 1) * P].bitcast(F32), ident)
                    last.then_inc(full_sem, 1)
            f = first["jobs"]
            pe.wait_ge(psA_free, f["A"])
            pe.wait_ge(psB_free, f["B"])
            pe.wait_ge(psT_free, f["T"])

            def gather(m, n, pieces=range(4)):
                if 0 in pieces:
                    pe.wait_ge(pick_ready, m + 1)
                    pe.wait_ge(psA_free, f["A"] + JOB_A * n)
                for q in of_pieces(pieces):
                    if q >= 2:
                        pe.wait_ge(gather_free, q - 1 + KD * m)
                    src = (toks_h, toks_l)[q // 4]
                    for k in range(2):
                        c = (q % 4 * 2 + k) * P
                        for t in range(NT):
                            last = pe.matmul(psAj[q % 2][:, k * 2 * P:(k + 1) * 2 * P], src[:, t, c:c + P],
                                             pick[:, t, :], start=(t == 0), stop=(t == NT - 1))
                    last.then_inc(gather_full, 1)

            def turn(j, n):
                pe.wait_ge(psB_free, f["B"] + j // 2 + JOB_V * n)
                for g, tiles in JT.get(j, ()):
                    pe.wait_ge(psT_free, f["T"] + g - 1 + JOB_T * n)
                    for k, q in enumerate(tiles):
                        last = pe.transpose(psT[g % 2][:, k * P:(k + 1) * P], gj[:, q * P:(q + 1) * P], ident)
                    last.then_inc(psT_full, 1)

            def bank_free(b, n):
                before = next(g % JOB_B for g in range(b - 1 + JOB_B, b - 1, -1) if JOB_BANK[g % JOB_B] == JOB_BANK[b])
                kind, c = JOB_GROUPS[before]
                m = n if before < b else n - 1
                if kind == "b":
                    return back_free, BACKS * m + BACKS + NT * c + (NT if before > ADD_AT[c] else 1)
                return psB_free, f["B"] + JOB_V * m + c + 1 + (FC if kind == "d" else 0)

            def half_products(h, n, bank, free, full_sem, stat):
                k0, k1, cols = half_shape(h)
                wh, wl = (half_of(w, h).rearrange("p (k n) -> p k n", k=k1 - k0) for w in (Wh, Wl))
                pe.wait_ge(half_lo, h + 1 + HALVES * n)
                if h % 2 == 0:
                    pe.wait_ge(*free)
                o = bank[:, 0:cols]
                for k in range(k0, k1):
                    pe.matmul(o, stat[0][:, k, :], wh[:, k - k0, :], start=(k == 0), stop=False)
                    pe.matmul(o, stat[0][:, k, :], wl[:, k - k0, :], start=False, stop=False)
                    last = pe.matmul(o, stat[1][:, k, :], wh[:, k - k0, :], start=False,
                                     stop=(h % 2 == 1 and k == k1 - 1))
                last.then_inc(full_sem if h % 2 else half_used, 1)

            def give_back(c, n):
                pe.wait_ge(psB_free, f["B"] + FC + c + 1 + JOB_V * n)
                for t in range(NT):
                    b = ADD_AT[c] + (t > 0)
                    if t < 2:
                        pe.wait_ge(*bank_free(b, n))
                    o, at = job_bank(b)[:, returned(t)], pickT[:, t * P:(t + 1) * P]
                    pe.matmul(o, at, yh[:, c % 2, :], start=True, stop=False)
                    last = pe.matmul(o, at, yl[:, c % 2, :], start=False, stop=True)
                    if t != 1:
                        last.then_inc(psB_full, 1)

            def job(i, p):
                n, m = job_number(i, p), gather_number(i, p)
                stat = [h[:, :, chosen(p)] for h in picked]
                if p is None:
                    gather(m, n)
                pe.wait_ge(gather_free, KD * m + KD)
                for h in range(HALVES):
                    j = h // 2
                    if j >= 2 * FC:
                        if h <= 4 * FC + 1:
                            pe.wait_ge(psT_free, f["T"] + JOB_T - 1 + h - 4 * FC + JOB_T * n)
                        b = W2_AT[j - 2 * FC]
                        half_products(h, n, job_bank(b), bank_free(b, n), psB_full, (mTh, mTl))
                    elif j % 2:
                        b = j // 2
                        half_products(h, n, job_bank(b), bank_free(b, n), psB_full, stat)
                    else:
                        a = j // 2
                        half_products(h, n, psAj[a % 2], (psA_free, f["A"] + a - 1 + JOB_A * n), psA_full, stat)
                    if h == 1:
                        pe.wait_ge(psT_free, f["T"] - 1 + JOB_T * n)
                        for t in range(NT):
                            last = pe.transpose(psT[0][:, t * P:(t + 1) * P], pick[:, t, chosen(p)].bitcast(F32), ident)
                        last.then_inc(psT_full, 1)
                    if h % 2 and j < 2 * FC and j in JT:
                        turn(j, n)
                    if h == 4 * FC:
                        turn(j, n)
                    if h in GATHER_AT and p == 1:
                        with pe.If(i < NE // 2 - 1):
                            gather(i + 1, n + 1, [GATHER_AT.index(h)])
                    if h % 2 and j > 2 * FC:
                        give_back(j - 2 * FC - 1, n)
                give_back(YC - 1, n)

            gather(0, 0)
            over_jobs(pe, job)

        @block.vector
        def _(dve):
            chain = [0]

            def link(ins):
                chain[0] += 1
                ins.then_inc(dve_chain, 1)
                dve.wait_ge(dve_chain, chain[0])

            def split_lo(u, i=0, per=12):
                dve.wait_ge(hi_ready, u + 1 + per * i)
                dve.tensor_tensor(lo_of(u), raw_of(u), hi_of(u).bitcast(F32), ALU.subtract).then_inc(lo_ready, 1)

            def step(u):
                if u + AHEAD < n_units:
                    split_lo(u + AHEAD)

            asked, lows = [0], [0]

            def ask_root(ins):
                ins.then_inc(ms_ready, 1)
                asked[0] += 1
                dve.wait_ge(root, asked[0])

            def low(dst, src, hi):
                lows[0] += 1
                dve.wait_ge(hT_hi, lows[0])
                dve.tensor_tensor(dst, src, hi.bitcast(F32), ALU.subtract).then_inc(hT_lo, 1)

            def ada(l):
                u0, b0 = base["ada", l], first["ada", l]["B"]

                def rows_out(j, i=0):
                    g = b0 + j
                    dve.wait_ge(psB_full, g + 1 + 6 * i)
                    dve.tensor_copy(mrow[0:4, bass.ds((j + 6 * i) * YN, YN)] if not isinstance(i, int)
                                    else mrow[0:4, (j + 6 * i) * YN:(j + 6 * i + 1) * YN],
                                    psB[g % 3][0:4, 0:YN]).then_inc(psB_free, 1)

                for j in range(6):
                    split_lo(u0 + AHEAD + j)
                    rows_out(j)
                with dve.Fori(1, 3) as i:
                    for j in range(6):
                        split_lo(u0 + AHEAD + j, i, 6)
                        rows_out(j, i)
                for j in range(6):
                    split_lo(u0 + AHEAD + 18 + j)
                    rows_out(j, 3)

            def mods(l):
                f = first["mods", l]
                g = f["T"]
                dve.wait_ge(psT_full, g + 1)
                v = psT[g % 2][:, 0:8 * KD].rearrange("p (k f c) -> p k f c", k=4, f=KD)
                for k in (1, 3):
                    gain = vecs[:, V_N[l, k // 2]:V_N[l, k // 2] + KD]
                    for c in range(2):
                        link(dve.scalar_tensor_tensor(out=mod[:, k, :, c], in0=v[:, k, :, c], scalar=1.0, in1=gain,
                                                      op0=ALU.add, op1=ALU.mult))
                link(dve.tensor_copy(mod[:, 0, :, :], v[:, 0, :, :]))
                dve.tensor_copy(mod[:, 2, :, :], v[:, 2, :, :]).then_inc(psT_free, 1)
                for n in range(8):
                    gate, cond, half = n // 4, n // 2 % 2, n % 2
                    g = f["B"] + n
                    dve.wait_ge(psB_full, g + 1)
                    dve.tensor_copy(gate_b[:, gate, cond, half * 512:(half + 1) * 512],
                                    psB[g % 3][:, :]).then_inc(psB_free, 1)

            norms = [0]

            def norm(l, w):
                n, g0 = norms[0], first["norm", l, w]["T"]
                norms[0] += 1
                if n == 3:
                    dve.wait_ge(state_out, 96)
                dve.wait_ge(sumsq, n + 1)
                dve.wait_ge(psT_free, first["mods", l]["T"] + 1)
                link(dve.reciprocal(stats[:, 28:31], stats[:, 4:7]))
                for t in range(NT):
                    ins = dve.tensor_scalar(xn[:, t, :], x[:, t, :], stats[:, 28 + t:29 + t], None, ALU.mult)
                    if t < NT - 1:
                        link(ins)
                ins.then_inc(xn_ready, 1)
                for f in range(KD):
                    dve.wait_ge(psT_free, g0 + f + 1)
                    dve.tensor_copy(hTh[:, f, :], hf[:, f % 2, :]).then_inc(hT_hi, 1)
                    low(hTl[:, f, :], hf[:, f % 2, :], hTh[:, f, :])

            def rms_heads(z, heads, hd):
                sq = scr[:, 0:heads * hd].rearrange("p (h d) -> p h d", h=heads)
                link(dve.tensor_tensor(sq, z, z, ALU.mult))
                ask_root(dve.tensor_reduce(stats[:, SS:SS + heads], sq, AX.X, ALU.add))
                link(dve.reciprocal(stats[:, RC:RC + heads], stats[:, RT:RT + heads]))

            def scaled(z, heads, hd, at, gain, factor=1.0):
                r = stats[:, RC + at:RC + at + heads].unsqueeze(2).to_broadcast([P, heads, hd])
                link(dve.scalar_tensor_tensor(out=z, in0=z, scalar=factor, in1=r, op0=ALU.mult, op1=ALU.mult))
                link(dve.tensor_tensor(z, z, gain.unsqueeze(1).to_broadcast([P, heads, hd]), ALU.mult))

            def rope(z, heads, w, t, at_c, at_s):
                cos = cst[:, at_c + (t - 1) * w:at_c + t * w].unsqueeze(1).to_broadcast([P, heads, w])
                sin = cst[:, at_s + (t - 1) * w:at_s + t * w].unsqueeze(1).to_broadcast([P, heads, w])
                rot = scr[:, 0:heads * w].rearrange("p (h d) -> p h d", h=heads)
                h = w // 2
                link(dve.tensor_tensor(rot[:, :, 0:h], z[:, :, h:w], sin[:, :, 0:h], ALU.mult))
                link(dve.tensor_tensor(rot[:, :, h:w], z[:, :, 0:h], sin[:, :, h:w], ALU.mult))
                link(dve.tensor_tensor(z, z, cos, ALU.mult))
                return dve.tensor_tensor(z, z, rot, ALU.add)

            marked = [-1]

            def nothing():
                marked[0] += 1
                return dve.memset(marks[:, marked[0]:marked[0] + 1], 0.0)

            def columns_out(u, g, dst):
                dve.wait_ge(psB_full, g + 1)
                n = units[u][2]
                first_col = n - 160 if u == base["in", 1] + 7 else 0
                dve.tensor_copy(dst, psB[g % 3][:, first_col:n]).then_inc(psB_free, 1)

            taps = [0]

            def tap():
                if taps[0] < CW * CT_V:
                    w, c = divmod(taps[0], CT_V)
                    src, k = cpad[:, c, w:w + COUT], dww[:, w * CT + c:w * CT + c + 1]
                    if w == 0:
                        ins = dve.tensor_scalar(yc[:, c, :], src, k, vecs[:, V_DWB + c:V_DWB + c + 1],
                                                ALU.mult, ALU.add)
                    else:
                        dve.wait_ge(conv_chain, taps[0] - CT_V + 1)
                        ins = dve.scalar_tensor_tensor(out=yc[:, c, :], in0=src, scalar=k, in1=yc[:, c, :],
                                                       op0=ALU.mult, op1=ALU.add)
                    ins.then_inc(conv_chain, 1)
                    taps[0] += 1

            def attend(a):
                cfg, f = ATT[a], first[f"attend{a}"]
                per = cfg["per"]
                for i in range(NS + 2):
                    if i < NS:
                        n = P * len(keys_of(i // 8))
                        g = f["A"] + i
                        dve.wait_ge(psA_full, g + 1)
                        dve.tensor_reduce(stats[:, 32 + i:33 + i], psA[g % 3][:, 0:n], AX.X,
                                          ALU.min).then_inc(bias_ready, 1)
                    if a == 0:
                        for _ in range(3):
                            tap()
                    if 1 <= i <= NS:
                        s = i - 1
                        n = P * len(keys_of(s // 8))
                        g = tgroup(a, s)
                        dve.wait_ge(psT_full, g + 1)
                        if s >= 2:
                            dve.wait_ge(*pv_signal(a, s - 2))
                        dve.tensor_copy(cfg["PT"][:, s % 2, 0:n], psT[g % 2][:, 0:n]).then_inc(psT_free, 1)
                    if i >= 2 and (i - 2) % per == per - 1:
                        rows_ready(a, (i - 2) // per)
                    if i in (otile_at(0), otile_at(1)):
                        o_low(a, i // 8 - 1)
                o_low(a, NT - 1)

            def o_low(a, t):
                k = otgroup(a, t)
                c = slice(cfg_ft(a), cfg_ft(a) + 4)
                lows[0] += 1
                dve.wait_ge(hT_hi, lows[0])
                link(dve.tensor_tensor(hTl[:, c, t * P:(t + 1) * P],
                                       psT[k % 2][:, :].rearrange("p (f n) -> p f n", f=4),
                                       hTh[:, c, t * P:(t + 1) * P].bitcast(F32), ALU.subtract))
                nothing().then_inc(psT_free, 1)
                nothing().then_inc(hT_lo, 1)

            def cfg_ft(a):
                return ATT[a]["ft"]

            def rows_ready(a, m):
                cfg, f = ATT[a], first[f"attend{a}"]
                per, n = cfg["per"], cfg["n"]
                t = m * per // 8
                g = f["B"] + m
                dve.wait_ge(psB_full, g + 1)
                dve.wait_ge(psA_free, f["A"] + (m + 1) * per)
                link(dve.reciprocal(stats[:, 16:16 + per], stats[:, 64 + m * per:64 + (m + 1) * per]))
                r = stats[:, 16:16 + per].unsqueeze(2).to_broadcast([P, per, n])
                src = psB[g % 3][:, :].rearrange("p (h d) -> p h d", h=per)
                if NT * a + t >= 1 and (a != 1 or m % 2 == 0):
                    pa, pt = divmod(NT * a + t - 1, NT)
                    dve.wait_ge(psT_full, otgroup(pa, pt) + 1)
                if a != 1:
                    dve.tensor_tensor(otok.rearrange("p (h d) -> p h d", h=per), src, r, ALU.mult).then_inc(psB_free, 1)
                    dve.wait_ge(psB_free, g + 1)
                    nothing().then_inc(o_ready, 1)
                    return
                o4 = osb.rearrange("p (h j d) -> p h j d", h=2, j=2)
                dve.tensor_tensor(osb.rearrange("p (h d) -> p h d", h=per), src, r, ALU.mult).then_inc(psB_free, 1)
                dve.wait_ge(psB_free, g + 1)
                o2 = od.rearrange("p (h d) -> p h d", h=2)
                link(dve.scalar_tensor_tensor(out=o2, in0=o4[:, :, 1, :], scalar=stats[:, 92:93], in1=o4[:, :, 0, :],
                                              op0=ALU.mult, op1=ALU.add))
                sq = scr[:, 0:256].rearrange("p (h d) -> p h d", h=2)
                link(dve.tensor_tensor(sq, o2, o2, ALU.mult))
                ask_root(dve.tensor_reduce(stats[:, 10:12], sq, AX.X, ALU.add))
                link(dve.reciprocal(stats[:, 14:16], stats[:, 12:14]))
                link(dve.scalar_tensor_tensor(out=o2, in0=o2, scalar=1.0 - LAMBDA_INIT,
                                              in1=stats[:, 14:16].unsqueeze(2).to_broadcast([P, 2, P]),
                                              op0=ALU.mult, op1=ALU.mult))
                half = m % 2
                ins = dve.tensor_tensor(otok[:, half * 256:(half + 1) * 256].rearrange("p (h d) -> p h d", h=2), o2,
                                        G["l1_diff_subln_g"].unsqueeze(1).to_broadcast([P, 2, P]), ALU.mult)
                if half == 1:
                    ins.then_inc(o_ready, 1)
                else:
                    link(ins)

            def gated(g, t, j, gate, y0, i=0, weight=None):
                n = y0 + NT * j + t
                if n - 2 > 0:
                    dve.wait_ge(x_added, n - 2 + 12 * i)
                dve.wait_ge(psB_full, g + 1 + 24 * i)
                gb = gate_b[:, gate, 0 if t == 0 else 1, j * YN:(j + 1) * YN]
                if weight is None:
                    ins = dve.tensor_tensor(ytmp[:, t, :], psB[g % 3][:, 0:YN], gb, ALU.mult)
                else:
                    ins = dve.scalar_tensor_tensor(out=ytmp[:, t, :], in0=psB[g % 3][:, 0:YN], scalar=weight, in1=gb,
                                                   op0=ALU.mult, op1=ALU.mult)
                ins.then_inc(psB_free, 1)

            def out_projection(l, y0):
                for j in range(YC):
                    step(base["out", l] + j)
                    for t in range(NT):
                        gated(first["out", l]["B"] + NT * j + t, t, j, 0, y0)

            def ffn(l, y0, h0):
                u0, f, k = base["ffn", l], first["ffn", l], (2 if l == 0 else NE)
                with dve.Fori(0, k) as i:
                    if l == 1:
                        dve.wait_ge(psB_free, f["B"] + 24 * i)
                        dve.tensor_copy(comb_e[:, :], comb[:, :, bass.ds(i, 1)].rearrange("p t e -> p (t e)")
                                        ).then_inc(comb_ready, 1)
                        dve.wait_ge(comb_ready, i + 1)
                    for j in range(3 * FC):
                        if j + AHEAD < 3 * FC or l == 0:
                            split_lo(u0 + j + AHEAD, i)
                        else:
                            with dve.If(i < k - 1):
                                split_lo(u0 + j + AHEAD, i)
                        if j < 2 * FC and j % 2:
                            c = j // 2
                            for t in range(NT):
                                g = f["B"] + NT * c + t
                                dve.wait_ge(psA_free, f["A"] + NT * c + t + 1 + 12 * i)
                                dve.wait_ge(psB_full, g + 1 + 24 * i)
                                dst = gt[:, t, c * FN:(c + 1) * FN]
                                dve.tensor_tensor(dst, dst, psB[g % 3][:, 0:FN], ALU.mult).then_inc(psB_free, 1)
                        for q in TGROUPS.get(j, ()):
                            dve.wait_ge(gT_hi, h0 + q + 1 + FT * i)
                            dve.tensor_tensor(gTl[:, q, :], psT[q % 2][:, 0:TOK], gTh[:, q, :].bitcast(F32),
                                              ALU.subtract).then_inc(psT_free, 1)
                        if j >= 2 * FC:
                            for t in range(NT):
                                gated(f["B"] + 12 + NT * (j - 2 * FC) + t, t, j - 2 * FC, 1, y0, i,
                                      comb_e[:, t:t + 1])

            link(dve.memset(chl[:, :, :].bitcast(F32), 0.0))
            link(dve.memset(comb_e[:, :], 1.0))
            dve.wait_ge(psT_full, 2)
            dve.tensor_copy(vecs[:, :], psT[0][:, 0:60]).then_inc(psT_free, 1)
            dve.tensor_copy(dww[:, :], psT[1][:, 0:CW * CT]).then_inc(psT_free, 1)
            dve.wait_ge(c_silu, 1)
            for c in range(2):
                cs = csil[:, c * KD:(c + 1) * KD]
                link(dve.tensor_copy(chl[:, :, 2 * c], cs))
                ins = dve.tensor_tensor(chl[:, :, 2 * c + 1], cs, chl[:, :, 2 * c].bitcast(F32), ALU.subtract)
                if c == 0:
                    link(ins)
            ins.then_inc(c_ready, 1)
            for u in range(AHEAD):
                split_lo(u)

            ada(0)
            mods(0)
            norm(0, 0)
            dve.wait_ge(pool_chain, 1)
            for j in range(CT):
                step(base["in", 0] + j)
                g = first["in0"]["B"] + j
                dve.wait_ge(psA_free, first["in0"]["A"] + j + 1)
                dve.wait_ge(psB_full, g + 1)
                for at, tok, n in CSEG:
                    ins = dve.tensor_tensor(cpad[:, j, at:at + n], psB[g % 3][:, tok:tok + n],
                                            hf[:, j % 2, tok:tok + n], ALU.mult)
                    if tok == 0:
                        link(ins)
                ins.then_inc(psB_free, 1)
            for j in range(3):
                u = base["in", 0] + CT + j
                step(u)
                for t in range(NT):
                    g = first["in0"]["B"] + CT + NT * j + t
                    if j < 2:
                        dve.wait_ge(psB_full, g + 1)
                        dve.tensor_copy(zq[:, t, 0:512].rearrange("p (h k d) -> p h k d", h=4, k=2)[:, :, j, :],
                                        psB[g % 3][:, 0:256].rearrange("p (h d) -> p h d", h=4)).then_inc(psB_free, 1)
                    else:
                        columns_out(u, g, zq[:, t, 512:768])
            dve.wait_ge(psB_free, first["in0"]["B"] + CT + 9)
            dve.wait_ge(gains_in, 16 * len(G))
            g0 = first["prep0"]["T"]
            for t in range(NT):
                z = zq[:, t, 0:640].rearrange("p (h d) -> p h d", h=10)
                rms_heads(z, 10, HD)
                scaled(z[:, 0:8, :], 8, HD, 0, G["l0_q_norm_g"], -(HD ** -0.5))
                scaled(z[:, 8:10, :], 2, HD, 8, G["l0_k_norm_g"])
                (rope(z, 10, HD, t, C_COS, C_SIN) if t else nothing()).then_inc(z_ready, 1)
                dve.wait_ge(z_ready, t + 1)
            attend(0)
            while taps[0] < CW * CT_V:
                tap()
            dve.wait_ge(conv_chain, CW * CT_V)
            dve.wait_ge(conv_chain_p, (CW - 1) * (CT - CT_V))
            nothing().then_inc(ln_in, 1)
            g = first["lnorm"]["B"]
            dve.wait_ge(psB_full, g + 1)
            for c in range(CT):
                ins = dve.tensor_tensor(yc[:, c, :], yc[:, c, :], psB[g % 3][:, 0:COUT], ALU.subtract)
                if c < CT - 1:
                    link(ins)
            ins.then_inc(psB_free, 1)
            dve.wait_ge(psB_free, g + 1)
            for c in range(CT):
                ins = dve.tensor_tensor(cpad[:, c, 0:COUT], yc[:, c, :], yc[:, c, :], ALU.mult)
                if c < CT - 1:
                    link(ins)
            ins.then_inc(ln_in, 1)
            g += 1
            dve.wait_ge(psB_full, g + 1)
            link(dve.tensor_copy(hf[:, 0, 0:P], psB[g % 3][:, 0:P]))
            dve.tensor_copy(hf[:, 0, P:TOK], psB[g % 3][:, 2 * PAD + P:COUT]).then_inc(psB_free, 1)
            dve.wait_ge(psB_free, g + 1)
            ask_root(nothing())
            link(dve.reciprocal(hf[:, 0, :], hf[:, 1, :]))
            for c in range(CT):
                link(dve.tensor_tensor(yv(c)[:, 0:P], yc[:, c, 0:P], hf[:, 0, 0:P], ALU.mult))
                dve.tensor_tensor(yv(c)[:, P:TOK], yc[:, c, 2 * PAD + P:COUT], hf[:, 0, P:TOK],
                                  ALU.mult).then_inc(ln_out, 1)
            for c in range(CT):
                low(hTl[:, c, :], ysil[:, c, :], hTh[:, c, :])
            out_projection(0, 0)
            norm(0, 1)
            dve.wait_ge(state_out, 32)
            ffn(0, 12, 0)

            ada(1)
            mods(1)
            dve.wait_ge(x_added, 36)
            for n, (q, k) in enumerate((("l1_lambda_q1", "l1_lambda_k1"), ("l1_lambda_q2", "l1_lambda_k2"))):
                link(dve.tensor_tensor(hf[:, 0, 0:HD], G[q], G[k], ALU.mult))
                ins = dve.tensor_reduce(stats[:, 88 + n:89 + n], hf[:, 0, 0:HD], AX.X, ALU.add)
                if n == 0:
                    link(ins)
            ins.then_inc(lam_in, 1)
            norm(1, 0)
            for j in range(8):
                u = base["in", 1] + j
                step(u)
                for t in range(NT):
                    dst = zd[:, t, j * 256:(j + 1) * 256] if j < 6 else (
                        zm[:, t, 0:256] if j == 6 else zm[:, t, 256:416])
                    columns_out(u, first["in1"]["B"] + NT * j + t, dst)
            dve.wait_ge(psB_free, first["in1"]["B"] + 24)
            dve.wait_ge(lam_e, 1)
            link(dve.tensor_tensor(stats[:, 93:94], stats[:, 91:92], stats[:, 90:91], ALU.subtract))
            link(dve.tensor_scalar(stats[:, 92:93], stats[:, 93:94], -LAMBDA_INIT, None, ALU.add))
            g0 = first["prep1"]["T"]
            for t in range(NT):
                z = zd[:, t, 0:2 * DIFF_W].rearrange("p (h d) -> p h d", h=16)
                rms_heads(z, 16, HD)
                scaled(z[:, 0:8, :], 8, HD, 0, G["l1_diff_q_norm_g"], -(HD ** -0.5))
                scaled(z[:, 8:16, :], 8, HD, 8, G["l1_diff_k_norm_g"])
                (rope(z, 16, HD, t, C_COS, C_SIN) if t else nothing()).then_inc(z_ready, 1)
                dve.wait_ge(z_ready, NT + t + 1)
            attend(1)
            dve.wait_ge(psB_free, first["in1"]["B"] + 24)
            for at, n, name in ((0, QR, "l1_mla_q_a_norm_g"), (QR, KVR, "l1_mla_kv_a_norm_g")):
                z = zm[:, :, at:at + n]
                rms_heads(z, NT, n)
                scaled(z, NT, n, 0, G[name])
            nothing().then_inc(z_ready, 1)
            g0 = first["latT"]["T"]
            for q in range(3):
                g = g0 + q
                n = TOK if q < 2 else 4 * P
                dst, hi = ((hTl[:, 4 + q, :], hTh[:, 4 + q, :]) if q < 2 else (ckvT(hTl), ckvT(hTh)))
                lows[0] += 1
                dve.wait_ge(hT_hi, lows[0])
                link(dve.tensor_tensor(dst, psT[g % 2][:, 0:n], hi.bitcast(F32), ALU.subtract))
                nothing().then_inc(psT_free, 1)
                nothing().then_inc(hT_lo, 1)
            dve.wait_ge(state_out, 64)
            b0 = first["lat"]["B"]
            for j in range(4):
                u = base["lat", 1] + j
                step(u)
                for t in range(NT if j < 2 else 4):
                    if j < 2:
                        columns_out(u, b0 + NT * j + t, qm[:, t, j * 384:(j + 1) * 384])
                    else:
                        columns_out(u, b0 + 2 * NT + 4 * (j - 2) + t, kv[:, t, (j - 2) * 512:(j - 1) * 512])
            dve.wait_ge(psB_free, b0 + 14)
            g0 = first["prep2"]["T"]
            for m in range(7):
                t = m if m < NT else m - NT
                if m < NT:
                    z = qm[:, t, :].rearrange("p (h d) -> p h d", h=MLA_H)
                    name, factor = "l1_mla_q_norm_g", -(QK ** -0.5)
                else:
                    z = ktmp[:, t % 2, :].rearrange("p (h d) -> p h d", h=MLA_H)
                    name, factor = "l1_mla_k_norm_g", 1.0
                    if t >= 2:
                        dve.wait_ge(psT_full, g0 + 2 * (m - 2) + 2)
                    kr = zm[:, t, QR + KVR:416] if t < NT else ckr[:, :]
                    link(dve.tensor_copy(z[:, :, 0:NOPE],
                                         kv[:, t, :].rearrange("p (h d) -> p h d", h=MLA_H)[:, :, 0:NOPE]))
                    link(dve.tensor_copy(z[:, :, NOPE:QK], kr.unsqueeze(1).to_broadcast([P, MLA_H, ROPE])))
                rms_heads(z, MLA_H, QK)
                scaled(z, MLA_H, QK, 0, G[name], factor)
                (rope(z[:, :, NOPE:QK], MLA_H, ROPE, t, C_COSR, C_SINR) if t in (1, 2) else nothing()
                 ).then_inc(z_ready, 1)
                dve.wait_ge(z_ready, 7 + m + 1)
            attend(2)
            out_projection(1, 36)
            norm(1, 1)
            step(base["router"])
            g = first["router"]["B"]
            dve.wait_ge(psB_full, g + NT)
            for t in range(NT):
                b = psB[(g + t) % 3][:, 0:NE]
                link(dve.max(mx8[:, t, :], b))
                dve.max_index(ix8[:, t, :], mx8[:, t, :], b).then_inc(psB_free, 1)
            dve.wait_ge(psB_free, g + NT)
            link(dve.tensor_copy(ix8f[:, :, :], ix8[:, :, :]))
            dve.tensor_tensor(rt[:, 0:3], mx8[:, :, 1], mx8[:, :, 0], ALU.subtract).then_inc(router_in, 1)
            dve.wait_ge(logit_e, 1)
            link(dve.tensor_scalar(rt[:, 8:11], rt[:, 4:7], 1.0, None, ALU.add))
            link(dve.reciprocal(rt[:, 12:15], rt[:, 8:11]))
            link(dve.tensor_tensor(rt[:, 16:19], rt[:, 12:15], rt[:, 4:7], ALU.mult))
            iota = cst[:, C_IOTA:C_IOTA + NE]
            for t in range(NT):
                link(dve.tensor_scalar(rt[:, 40:48], iota, ix8f[:, t, 0:1], None, ALU.is_equal))
                link(dve.scalar_tensor_tensor(out=mask[:, t, :], in0=iota, scalar=ix8f[:, t, 1:2], in1=rt[:, 40:48],
                                              op0=ALU.is_equal, op1=ALU.add))
                link(dve.tensor_scalar(rt[:, 24:32], rt[:, 40:48], rt[:, 12 + t:13 + t], None, ALU.mult))
                link(dve.tensor_scalar(rt[:, 32:40], iota, ix8f[:, t, 1:2], rt[:, 16 + t:17 + t],
                                       ALU.is_equal, ALU.mult))
                link(dve.tensor_tensor(comb[:, t, :], rt[:, 24:32], rt[:, 32:40], ALU.add))
            nothing().then_inc(mask_ready, 1)
            g = first["tables"]["B"]
            dve.wait_ge(psB_full, g + 1)
            all_places = slot[:, :, 0:NE]
            link(dve.tensor_tensor(all_places, psB[g % 3][:, 0:NT * NE].rearrange("p (t e) -> p t e", t=NT),
                                   mask[:, :, :], ALU.mult))
            link(dve.tensor_scalar(all_places, all_places, -1.0, None, ALU.add))
            dve.tensor_copy(jobs[:, 0:NE], psB[g % 3][:, NT * NE:(NT + 1) * NE]).then_inc(psB_free, 1)
            dve.wait_ge(psB_free, g + 1)
            f = first["jobs"]

            def choose(e, n, start, p):
                if isinstance(e, int):
                    src = slot[:, :, e]
                else:
                    src = slot[:, :, bass.ds(e, 1)].rearrange("p t e -> p (t e)")
                dve.tensor_scalar(slot_e[:, p or 0, :], src, start, None, ALU.subtract).then_inc(place_ready, 1)
                dve.wait_ge(place_ready, n + 1)
                for t in range(NT):
                    ins = dve.tensor_scalar(pick[:, t, chosen(p)], jcst[:, 2 * P:3 * P], slot_e[:, p or 0, t:t + 1],
                                            None, ALU.is_equal)
                    ins.then_inc(pick_ready if t == NT - 1 and p != 0 else pick_part, 1)

            dve.wait_ge(jcst_in, 16)
            choose(0, 0, 0.0, 0)
            choose(1, 1, 0.0, 1)
            for q in range(2 * NT):
                g = first["tokens"]["B"] + q
                dve.wait_ge(psB_full, g + 1)
                dve.tensor_copy(toks_l[:, q // 2, q % 2 * 512:(q % 2 + 1) * 512], psB[g % 3][:, :]).then_inc(psB_free, 1)
            def split_half(h, n):
                dve.wait_ge(half_hi, h + 1 + HALVES * n)
                dve.tensor_tensor(half_of(Wl, h), half_of(raw, h), half_of(Wh, h).bitcast(F32),
                                  ALU.subtract).then_inc(half_lo, 1)

            def turned(j, n):
                for g, tiles in JT.get(j, ()):
                    k = len(tiles)
                    dve.wait_ge(gT_hi, 2 * FT + g + (JOB_T - 1) * n)
                    c = slice(tiles[0], tiles[-1] + 1)
                    dve.tensor_tensor(mTl[:, c, :], psT[g % 2][:, 0:P * k].rearrange("p (f n) -> p f n", f=k),
                                      mTh[:, c, :].bitcast(F32), ALU.subtract).then_inc(psT_free, 1)

            def job(i, p):
                n = job_number(i, p)
                if p is not None:
                    e = n
                else:
                    e = dve.value_load(jobs_i[0:1, bass.ds(i + 1, 1)], min_val=0, max_val=NE - 1)
                    for h in range(HSLOTS - 1):
                        split_half(h, n)
                    choose(e, n, jobs[:, bass.ds(i + 88, 1)], None)
                for h in range(HALVES):
                    j = h // 2
                    ahead = h + HSLOTS - 1
                    if ahead < HALVES:
                        split_half(ahead, n)
                    elif p == 0:
                        split_half(ahead - HALVES, n + 1)
                    elif p == 1:
                        with dve.If(i < NE // 2 - 1):
                            split_half(ahead - HALVES, n + 1)
                    if h == 4:
                        dve.wait_ge(back_free, BACKS * n + BACKS)
                        dve.tensor_copy(comb_e[:, :], comb[:, :, bass.ds(e, 1)].rearrange("p t e -> p (t e)")
                                        ).then_inc(comb_ready, 1)
                    if h == 1:
                        dve.wait_ge(psT_full, f["T"] + 1 + JOB_T * n)
                        dve.tensor_copy(pickT[:, :], psT[0][:, 0:TOK]).then_inc(psT_free, 1)
                    if h == 8 and p == 1:
                        with dve.If(i < NE // 2 - 1):
                            choose(n + 1, n + 1, 0.0, 0)
                            choose(n + 2, n + 2, 0.0, 1)
                    if h == 4 * FC:
                        turned(j, n)
                    if h % 2 == 0:
                        continue
                    if j < 2 * FC and j % 2:
                        c = j // 2
                        dve.wait_ge(psA_free, f["A"] + c + 1 + JOB_A * n)
                        dve.wait_ge(psB_full, f["B"] + c + 1 + JOB_B * n)
                        dst = gj[:, c * FN:(c + 1) * FN]
                        dve.tensor_tensor(dst, dst, job_bank(c)[:, 0:FN], ALU.mult).then_inc(psB_free, 1)
                    elif j < 2 * FC:
                        turned(j, n)
                    else:
                        c = j - 2 * FC
                        dve.wait_ge(y_hi, c + 1 + YC * n)
                        dve.tensor_tensor(yl[:, c % 2, :], job_bank(W2_AT[c])[:, 0:YN], yh[:, c % 2, :].bitcast(F32),
                                          ALU.subtract).then_inc(psB_free, 1)

            for h in range(HSLOTS - 1):
                split_half(h, 0)
            link(dve.tensor_scalar(jobs[:, 8:16], jobs[:, 0:8], P + 0.5, None, ALU.is_gt))
            link(dve.scalar_tensor_tensor(out=jobs[:, 16:24], in0=jobs[:, 0:8], scalar=2 * P + 0.5,
                                          in1=jobs[:, 8:16], op0=ALU.is_gt, op1=ALU.add))
            for e in range(1, NE):
                link(dve.tensor_tensor(jobs[:, 16 + e:17 + e], jobs[:, 15 + e:16 + e], jobs[:, 16 + e:17 + e],
                                       ALU.add))
            run = jobs[:, 16:24].unsqueeze(1).to_broadcast([P, EXTRA, NE])
            below = jobs[:, 24:24 + EXTRA * NE].rearrange("p (j e) -> p j e", j=EXTRA)
            link(dve.tensor_tensor(below, run, iota[:, 0:EXTRA].unsqueeze(2).to_broadcast([P, EXTRA, NE]),
                                   ALU.is_le))
            link(dve.tensor_copy(jobs[:, 64:65], jobs[:, 23:24]))
            link(dve.tensor_reduce(jobs[:, 65:65 + EXTRA], below, AX.X, ALU.add))
            link(dve.tensor_scalar(jobs[:, 65:65 + EXTRA], jobs[:, 65:65 + EXTRA], NE - 1.0, None, ALU.min))
            link(dve.tensor_tensor(below, below, run, ALU.mult))
            link(dve.tensor_reduce(jobs[:, 72:72 + EXTRA], below, AX.X, ALU.max))
            link(dve.tensor_tensor(jobs[:, 80:80 + EXTRA], iota[:, 0:EXTRA], jobs[:, 72:72 + EXTRA], ALU.subtract))
            link(dve.tensor_scalar(jobs[:, 88:88 + EXTRA], jobs[:, 80:80 + EXTRA], float(P), float(P),
                                   ALU.mult, ALU.add))
            dve.tensor_copy(jobs_i[:, 0:1 + EXTRA], jobs[:, 64:65 + EXTRA]).then_inc(table_ready, 1)
            more = over_jobs(dve, job)
            for c in range(YC):
                cols = slice(c * YN, (c + 1) * YN)
                dve.wait_ge(y_added, BACKS * (NE - 1) + 6 + NT * c + BACKS * more)
                link(dve.tensor_tensor(yq[:, :, cols], yq[:, :, cols],
                                       gate_b[:, 1, 1, cols].unsqueeze(1).to_broadcast([P, 2, YN]), ALU.mult))
                dve.tensor_tensor(x[:, 1:NT, cols], x[:, 1:NT, cols], yq[:, :, cols], ALU.add).then_inc(x_done_q, 1)


_OUTS = [(1, P, D), (1, 2 * P, D), (1, P, 2, HD), (1, P, 2, HD), (1, P, 4, 2, HD), (1, P, 4, 2 * HD),
         (1, P, KVR), (1, P, ROPE)]


def kernel(**inputs):
    import concourse.bacc as _bacc
    from concourse.bass_utils import run_bass_kernel_spmd as _run

    nc = _bacc.Bacc("TRN2", target_bir_lowering=False, num_devices=1)
    arrays = {f"in_{n}": np.ascontiguousarray(a) for n, a in inputs.items()}
    arrays["in_consts"] = constants()
    arrays["in_job_consts"] = job_constants()
    A = {n[3:]: nc.dram_tensor(n, a.shape, mybir.dt.from_np(a.dtype), kind="ExternalInput").ap()
         for n, a in arrays.items()}
    out = [nc.dram_tensor(f"out_{i}", s, F32, kind="ExternalOutput").ap() for i, s in enumerate(_OUTS)]
    trunk_step(nc, A, out)
    r = _run(nc, [arrays], core_ids=[0])
    return tuple(r.results[0][f"out_{i}"] for i in range(len(_OUTS)))
```

```python
import math
from contextlib import ExitStack

import numpy as np

import concourse.bass as bass
from concourse import mybir

F32 = mybir.dt.float32
F32R = mybir.dt.float32r
U32 = mybir.dt.uint32
I32 = mybir.dt.int32
ACT = mybir.ActivationFunctionType
ALU = mybir.AluOpType
AX = mybir.AxisListType

P = 128
D = 1024
KD = D // P
NT = 3
TOK = NT * P
NC = 512
CT = NC // P
CW = 31
PAD = CW // 2
CSEG = [(PAD, 0, P), (3 * PAD + P, P, 2 * P)]
CLEN = 4 * PAD + TOK
COUT = CLEN - 2 * PAD
CT_V = 2
HD = 64
DIFF_W = 512
MLA_H, NOPE, ROPE, VD, QR, KVR = 8, 64, 32, 64, 256, 128
QK = NOPE + ROPE
LAMBDA_INIT = 0.8 - 0.6 * math.exp(-0.3 * 1)
NE = 8
FE = 1408
FT = FE // P
FC = 4
FN = FE // FC
YC = 4
YN = D // YC
RMS_EPS = 1e-6
LN_EPS = 1e-5

R = 2
R_SMALL = 3
S = 2
SLOT = 3072
assert SLOT >= KD * FN == FT * YN
QKV0 = 3
ASIDE = 6 * D // YN
PREP_ASIDES = 2
ASIDE_STEPS = 19
AHEAD = S - 1

HALVES = 6 * FC
HSLOTS = 4
HSLOT = R * SLOT // HSLOTS
HALF_K = [(0, 4), (4, 8)], [(0, 6), (6, 11)]
URGENT_A = [4 * FC]
URGENT_V = [4 * FC - 1, 4 * FC, HALVES - 1]
GATHER_AT = [4 * FC - 1, 4 * FC, 4 * FC + 2, 4 * FC + 4]
EXTRA = 5
JOB_A, JOB_B, JOB_T = 4, 16, 6
JOB_GROUPS = [("u", 0), ("u", 1), ("u", 2), ("u", 3), ("d", 0), ("d", 1), ("b", 0), ("b", 0), ("d", 2),
              ("b", 1), ("b", 1), ("d", 3), ("b", 2), ("b", 2), ("b", 3), ("b", 3)]
JOB_BANK = [0, 1, 2, 3, 0, 1, 2, 3, 0, 2, 3, 1, 2, 3, 0, 1]
W2_AT = [JOB_GROUPS.index(("d", c)) for c in range(YC)]
ADD_AT = [JOB_GROUPS.index(("b", c)) for c in range(YC)]
JOB_V = FC + YC
BACKS = 3 * YC
assert len(JOB_GROUPS) == JOB_B
assert HSLOT >= 6 * YN and HALVES % HSLOTS == 0

C_ID, C_LN = 0, 128
C_COS, C_SIN = 256, 384
C_COSR, C_SINR = 512, 576
C_SEL, C_SELB = 640, 642
C_IOTA, C_EPS = 898, 906
C_END = 908


def constants():
    c = np.zeros((P, C_END), np.float32)
    c[:, C_ID:C_ID + P] = np.eye(P, dtype=np.float32)
    c[:, C_LN:C_LN + P] = np.float32(1.0 / NC)
    n = 2 * P
    row = np.repeat(np.arange(n // 64), 64).astype(np.float32)
    col = np.tile(np.arange(64), n // 64).astype(np.float32)
    for rot, at_c, at_s in ((HD, C_COS, C_SIN), (ROPE, C_COSR, C_SINR)):
        nf = rot // 4
        inv = (np.float32(10000.0) ** (-np.arange(nf, dtype=np.float32) / np.float32(nf))).astype(np.float32)
        ang = np.concatenate([row[:, None] * inv, col[:, None] * inv], axis=-1).astype(np.float32)
        cos, sin = np.cos(ang), np.sin(ang)
        for t in range(2):
            a = slice(t * P, (t + 1) * P)
            c[:, at_c + t * rot:at_c + (t + 1) * rot] = np.concatenate([cos[a], cos[a]], axis=-1)
            c[:, at_s + t * rot:at_s + (t + 1) * rot] = np.concatenate([-sin[a], sin[a]], axis=-1)
    c[[0, 1, 4], C_SEL] = 1.0
    c[[2, 3, 4], C_SEL + 1] = 1.0
    c[[0, 1, 4], C_SELB:C_SELB + P] = 1.0
    c[[2, 3, 4], C_SELB + P:C_SELB + 2 * P] = 1.0
    c[:, C_IOTA:C_IOTA + NE] = np.arange(NE)
    c[:, C_EPS] = RMS_EPS
    c[:, C_EPS + 1] = LN_EPS
    return c


def job_constants():
    return np.concatenate([np.triu(np.ones((P, P))), np.ones((P, P)),
                           np.tile(np.arange(P), (P, 1))], axis=1).astype(np.float32)


def trunk_step(nc, A, out):
    ctx = ExitStack()
    with ctx:
        def sb(name, shape, dt=F32):
            return ctx.enter_context(nc.sbuf_tensor(name, shape, dt))

        def sem(name):
            return ctx.enter_context(nc.semaphore(name))

        x = sb("x", [P, NT, D])
        hTh = sb("hTh", [P, KD, TOK], F32R)
        hTl = sb("hTl", [P, KD, TOK], F32R)
        work = sb("work", [P, NT * FE])
        raw = sb("raw", [P, R * SLOT])
        Wh = sb("Wh", [P, S * SLOT], F32R)
        Wl = sb("Wl", [P, S * SLOT], F32R)
        gate_b = sb("gate_b", [P, 2, 2, D])
        cst = sb("cst", [P, C_END])
        hf = sb("hf", [P, 2, TOK])
        scr = sb("scr", [P, 1024])
        csil = sb("csil", [P, 2 * KD])
        chl = sb("chl", [P, KD, P], F32R)
        vecs = sb("vecs", [P, 60])
        dww = sb("dww", [P, CW * CT])
        mod = sb("mod", [P, 4, KD, 2])
        gains = sb("gains", [P, 1216])
        stats = sb("stats", [P, 160])
        comb = sb("comb", [P, NT, NE])
        comb_e = sb("comb_e", [P, NT])
        mx8 = sb("mx8", [P, NT, 8])
        ix8 = sb("ix8", [P, NT, 8], U32)
        ix8f = sb("ix8f", [P, NT, 8])
        rt = sb("rt", [P, 64])
        mask = sb("mask", [P, NT, NE])
        slot = sb("slot", [P, NT, NE + 2])
        slot_e = sb("slot_e", [P, 2, NT])
        jobs = sb("jobs", [P, 112])
        jobs_i = sb("jobs_i", [P, 8], I32)
        marks = sb("marks", [P, 88])

        cckv = sb("cckv", [P, KVR])
        ckr = sb("ckr", [P, ROPE])

        def phase(*specs):
            with ExitStack() as own:
                return [own.enter_context(nc.sbuf_tensor(n, s, d)) for n, s, d in specs]

        stage, stage_w = phase(("stage", [P, P], F32), ("stage_w", [P, P], F32))
        (mrow,) = phase(("mrow", [P, 6 * D], F32))
        zq, cpad, yc, qT0, kT0, PT0, ck0, cv0 = phase(
            ("zq", [P, NT, 768], F32), ("cpad", [P, CT, CLEN], F32), ("yc", [P, CT, COUT], F32),
            ("qT0", [P, 4, TOK], F32), ("kT0", [P, 4 * P], F32), ("PT0", [P, 2, TOK], F32),
            ("ck0", [P, P], F32), ("cv0", [P, P], F32))
        gTh, gTl, mod_rows = phase(("gTh", [P, FT, TOK], F32R), ("gTl", [P, FT, TOK], F32R),
                                   ("mod_rows", [8 * KD, P], F32))
        zd, qT1, kT1, PT1, cdk, cdv = phase(
            ("zd", [P, NT, 3 * DIFF_W], F32), ("qT1", [P, 4, TOK], F32), ("kT1", [P, 4, 4 * P], F32),
            ("PT1", [P, 2, TOK], F32), ("cdk", [P, DIFF_W], F32), ("cdv", [P, DIFF_W], F32))
        kv, kT2, qT2 = phase(
            ("kv", [P, 4, 1024], F32), ("kT2", [P, 8, 4 * P], F32), ("qT2", [P, 8, TOK], F32))
        PT2 = hf
        toks_h, toks_l, mTh, mTl, yh, yl, pick, pickT = phase(
            ("toks_h", [P, NT, D], F32R), ("toks_l", [P, NT, D], F32R), ("mTh", [P, FT, P], F32R),
            ("mTl", [P, FT, P], F32R), ("yh", [P, 2, YN], F32R), ("yl", [P, 2, YN], F32R),
            ("pick", [P, NT, 2 * P], F32R), ("pickT", [P, TOK], F32R))
        jcst = hf[:, 0, 0:3 * P]

        xn = work[:, 0:NT * D].rearrange("p (t n) -> p t n", t=NT)
        gt = work[:, :].rearrange("p (t n) -> p t n", t=NT)
        zm = work[:, 0:NT * 416].rearrange("p (t n) -> p t n", t=NT)
        osb = work[:, 1248:1760]
        od = work[:, 1760:2016]
        Pb = work[:, 2784:3552].rearrange("p (b n) -> p b n", b=2)
        otok = work[:, 3552:4064]
        ysil = work[:, 0:CT * TOK].rearrange("p (c n) -> p c n", c=CT)
        ytmp = scr[:, 0:3 * YN].rearrange("p (b n) -> p b n", b=3)

        ident = cst[:, C_ID:C_ID + P]
        avg = cst[:, C_LN:C_LN + P]
        eps_rms = cst[:, C_EPS:C_EPS + 1]
        eps_ln = cst[:, C_EPS + 1:C_EPS + 2]
        G = {}
        at = 0
        for name, n in (("l0_q_norm_g", HD), ("l0_k_norm_g", HD), ("l1_diff_q_norm_g", HD),
                        ("l1_diff_k_norm_g", HD), ("l1_lambda_q1", HD), ("l1_lambda_k1", HD),
                        ("l1_lambda_q2", HD), ("l1_lambda_k2", HD), ("l1_diff_subln_g", P),
                        ("l1_mla_q_a_norm_g", QR), ("l1_mla_kv_a_norm_g", KVR),
                        ("l1_mla_q_norm_g", QK), ("l1_mla_k_norm_g", QK)):
            G[name] = gains[:, at:at + n]
            at += n
        V_N = {(0, 0): 16, (0, 1): 24, (1, 0): 32, (1, 1): 40}
        V_DWB, V_LNG, V_LNB = 48, 52, 56

        psA = [ctx.enter_context(nc.psum_tensor(f"psA{i}", [P, 512], F32)) for i in range(3)]
        psB = [ctx.enter_context(nc.psum_tensor(f"psB{i}", [P, 512], F32)) for i in range(3)]
        psT = [ctx.enter_context(nc.psum_tensor(f"psT{i}", [P, 512], F32)) for i in range(2)]

        def rows(w):
            return w.rearrange("(k p) n -> p k n", p=P)

        units = []

        def unit(kt, n, *pieces):
            units.append((pieces, kt, n))

        base = {}
        for l in range(2):
            ada = rows(A[f"l{l}_ada_w"])
            w_in, w_out = rows(A[f"l{l}_w_in"]), rows(A[f"l{l}_w_out"])
            if l == 0:
                base["ada", l] = len(units)
                for u in range(6 * D // YN):
                    unit(KD, YN, (0, ada[:, :, u * YN:(u + 1) * YN]))
            else:
                aside = [ada[:, :, u * YN:(u + 1) * YN] for u in range(ASIDE)]
            base["in", l] = len(units)
            if l == 0:
                for j in range(QKV0):
                    unit(KD, 256, (0, w_in[:, :, 2 * NC + j * 256:2 * NC + (j + 1) * 256]))
                for j in range(CT):
                    unit(KD, 2 * P, (0, w_in[:, :, j * P:(j + 1) * P]),
                         (P, w_in[:, :, NC + j * P:NC + (j + 1) * P]))
            else:
                unit(KD, 256, (0, w_in[:, :, 1536:1792]))
                unit(KD, 256, (0, w_in[:, :, 1696:1952]))
                for j in range(6):
                    unit(KD, 256, (0, w_in[:, :, j * 256:(j + 1) * 256]))
                qb, kvb = rows(A["l1_mla_w_qb"]), rows(A["l1_mla_w_kvb"])
                base["lat", l] = len(units)
                for j in range(2):
                    unit(2, 384, (0, qb[:, :, j * 384:(j + 1) * 384]))
                for j in range(2):
                    unit(1, 512, (0, kvb[:, :, j * 512:(j + 1) * 512]))
            base["out", l] = len(units)
            for j in range(YC):
                unit(KD, YN, (0, w_out[:, :, j * YN:(j + 1) * YN]))
            if l == 1:
                base["router"] = len(units)
                unit(KD, NE, (0, rows(A["l1_router_w"])))
            base["ffn", l] = len(units)
            for i in range(2 if l == 0 else 0):
                for j in range(3 * FC):
                    unit(KD if j < 2 * FC else FT, FN if j < 2 * FC else YN, (0, None))
        n_units = len(units)
        ffn_w = [
            (A["l0_ffn_w1"].rearrange("(k p) (e n) -> e p k n", p=P, e=2),
             A["l0_ffn_w3"].rearrange("(k p) (e n) -> e p k n", p=P, e=2),
             A["l0_ffn_w2"].rearrange("(e k p) n -> e p k n", p=P, e=2)),
            (A["l1_moe_w1"].rearrange("e (k p) n -> e p k n", p=P),
             A["l1_moe_w3"].rearrange("e (k p) n -> e p k n", p=P),
             A["l1_moe_w2"].rearrange("e (k p) n -> e p k n", p=P)),
        ]
        rings = []
        for u in range(n_units):
            if base["ffn", 0] <= u < base["in", 1]:
                k = (u - base["ffn", 0]) % R
                rings.append((k, k * SLOT, R))
            else:
                k = (u - base["ffn", 0] if u < base["ffn", 0] else base["in", 1] - u) % R_SMALL
                rings.append((k, k * (R * SLOT // R_SMALL), R_SMALL))
        landed, count = [], [0] * R_SMALL
        for u, (pieces, _, _) in enumerate(units):
            count[rings[u][0]] += 16 * len(pieces)
            landed.append(count[rings[u][0]])

        def raw_of(u):
            _, kt, n = units[u]
            at = rings[u][1]
            return raw[:, at:at + kt * n]

        def hi_of(u):
            _, kt, n = units[u]
            at = u % S * SLOT
            return Wh[:, at:at + kt * n]

        def lo_of(u):
            _, kt, n = units[u]
            at = u % S * SLOT
            return Wl[:, at:at + kt * n]

        def by_k(view, u):
            return view.rearrange("p (k n) -> p k n", k=units[u][1])

        first = {}
        groups = {"A": 0, "B": 0, "T": 0}

        def takes(name, a=0, b=0, t=0):
            first[name] = dict(groups)
            groups["A"] += a
            groups["B"] += b
            groups["T"] += t

        takes("setup", t=2)
        for l in range(2):
            if l == 0:
                takes(("ada", l), b=24)
            takes(("mods", l), b=8 if l == 0 else 0, t=1)
            takes(("norm", l, 0), t=KD)
            if l == 0:
                takes("in0", a=CT, b=NT * QKV0 + CT)
                takes("prep0", t=4)
                takes("attend0", a=24, b=3, t=24 + NT)
                takes("lnorm", b=2)
            else:
                takes("in1", b=24)
                takes("latT", t=3)
                takes("prep1", t=7)
                takes("attend1", a=24, b=6, t=24 + NT)
                takes("lat", b=14)
                takes("prep2", t=14)
                takes("attend2", a=24, b=3, t=24 + NT)
            takes(("out", l), b=NT * YC)
            takes(("norm", l, 1), t=KD)
            if l == 1:
                takes("router", b=NT)
            if l == 0:
                takes(("ffn", l), a=12 * 2, b=24 * 2, t=FT * 2)
            else:
                takes("tables", b=1)
                takes("tokens", a=2 * NT, b=2 * NT)
                takes("jobs")

        raw_landed = [sem(f"raw_landed{i}") for i in range(R_SMALL)]
        squares_made = sem("squares_made")
        keys_part = sem("keys_part")
        bias_added = sem("bias_added")
        rows_back = sem("rows_back")
        gates_back = sem("gates_back")
        aside_landed = [sem(f"aside_landed{i}") for i in range(R_SMALL)]
        aside_used = sem("aside_used")
        aside_free = sem("aside_free")
        rows_kept = [sem(f"rows_kept{i}") for i in range(2)]
        hi_ready = sem("hi_ready")
        lo_ready = sem("lo_ready")
        psA_full, psA_free = sem("psA_full"), sem("psA_free")
        psB_full, psB_free = sem("psB_full"), sem("psB_free")
        psT_full, psT_free = sem("psT_full"), sem("psT_free")
        const_in = sem("const_in")
        gains_in = sem("gains_in")
        cache_in = sem("cache_in")
        bias_in = sem("bias_in")
        x_in = sem("x_in")
        y_out = sem("y_out")
        state_out = sem("state_out")
        dve_chain = sem("dve_chain")
        act_chain = sem("act_chain")
        pool_chain = sem("pool_chain")
        c_silu = sem("c_silu")
        c_ready = sem("c_ready")
        sumsq = sem("sumsq")
        root = sem("root")
        ms_ready = sem("ms_ready")
        xn_ready = sem("xn_ready")
        hT_hi = sem("hT_hi")
        hT_lo = sem("hT_lo")
        mod_part = sem("mod_part")
        z_ready = sem("z_ready")
        bias_ready = sem("bias_ready")
        pv_done = sem("pv_done")
        o_ready = sem("o_ready")
        x_added = sem("x_added")
        ln_in = sem("ln_in")
        ln_out = sem("ln_out")
        comb_ready = sem("comb_ready")
        back_free = sem("back_free")
        gather_full = sem("gather_full")
        gather_free = sem("gather_free")
        y_added = sem("y_added")
        x_done_p = sem("x_done_p")
        x_done_q = sem("x_done_q")
        logit_e = sem("logit_e")
        router_in = sem("router_in")
        lam_in = sem("lam_in")
        lam_e = sem("lam_e")
        gT_hi = sem("gT_hi")
        conv_chain = sem("conv_chain")
        tap_made = sem("tap_made")
        conv_chain_p = sem("conv_chain_p")

        half_landed = [sem(f"half_landed{i}") for i in range(HSLOTS)]
        half_hi = sem("half_hi")
        half_lo = sem("half_lo")
        half_used = sem("half_used")
        mask_ready = sem("mask_ready")
        table_ready = sem("table_ready")
        jcst_in = sem("jcst_in")
        place_ready = sem("place_ready")
        pick_ready = sem("pick_ready")
        pick_part = sem("pick_part")
        y_hi = sem("y_hi")

        def wait(eng, s, v):
            if not isinstance(v, int) or v > 0:
                eng.wait_ge(s, v)

        H, at = {}, 0
        for name, n in (("norm0", KD), ("att0", NT), ("conv", CT), ("norm1", KD), ("norm2", KD),
                        ("latT", 3), ("att1", NT), ("att2", NT), ("norm3", KD)):
            H[name] = at
            at += n

        last_group = {}
        for l in range(2):
            for u in range(24 if l == 0 else 0):
                last_group[base["ada", l] + u] = ("B", first["ada", l]["B"] + u)
            for j in range(YC):
                last_group[base["out", l] + j] = ("B", first["out", l]["B"] + NT * j + NT - 1)
            for i in range(2 if l == 0 else 0):
                f = first["ffn", l]
                for j in range(3 * FC):
                    if j < 2 * FC and j % 2 == 0:
                        g = ("A", f["A"] + 12 * i + NT * (j // 2) + NT - 1)
                    elif j < 2 * FC:
                        g = ("B", f["B"] + 24 * i + NT * (j // 2) + NT - 1)
                    else:
                        g = ("B", f["B"] + 24 * i + 12 + NT * (j - 2 * FC) + NT - 1)
                    last_group[base["ffn", l] + 12 * i + j] = g
        for j in range(CT):
            last_group[base["in", 0] + QKV0 + j] = ("B", first["in0"]["B"] + NT * QKV0 + j)
        for j in range(QKV0):
            last_group[base["in", 0] + j] = ("B", first["in0"]["B"] + NT * j + NT - 1)
        for j in range(8):
            last_group[base["in", 1] + j] = ("B", first["in1"]["B"] + NT * j + NT - 1)
        for j in range(2):
            last_group[base["lat", 1] + j] = ("B", first["lat"]["B"] + NT * j + NT - 1)
            last_group[base["lat", 1] + 2 + j] = ("B", first["lat"]["B"] + 2 * NT + 4 * j + 3)
        last_group[base["router"]] = ("B", first["router"]["B"] + NT - 1)
        full = {"A": psA_full, "B": psB_full}

        TGROUPS = {2: (0, 1), 4: (2, 3, 4), 6: (5, 6, 7), 8: (8, 9, 10)}

        def otile_at(t):
            return 8 * t + 12

        def tgroup(a, s):
            return first[f"attend{a}"]["T"] + s + sum(otile_at(t) <= s for t in range(NT - 1))

        def otgroup(a, t):
            f = first[f"attend{a}"]["T"]
            return f + otile_at(t) + t if t < NT - 1 else f + 8 * NT + NT - 1

        def ckvT(h):
            return h[:, 6:8, :].rearrange("p a b -> p (a b)")[:, 0:4 * P]

        def yv(c):
            return cpad[:, c, 0:TOK]

        def half_shape(h):
            (k0, k1), n = HALF_K[h >= 4 * FC][h % 2], (FN if h < 4 * FC else YN)
            return k0, k1, n

        def half_of(t, h):
            k0, k1, n = half_shape(h)
            at = h % HSLOTS * HSLOT
            return t[:, at:at + (k1 - k0) * n]

        def used_signal(h, n):
            j = h // 2
            if h % 2 == 0:
                return half_used, 3 * FC * n + j + 1
            if j >= 2 * FC:
                return psB_full, first["jobs"]["B"] + W2_AT[j - 2 * FC] + 1 + JOB_B * n
            if j % 2:
                return psB_full, first["jobs"]["B"] + j // 2 + 1 + JOB_B * n
            return psA_full, first["jobs"]["A"] + j // 2 + 1 + JOB_A * n

        JT = {2: ((1, (0,)), (2, (1,))), 4: ((3, (2, 3, 4)),), 6: ((4, (5, 6, 7)),), 8: ((5, (8, 9, 10)),)}
        psAj, psBj = psA[0:2], psB + psA[2:3]

        def job_bank(b):
            return psBj[JOB_BANK[b]]

        def returned(t):
            return slice((t == 2) * YN, (t == 2) * YN + YN)

        yp = scr[:, 0:D]
        yq = work[:, FE:FE + 2 * D].rearrange("p (t n) -> p t n", t=2)
        ytj = work[:, FE + 2 * D:FE + 2 * D + NT * YN].rearrange("p (t n) -> p t n", t=NT)

        def y_rows(t, c):
            cols = slice(c * YN, (c + 1) * YN)
            return yp[:, cols] if t == 0 else yq[:, t - 1, cols]
        picked = [h[:, :, 0:2 * P] for h in (hTh, hTl)]
        gj = work[:, 0:FE]

        def job_number(i, p):
            return 2 * i + p if p is not None else i + NE

        def gather_number(i, p):
            return i if p is not None else i + NE // 2

        def of_pieces(pieces):
            return [2 * k + r for k in pieces for r in range(2)]

        def chosen(p):
            return slice((p or 0) * P, (p or 0) * P + P)

        def over_jobs(eng, body):
            with eng.Fori(0, NE // 2) as i:
                for p in range(2):
                    body(i, p)
            return further_jobs(eng, body)

        def further_jobs(eng, body):
            eng.wait_ge(table_ready, 1)
            more = eng.value_load(jobs_i[0:1, 0:1], min_val=0, max_val=EXTRA)
            with eng.Fori(0, EXTRA) as i:
                with eng.If(i < more):
                    body(i, None)
            return more

        qm = work[:, 1248:3552].rearrange("p (t n) -> p t n", t=NT)
        SS, RT, RC = 96, 112, 128

        def keys_of(t):
            return [0] if t == 0 else [1, 2, 3]

        def key_cols(t):
            return (0, P) if t == 0 else (P, 4 * P)

        def head0(s):
            t, h = divmod(s, 8)
            r = slice((h // 4) * HD, (h // 4 + 1) * HD)
            lo, hi = key_cols(t)
            return (qT0[r, h % 4, t * P:(t + 1) * P], kT0[r, lo:hi],
                    [(zq[:, k, 640:768] if k < 3 else cv0[:, :])[:, (h // 4) * HD:(h // 4 + 1) * HD]
                     for k in keys_of(t)])

        def head1(s):
            t, h = divmod(s, 8)
            r = slice((h % 2) * HD, (h % 2 + 1) * HD)
            lo, hi = key_cols(t)
            return (qT1[r, h // 2, t * P:(t + 1) * P], kT1[r, h // 2, lo:hi],
                    [(zd[:, k, 1024:1536] if k < 3 else cdv[:, :])[:, (h // 2) * P:(h // 2 + 1) * P]
                     for k in keys_of(t)])

        def head2(s):
            t, h = divmod(s, 8)
            lo, hi = key_cols(t)
            return (qT2[0:QK, h, t * P:(t + 1) * P], kT2[0:QK, h, lo:hi],
                    [kv[:, k, h * P + NOPE:(h + 1) * P] for k in keys_of(t)])

        ATT = [
            dict(per=8, n=HD, head=head0, PT=PT0, ft=4, no=0),
            dict(per=4, n=P, head=head1, PT=PT1, ft=0, no=1),
            dict(per=8, n=VD, head=head2, PT=PT2, ft=4, no=2),
        ]
        NS = 8 * NT

        def pv_signal(a, s):
            per = ATT[a]["per"]
            if s % per == per - 1:
                return psB_full, first[f"attend{a}"]["B"] + s // per + 1
            return pv_done, sum(NS - NS // ATT[b]["per"] for b in range(a)) + s - s // per + 1

        def heads_of(prep, m):
            if prep == 0:
                z, heads, hd, sq = zq[:, m, 0:640], 10, HD, work[:, m % 2 * 640:(m % 2 + 1) * 640]
            elif prep == 1:
                z, heads, hd = zd[:, m % NT, m // NT * DIFF_W:(m // NT + 1) * DIFF_W], 8, HD
                sq = work[:, 1248 + m % 2 * DIFF_W:1248 + (m % 2 + 1) * DIFF_W]
            else:
                z, heads, hd = qm[:, m % NT, :], MLA_H, QK
                sq = scr[:, 256:1024] if m % 2 == 0 else hf[:, :, :].rearrange("p a b -> p (a b)")
            z, sq = (v.rearrange("p (h d) -> p h d", h=heads) for v in (z, sq))
            return z, heads, hd, sq

        PREP_AT = [0, NT, 3 * NT]
        Z_LAT, Z1, Z2 = NT + 1, NT + 1, 3 * NT + 1
        ITEM_AT = {4: 0, 5: 1, 6: 2, 7: 3}
        TURNS1 = [(0, 0), (0, 1), (0, 2), (1, 0), (1, NT), (1, 1), (1, 2)]

        mrow_kept = nc.dram_tensor("mrow_kept", [2, 6 * D], F32).ap()

        def aside_step(s):
            return s < ASIDE_STEPS

        def aside_before(s):
            return PREP_ASIDES + sum(aside_step(r) for r in range(s))

        def aside_raw(d):
            at = (rings[base["out", 0] - R_SMALL][0] + d) % R_SMALL * (R * SLOT // R_SMALL)
            return raw[:, at:at + KD * YN].rearrange("p (k n) -> p k n", k=KD)

        def aside_rows(d):
            return work[0:2, 1760 + d % 2 * YN:1760 + (d % 2 + 1) * YN]

        def aside_bank(d):
            if d < PREP_ASIDES:
                return psB[(first["attend0"]["B"] + 1 + d % 2) % 3][0:2, 0:YN]
            if d < aside_before(NS):
                s = next(r for r in range(NS) if aside_before(r + 1) == d + 1)
                return psB[(first["attend0"]["B"] + s // 8 + 1) % 3][0:2, 0:YN]
            return psA[d % 2][0:2, 0:YN]

        def tap_product(n):
            return work[:, n % 3 * COUT:n % 3 * COUT + COUT]

        block = ctx.enter_context(nc.Block())

        @block.sync
        def _(sp):
            def load(u, i=0, j=0, view=None):
                _, kt, n = units[u + j]
                slot, _, ring = rings[u + j]
                behind = u + j - base["in", 1] in (0, 1, 2)
                wait(sp, lo_ready, u + j + 12 * i - (1 if behind else ring - 1))
                dst = by_k(raw_of(u + j), u + j)
                if view is not None:
                    sp.dma_start(dst, view).then_inc(raw_landed[slot], 16)
                    return
                pieces = units[u + j][0]
                for c, src in pieces:
                    sp.dma_start(dst[:, :, c:c + n // len(pieces)], src).then_inc(raw_landed[slot], 16)

            def load_ffn(l, i):
                w1, w3, w2 = ffn_w[l]
                for j in range(3 * FC):
                    if j < 2 * FC:
                        c = j // 2
                        view = (w1, w3)[j % 2][i, :, :, c * FN:(c + 1) * FN]
                    else:
                        c = j - 2 * FC
                        view = w2[i, :, :, c * YN:(c + 1) * YN]
                    load(base["ffn", l], i, j, view)

            sp.dma_start(stage[0:KD, :], A["c_ctx"].rearrange("(k p) -> k p", p=P)).then_inc(const_in, 16)
            sp.dma_start(stage[KD:2 * KD, :], A["c"].rearrange("b (k p) -> (b k) p", p=P)).then_inc(const_in, 16)
            sp.dma_start(cst[:, :], A["consts"]).then_inc(const_in, 16)
            for (l, w), r in V_N.items():
                sp.dma_start(stage[r:r + KD, :],
                             A[f"l{l}_norm{w + 1}_g"].rearrange("(k p) -> k p", p=P)).then_inc(const_in, 16)
            for name, r in (("l0_conv_dw_b", V_DWB), ("l0_conv_ln_g", V_LNG), ("l0_conv_ln_b", V_LNB)):
                sp.dma_start(stage[r:r + CT, :], A[name].rearrange("(k p) -> k p", p=P)).then_inc(const_in, 16)
            sp.dma_start(stage_w[0:CW * CT, :],
                         A["l0_conv_dw_w"].rearrange("w (k p) -> (w k) p", p=P)).then_inc(const_in, 16)

            def load_half(e, h, n, ring_free=False):
                k0, k1, cols = half_shape(h)
                j = h // 2
                w1, w3, w2 = ffn_w[1]
                c = (j // 2 if j < 2 * FC else j - 2 * FC) * cols
                view = (w2 if j >= 2 * FC else (w1, w3)[j % 2])[e, :, k0:k1, c:c + cols]
                if not ring_free and h != 4 * FC:
                    sp.wait_ge(half_lo, h + (2 if h == 4 * FC - 1 else 1) - HSLOTS + HALVES * n)
                sp.dma_start(half_of(raw, h).rearrange("p (k n) -> p k n", k=k1 - k0),
                             view).then_inc(half_landed[h % HSLOTS], 16)

            for u in range(base["ada", 0], base["out", 0]):
                load(u)
            for d in range(ASIDE + R_SMALL):
                if d < ASIDE:
                    if d < R_SMALL:
                        sp.wait_ge(lo_ready, base["out", 0] - R_SMALL + d + 1)
                    else:
                        sp.wait_ge(aside_used, d - R_SMALL + 1)
                    sp.dma_start(aside_raw(d), aside[d]).then_inc(aside_landed[d % R_SMALL], 16)
                else:
                    sp.wait_ge(aside_used, d - R_SMALL + 1)
                    load(base["out", 0] + d - ASIDE)
                if d >= R_SMALL:
                    k = d - R_SMALL
                    sp.wait_ge(aside_free, k + 1)
                    sp.dma_start(mrow_kept[:, k * YN:(k + 1) * YN], aside_rows(k)).then_inc(rows_kept[k % 2], 16)
            load(base["out", 0] + R_SMALL)
            with sp.Fori(0, 2) as i:
                load_ffn(0, i)
            for u in range(base["in", 1], n_units):
                load(u)
            sp.wait_ge(lo_ready, n_units)
            for h in range(HSLOTS):
                load_half(0, h, 0, ring_free=True)

            def job(i, one_each):
                if one_each:
                    for h in range(HSLOTS, HALVES):
                        load_half(i, h, i)
                    for h in range(HSLOTS):
                        load_half(i + 1, h, i + 1)
                else:
                    e = sp.value_load(jobs_i[0:1, bass.ds(i + 1, 1)], min_val=0, max_val=NE - 1)
                    for h in range(HALVES):
                        load_half(e, h, i + NE)

            with sp.Fori(0, NE - 1) as i:
                job(i, True)
            for h in range(HSLOTS, HALVES):
                load_half(NE - 1, h, NE - 1)
            further_jobs(sp, job)
            sp.wait_ge(x_done_p, YC)
            sp.dma_start(out[0][0], x[:, 0, :]).then_inc(y_out, 16)
            sp.wait_ge(x_done_q, YC)
            sp.dma_start(out[1][0].rearrange("(t p) n -> p t n", p=P), x[:, 1:NT, :]).then_inc(y_out, 16)
            sp.wait_ge(y_out, 32)
            sp.wait_ge(state_out, 16 * 6)

        @block.gpsimd
        def _(pool):
            pool.dma_start(x[:, 0, :], A["x_prompt"][0]).then_inc(x_in, 16)
            pool.dma_start(x[:, 1:NT, :], A["x_sample"][0].rearrange("(t p) n -> p t n", p=P)).then_inc(x_in, 16)
            for name, view in G.items():
                pool.dma_start(view, A[name].partition_broadcast(P)).then_inc(gains_in, 16)
            pool.dma_start(cckv[:, :], A["cache_l1_mla_ckv"][0]).then_inc(cache_in, 16)
            pool.dma_start(ckr[:, :], A["cache_l1_mla_krope"][0]).then_inc(cache_in, 16)

            def gate_back(gate):
                for c in range(2):
                    src = mrow_kept[c:c + 1, (3 * gate + 2) * D:(3 * gate + 3) * D].rearrange("a n -> (a n)")
                    pool.dma_start(gate_b[:, gate, c, :], src.partition_broadcast(P)).then_inc(gates_back, 16)

            def add(b, i=0):
                for j in range(YC):
                    for t in range(NT):
                        pool.wait_ge(psB_free, b + j * NT + t + 1 + 24 * i)
                        dst = x[:, t, j * YN:(j + 1) * YN]
                        pool.tensor_tensor(dst, dst, ytmp[:, t, :], ALU.add).then_inc(x_added, 1)

            pool.wait_ge(psT_full, first["ada", 0]["T"])
            pool.dma_start(mrow[4:5, :], A["l0_ada_b"].rearrange("(a n) -> a n", a=1)).then_inc(bias_in, 16)
            pool.wait_ge(psB_free, first["mods", 0]["B"] + 8)
            pool.wait_ge(psT_free, first["mods", 0]["T"] + 1)
            pool.dma_start(ck0[:, :], A["cache_l0_gqa_k"].rearrange("b s h d -> (b s) (h d)")).then_inc(cache_in, 16)
            pool.dma_start(cv0[:, :], A["cache_l0_gqa_v"].rearrange("b s h d -> (b s) (h d)")).then_inc(cache_in, 16)
            pool.memset(cpad[:, :, :], 0.0).then_inc(pool_chain, 1)
            pool.wait_ge(z_ready, 1)
            pool.dma_start(out[2].rearrange("b s h d -> (b s) (h d)"), zq[:, 0, 512:640]).then_inc(state_out, 16)
            pool.dma_start(out[3].rearrange("b s h d -> (b s) (h d)"), zq[:, 0, 640:768]).then_inc(state_out, 16)
            for n in range(CT - CT_V, CW * (CT - CT_V)):
                w, c = divmod(n, CT - CT_V)
                k = n - (CT - CT_V)
                dst = yc[:, CT_V + c, :]
                pool.wait_ge(tap_made, n + 1)
                wait(pool, conv_chain_p, k - (CT - CT_V) + 1)
                pool.tensor_tensor(dst, dst, tap_product(n), ALU.add).then_inc(conv_chain_p, 1)
            add(first["out", 0]["B"])
            for kept in rows_kept:
                pool.wait_ge(kept, 16 * ASIDE // 2)
            for c in range(2):
                pool.dma_start(mrow_kept[c:c + 1, :], A["l1_ada_b"].rearrange("(a n) -> a n", a=1),
                               accum_op=ALU.add).then_inc(bias_added, 16)
            pool.wait_ge(bias_added, 32)
            for c in range(2):
                for k, col in enumerate((0, D, 3 * D, 4 * D)):
                    r = (4 * c + k) * KD
                    pool.dma_start(mod_rows[r:r + KD, :], mrow_kept[c:c + 1, col:col + D].rearrange(
                        "a (f n) -> (a f) n", n=P)).then_inc(rows_back, 16)
            pool.wait_ge(x_added, 12)
            gate_back(0)
            with pool.Fori(0, 2) as i:
                add(first["ffn", 0]["B"] + 12, i)
            pool.wait_ge(x_added, 36)
            gate_back(1)
            pool.wait_ge(psB_free, first["mods", 1]["B"])
            pool.wait_ge(psT_full, first["mods", 1]["T"])
            pool.dma_start(cdk[:, :], A["cache_l1_diff_k"].rearrange("b s h j d -> (b s) (h j d)")).then_inc(cache_in, 16)
            pool.dma_start(cdv[:, :], A["cache_l1_diff_v"].rearrange("b s h d -> (b s) (h d)")).then_inc(cache_in, 16)
            pool.wait_ge(state_out, 32)
            pool.wait_ge(z_ready, Z1 + NT + 1)
            pool.wait_ge(psB_free, first["in1"]["B"] + 24)
            pool.dma_start(out[4].rearrange("b s h j d -> (b s) (h j d)"), zd[:, 0, 512:1024]).then_inc(state_out, 16)
            pool.dma_start(out[5].rearrange("b s h d -> (b s) (h d)"), zd[:, 0, 1024:1536]).then_inc(state_out, 16)
            pool.wait_ge(state_out, 64)
            pool.wait_ge(z_ready, Z_LAT)
            pool.dma_start(out[6][0], zm[:, 0, QR:QR + KVR]).then_inc(state_out, 16)
            pool.dma_start(out[7][0], zm[:, 0, QR + KVR:416]).then_inc(state_out, 16)
            add(first["out", 1]["B"])
            pool.wait_ge(hT_lo, H["norm3"] + KD)
            pool.dma_start(jcst[:, :], A["job_consts"]).then_inc(jcst_in, 16)

            def job(i, p):
                n = job_number(i, p)
                for c in range(YC):
                    for t in range(NT):
                        pool.wait_ge(back_free, BACKS * n + BACKS + NT * c + t + 1)
                        pool.tensor_tensor(y_rows(t, c), y_rows(t, c), ytj[:, t, :], ALU.add).then_inc(y_added, 1)

            pool.memset(yp, 0.0).then_inc(y_added, 1)
            pool.memset(yq[:, 0, :], 0.0).then_inc(y_added, 1)
            pool.memset(yq[:, 1, :], 0.0).then_inc(y_added, 1)
            more = over_jobs(pool, job)
            for c in range(YC):
                pool.wait_ge(y_added, BACKS * (NE - 1) + 6 + NT * c + BACKS * more)
                pool.tensor_tensor(y_rows(0, c), y_rows(0, c), gate_b[:, 1, 0, c * YN:(c + 1) * YN],
                                   ALU.mult).then_inc(pool_chain, 1)
                pool.wait_ge(pool_chain, 2 + c)
                dst = x[:, 0, c * YN:(c + 1) * YN]
                pool.tensor_tensor(dst, dst, y_rows(0, c), ALU.add).then_inc(x_done_p, 1)

        @block.scalar
        def _(act):
            chain = [0]

            def link(ins):
                chain[0] += 1
                ins.then_inc(act_chain, 1)
                act.wait_ge(act_chain, chain[0])

            def split_hi(u, i=0, per=12):
                act.wait_ge(raw_landed[rings[u][0]], landed[u] + 16 * (per // rings[u][2]) * i)
                if u >= S:
                    group, g = last_group[u - S]
                    grows = 6 if per == 6 else 12 if group == "A" else 24
                    act.wait_ge(full[group], g + 1 + grows * i)
                elif not isinstance(i, int):
                    act.wait_ge(psB_full, last_group[u - S + per][1] + 1 + per * (i - 1))
                act.copy(hi_of(u), raw_of(u)).then_inc(hi_ready, 1)

            def step(u):
                if u + AHEAD < n_units:
                    split_hi(u + AHEAD)

            tables = [63]

            def table_of(function):
                tables[0] += 1
                act.activation(marks[0:1, tables[0]:tables[0] + 1], cst[0:1, 0:1], function)

            roots = [0]

            def square_root(o, i, scale, eps):
                roots[0] += 1
                act.wait_ge(ms_ready, roots[0])
                act.activation(o, i, ACT.Sqrt, scale=scale, bias=eps).then_inc(root, 1)

            def ada(l):
                u0 = base["ada", l] + AHEAD
                for j in range(6):
                    split_hi(u0 + j)
                with act.Fori(1, 3) as i:
                    for j in range(6):
                        split_hi(u0 + j, i, 6)
                for j in range(6):
                    split_hi(u0 + 18 + j)

            norms = [0]

            def norm():
                n = norms[0]
                act.wait_ge(x_in, 32)
                table_of(ACT.Sqrt)
                adds = [0, 12, 36, 48][n]
                wait(act, x_added, adds - NT)
                for t in range(NT):
                    link(act.activation(hf[:, :, :].rearrange("p a b -> p (a b)"), x[:, t, 0:D - YN], ACT.Square,
                                        accum_out=stats[:, t:t + 1]))
                link(act.activation(stats[:, 60:63], stats[:, 0:3], ACT.Identity, scale=1.0 / D, bias=eps_rms))
                for t in range(NT):
                    wait(act, x_added, adds - NT + t + 1 if adds else 0)
                    link(act.activation(scr[:, D - YN:D], x[:, t, D - YN:D], ACT.Square,
                                        accum_out=stats[:, 56 + t:57 + t]))
                    act.activation(stats[:, 4 + t:5 + t], stats[:, 56 + t:57 + t], ACT.Sqrt, scale=1.0 / D,
                                   bias=stats[:, 60 + t:61 + t]).then_inc(sumsq, 1)
                l, w = divmod(n, 2)
                act.wait_ge(psT_free, first["mods", l]["T"] + 1)
                for f in range(KD):
                    g = first["norm", l, w]["T"] + f
                    act.wait_ge(psT_full, g + 1)
                    if f >= 2:
                        act.wait_ge(hT_lo, H[f"norm{n}"] + f - 1)
                    for c, (a, b) in enumerate(((0, P), (P, TOK))):
                        act.activation(hf[:, f % 2, a:b], psT[g % 2][:, a:b], ACT.Identity,
                                       scale=mod[:, 2 * w + 1, f, c:c + 1], bias=mod[:, 2 * w, f, c:c + 1]
                                       ).then_inc(psT_free if c else mod_part, 1)
                norms[0] += 1

            def o_split(a, t):
                k = otgroup(a, t)
                act.wait_ge(psT_full, k + 1)
                act.copy(hTh[:, ATT[a]["ft"]:ATT[a]["ft"] + 4, t * P:(t + 1) * P],
                         psT[k % 2][:, :].rearrange("p (f n) -> p f n", f=4)).then_inc(hT_hi, 1)

            taps = [0]

            def tap():
                n = taps[0]
                if n >= CW * (CT - CT_V):
                    return
                taps[0] += 1
                w, c = divmod(n, CT - CT_V)
                src, k = cpad[:, CT_V + c, w:w + COUT], dww[:, w * CT + CT_V + c:w * CT + CT_V + c + 1]
                if w == 0:
                    act.activation(yc[:, CT_V + c, :], src, ACT.Identity, scale=k,
                                   bias=vecs[:, V_DWB + CT_V + c:V_DWB + CT_V + c + 1]).then_inc(tap_made, 1)
                    return
                wait(act, conv_chain_p, n - 3 - (CT - CT_V) + 1)
                act.mul(tap_product(n), src, k).then_inc(tap_made, 1)

            def aside_out(d):
                act.wait_ge(aside_used, d + 1)
                if d >= 2:
                    act.wait_ge(rows_kept[d % 2], 16 * (d // 2))
                act.copy(aside_rows(d), aside_bank(d)).then_inc(aside_free, 1)

            def attend(a):
                f = first[f"attend{a}"]
                table_of(ACT.Exp)
                for s in range(NS):
                    n = P * len(keys_of(s // 8))
                    g = f["A"] + s
                    act.wait_ge(bias_ready, NS * a + s + 1)
                    if s >= 2:
                        act.wait_ge(psT_full, tgroup(a, s - 2) + 1)
                    act.activation(Pb[:, s % 2, 0:n], psA[g % 3][:, 0:n], ACT.Exp, scale=-1.0,
                                   bias=stats[:, 32 + s:33 + s],
                                   accum_out=stats[:, 64 + s:65 + s]).then_inc(psA_free, 1)
                    if a == 0:
                        for _ in range(3):
                            tap()
                        if s >= 2 and aside_step(s - 2):
                            aside_out(aside_before(s - 2))
                    if a == 1 and s % 4 == 1 and s > 4:
                        square_root(stats[:, 12:14], stats[:, 10:12], 1.0 / P, eps_rms)
                        table_of(ACT.Exp)
                    if s in (otile_at(0), otile_at(1)):
                        o_split(a, s // 8 - 1)
                if a == 1:
                    square_root(stats[:, 12:14], stats[:, 10:12], 1.0 / P, eps_rms)
                if a == 0:
                    for d in range(aside_before(NS - 2), aside_before(NS)):
                        aside_out(d)
                o_split(a, NT - 1)

            def ffn(l):
                u0, f = base["ffn", l], first["ffn", l]
                table_of(ACT.Silu)
                act.wait_ge(state_out, 32)

                def gate_tiles(j, i):
                    for q in TGROUPS.get(j, ()):
                        act.wait_ge(psT_full, f["T"] + q + 1 + FT * i)
                        act.copy(gTh[:, q, :], psT[q % 2][:, 0:TOK]).then_inc(gT_hi, 1)

                with act.Fori(0, 2) as i:
                    for j in range(3 * FC):
                        if j == 2 * FC:
                            gate_tiles(j, i)
                        split_hi(u0 + j + AHEAD, i)
                        if j < 2 * FC and j % 2 == 0:
                            for t in range(NT):
                                g = f["A"] + NT * (j // 2) + t
                                act.wait_ge(psA_full, g + 1 + 12 * i)
                                act.activation(gt[:, t, j // 2 * FN:(j // 2 + 1) * FN], psA[g % 3][:, 0:FN],
                                               ACT.Silu).then_inc(psA_free, 1)
                        if j < 2 * FC:
                            gate_tiles(j, i)

            def qk_root(hd, heads, at=0):
                square_root(stats[:, RT + at:RT + at + heads], stats[:, SS + at:SS + at + heads], 1.0 / hd, eps_rms)

            act.wait_ge(const_in, 16 * 11)
            act.wait_ge(psT_free, 1)
            act.activation(csil[:, :], vecs[:, 0:2 * KD], ACT.Silu).then_inc(c_silu, 1)
            for u in range(AHEAD):
                split_hi(u)

            ada(0)
            norm()
            def squares(prep, m):
                z, _, _, sq = heads_of(prep, m)
                if prep == 2 and m >= NT:
                    t = m - NT
                    kr = zm[:, t, QR + KVR:416] if t < NT else ckr[:, :]
                    act.copy(z[:, :, 0:NOPE], kv[:, t, :].rearrange("p (h d) -> p h d", h=MLA_H)[:, :, 0:NOPE]
                             ).then_inc(keys_part, 1)
                    act.copy(z[:, :, NOPE:QK], kr.unsqueeze(1).to_broadcast([P, MLA_H, ROPE])).then_inc(keys_part, 1)
                    act.wait_ge(keys_part, 2 * t + 2)
                act.activation(sq, z, ACT.Square).then_inc(squares_made, 1)

            def transposed_in(g, dst):
                act.wait_ge(psT_full, g + 1)
                act.copy(dst, psT[g % 2][0:dst.shape[0], :].rearrange("p (f n) -> p f n", f=4)).then_inc(psT_free, 1)

            for j in range(QKV0):
                step(base["in", 0] + j)
            for j in range(CT):
                if j < CT - 1:
                    step(base["in", 0] + QKV0 + j)
                if j < NT:
                    act.wait_ge(psB_free, first["in0"]["B"] + NT * QKV0)
                    squares(0, j)
                    qk_root(HD, 10)
                    table_of(ACT.Sigmoid)
                g = first["in0"]["A"] + j
                act.wait_ge(psA_full, g + 1)
                if j == 0:
                    act.wait_ge(hT_lo, H["norm0"] + KD)
                if j >= 2:
                    act.wait_ge(psB_free, first["in0"]["B"] + NT * QKV0 + j - 1)
                act.activation(hf[:, j % 2, :], psA[g % 3][:, 0:TOK], ACT.Sigmoid).then_inc(psA_free, 1)
            g0 = first["prep0"]["T"]
            act.wait_ge(psB_free, first["in0"]["B"] + NT * QKV0 + CT)
            for t in range(NT):
                transposed_in(g0 + t, qT0[:, :, t * P:(t + 1) * P])
                if t < PREP_ASIDES:
                    aside_out(t)
            transposed_in(g0 + NT, kT0[:, :].rearrange("p (f n) -> p f n", f=4))
            attend(0)
            aside_out(aside_before(NS))
            table_of(ACT.Sqrt)
            square_root(hf[:, 1, :], hf[:, 0, :], 1.0, eps_ln)
            table_of(ACT.Silu)
            for c in range(CT):
                act.wait_ge(ln_out, c + 1)
                link(act.activation(ysil[:, c, :], yv(c), ACT.Silu, scale=vecs[:, V_LNG + c:V_LNG + c + 1],
                                    bias=vecs[:, V_LNB + c:V_LNB + c + 1]))
                act.copy(hTh[:, c, :], ysil[:, c, :]).then_inc(hT_hi, 1)
            for d in range(aside_before(NS) + 1, ASIDE):
                aside_out(d)
            for j in range(-1, YC):
                step(base["out", 0] + j)
            norm()
            ffn(0)

            norm()
            table_of(ACT.Exp)
            act.wait_ge(lam_in, 1)
            act.activation(stats[:, 90:92], stats[:, 88:90], ACT.Exp).then_inc(lam_e, 1)
            for j in range(8):
                step(base["in", 1] + j)
                if j in (1, 2):
                    qk_root((QR, KVR)[j - 1], NT)
                if j in ITEM_AT:
                    act.wait_ge(psB_free, first["in1"]["B"] + NT * j)
                    squares(1, ITEM_AT[j])
                    qk_root(HD, 8)
            g0 = first["prep1"]["T"]
            act.wait_ge(psB_free, first["in1"]["B"] + 24)
            squares(1, 4)
            for q in range(3):
                k = first["latT"]["T"] + q
                act.wait_ge(psT_full, k + 1)
                dst = hTh[:, 4 + q, :] if q < 2 else ckvT(hTh)
                act.copy(dst, psT[k % 2][:, 0:TOK if q < 2 else 4 * P]).then_inc(hT_hi, 1)
            squares(1, 5)
            for n, (k, t) in enumerate(TURNS1):
                transposed_in(g0 + n, (qT1, kT1)[k][:, :, t * P:(t + 1) * P])
                if n in (0, 4):
                    qk_root(HD, 8)
            attend(1)
            for j in range(4):
                step(base["lat", 1] + j)
            g0 = first["prep2"]["T"]
            act.wait_ge(psB_free, first["lat"]["B"] + 14)
            squares(2, 0)
            squares(2, 1)
            qk_root(QK, MLA_H)
            for m in range(NT + 4):
                if m + 1 < NT + 4:
                    qk_root(QK, MLA_H, MLA_H * ((m + 1) % 2))
                if m + 2 < NT + 4:
                    squares(2, m + 2)
                t = m if m < NT else m - NT
                for half in range(2):
                    transposed_in(g0 + 2 * m + half,
                                  (qT2 if m < NT else kT2)[0:QK, 4 * half:4 * half + 4, t * P:(t + 1) * P])
            attend(2)
            for j in range(YC):
                step(base["out", 1] + j)
            norm()
            step(base["router"])
            table_of(ACT.Exp)
            act.wait_ge(router_in, 1)
            act.activation(rt[:, 4:7], rt[:, 0:3], ACT.Exp).then_inc(logit_e, 1)
            for q in range(2 * NT):
                g = first["tokens"]["A"] + q
                act.wait_ge(psA_full, g + 1)
                act.copy(toks_h[:, q // 2, q % 2 * 512:(q % 2 + 1) * 512], psA[g % 3][:, :]).then_inc(psA_free, 1)

            def split_half(h, n):
                k0, k1, cols = half_shape(h)
                act.wait_ge(half_landed[h % HSLOTS], 16 * (h // HSLOTS + 1) + 16 * (HALVES // HSLOTS) * n)
                act.copy(half_of(Wh, h), half_of(raw, h)).then_inc(half_hi, 1)

            def gathered(m, pieces=range(4)):
                for q in of_pieces(pieces):
                    act.wait_ge(gather_full, q + 1 + KD * m)
                    act.copy(picked[q // 4][:, q % 4 * 2:q % 4 * 2 + 2, :],
                             psAj[q % 2][:, :].rearrange("p (f n) -> p f n", f=2)).then_inc(gather_free, 1)

            def job(i, p):
                n = job_number(i, p)
                f = first["jobs"]
                if p is None:
                    act.wait_ge(psB_full, f["B"] + JOB_B * n)
                    for h in range(HSLOTS - 1):
                        split_half(h, n)
                    gathered(gather_number(i, p))
                for h in range(HALVES):
                    ahead = h + HSLOTS - 1
                    if h in URGENT_A:
                        results(h, n)
                    if ahead < HALVES:
                        act.wait_ge(*used_signal(h - 1, n) if h else used_signal(HALVES - 1, n - 1))
                        split_half(ahead, n)
                    elif p == 0:
                        act.wait_ge(*used_signal(h - 1, n))
                        split_half(ahead - HALVES, n + 1)
                    elif p == 1:
                        with act.If(i < NE // 2 - 1):
                            act.wait_ge(*used_signal(h - 1, n))
                            split_half(ahead - HALVES, n + 1)
                    if h not in URGENT_A:
                        results(h, n)
                    if h in GATHER_AT and p == 1:
                        with act.If(i < NE // 2 - 1):
                            gathered(i + 1, [GATHER_AT.index(h)])
                    if h % 2 and h // 2 > 2 * FC:
                        given_back(h // 2 - 2 * FC - 1, n)
                given_back(YC - 1, n)

            def results(h, n):
                j, f = h // 2, first["jobs"]
                if h == 4 * FC:
                    transposed(j, n)
                elif h % 2 and j < 2 * FC and j % 2 == 0:
                    g = j // 2
                    act.wait_ge(psA_full, f["A"] + g + 1 + JOB_A * n)
                    act.activation(gj[:, j // 2 * FN:(j // 2 + 1) * FN], psAj[g % 2][:, 0:FN],
                                   ACT.Silu).then_inc(psA_free, 1)
                    transposed(j, n)
                elif h % 2 and j >= 2 * FC:
                    c = j - 2 * FC
                    act.wait_ge(psB_full, f["B"] + W2_AT[c] + 1 + JOB_B * n)
                    act.copy(yh[:, c % 2, :], job_bank(W2_AT[c])[:, 0:YN]).then_inc(y_hi, 1)
                    if c == 0:
                        act.wait_ge(comb_ready, n + 1)

            def given_back(c, n):
                for t in range(NT):
                    b = ADD_AT[c] + (t > 0)
                    act.wait_ge(y_added, BACKS * n + NT * c + t + 1)
                    act.wait_ge(psB_full, first["jobs"]["B"] + b + 1 + JOB_B * n)
                    act.activation(ytj[:, t, :], job_bank(b)[:, returned(t)], ACT.Identity,
                                   scale=comb_e[:, t:t + 1]).then_inc(back_free, 1)

            def transposed(j, n):
                for g, tiles in JT.get(j, ()):
                    act.wait_ge(psT_full, first["jobs"]["T"] + g + 1 + JOB_T * n)
                    act.copy(mTh[:, tiles[0]:tiles[-1] + 1, :],
                             psT[g % 2][:, 0:P * len(tiles)].rearrange("p (f n) -> p f n", f=len(tiles))
                             ).then_inc(gT_hi, 1)

            table_of(ACT.Silu)
            for h in range(HSLOTS - 1):
                split_half(h, 0)
            act.copy(marks[0:1, 63:64], cst[0:1, 0:1]).then_inc(back_free, BACKS)
            gathered(0)
            over_jobs(act, job)

        @block.tensor
        def _(pe):
            def free_a(g, i=0, per=12):
                if g >= 3:
                    pe.wait_ge(psA_free, g - 2 + per * i)

            def free_b(g, i=0, per=24):
                if g >= 3:
                    pe.wait_ge(psB_free, g - 2 + per * i)

            def free_t(g):
                if g >= 2:
                    pe.wait_ge(psT_free, g - 1)

            def split_products(o, pairs):
                n = len(pairs)
                for k, (sh, sl, mh, ml) in enumerate(pairs):
                    pe.matmul(o, sh, mh, start=(k == 0), stop=False)
                    pe.matmul(o, sh, ml, start=False, stop=False)
                    last = pe.matmul(o, sl, mh, start=False, stop=(k == n - 1))
                return last

            def rows_times(o, u, stat, t, cols=None):
                _, kt, n = units[u]
                wh, wl = by_k(hi_of(u), u), by_k(lo_of(u), u)
                return split_products(o[:, 0:n], [
                    (stat[0][:, k, t * P:(t + 1) * P], stat[1][:, k, t * P:(t + 1) * P], wh[:, k, :], wl[:, k, :])
                    for k in range(kt)])

            def unit_b(u, b0, stat, tiles=NT):
                pe.wait_ge(lo_ready, u + 1)
                for t in range(tiles):
                    g = b0 + t
                    free_b(g)
                    rows_times(psB[g % 3], u, stat, t).then_inc(psB_full, 1)

            def ada(l):
                u0, b0 = base["ada", l], first["ada", l]["B"]

                def one(j, i=0):
                    u, g = u0 + j, b0 + j
                    pe.wait_ge(lo_ready, u + 1 + 6 * i)
                    free_b(g, i, 6)
                    wh, wl = by_k(hi_of(u), u), by_k(lo_of(u), u)
                    for k in range(KD):
                        pe.matmul(psB[g % 3][:, 0:YN], chl[:, k, :], wh[:, k, :], start=(k == 0), stop=False)
                        last = pe.matmul(psB[g % 3][:, 0:YN], chl[:, k, :], wl[:, k, :], start=False,
                                         stop=(k == KD - 1))
                    last.then_inc(psB_full, 1)

                for j in range(6):
                    one(j)
                with pe.Fori(1, 4) as i:
                    for j in range(6):
                        one(j, i)

            def mods(l):
                f = first["mods", l]
                g = f["T"]
                free_t(g)
                if l == 1:
                    pe.wait_ge(rows_back, 16 * 8)
                    pe.transpose(psT[g % 2][:, 0:8 * KD], mod_rows[:, :],
                                 ident[0:8 * KD, 0:8 * KD]).then_inc(psT_full, 1)
                    return
                pe.wait_ge(psB_free, f["B"])
                pe.wait_ge(bias_in, 16)
                chunks = [*range(0, 2 * KD), *range(3 * KD, 5 * KD)]
                for n, c in enumerate(chunks):
                    last = pe.matmul(psT[g % 2][:, 2 * n:2 * n + 2], mrow[0:5, c * P:(c + 1) * P],
                                     cst[0:5, C_SEL:C_SEL + 2], start=True, stop=True)
                last.then_inc(psT_full, 1)

            def gate_part(n):
                gate, cond, half = n // 4, n // 2 % 2, n % 2
                g = first["mods", 0]["B"] + n
                free_b(g)
                c0 = (3 * gate + 2) * D + half * 512
                pe.matmul(psB[g % 3][:, :], cst[0:5, C_SELB + cond * P:C_SELB + (cond + 1) * P],
                          mrow[0:5, c0:c0 + 512], start=True, stop=True).then_inc(psB_full, 1)

            norms = [0]

            def norm(l, w, u=None, b0=None):
                g0 = first["norm", l, w]["T"]
                if l == w == 0:
                    gate_part(0)
                    gate_part(1)
                pe.wait_ge(xn_ready, norms[0] + 1)

                def products(k):
                    if k == 0:
                        pe.wait_ge(lo_ready, u + 1)
                        for t in range(NT):
                            free_b(b0 + t)
                    pe.wait_ge(hT_lo, H[f"norm{norms[0]}"] + k + 1)
                    wh, wl, n = by_k(hi_of(u), u)[:, k, :], by_k(lo_of(u), u)[:, k, :], units[u][2]
                    for t in range(NT):
                        o = psB[(b0 + t) % 3][:, 0:n]
                        sh, sl = (h[:, k, t * P:(t + 1) * P] for h in (hTh, hTl))
                        pe.matmul(o, sh, wh, start=(k == 0), stop=False)
                        pe.matmul(o, sh, wl, start=False, stop=False)
                        last = pe.matmul(o, sl, wh, start=False, stop=(k == KD - 1))
                        if k == KD - 1:
                            last.then_inc(psB_full, 1)

                for f in range(KD):
                    free_t(g0 + f)
                    for t in range(NT):
                        last = pe.transpose(psT[(g0 + f) % 2][:, t * P:(t + 1) * P], xn[:, t, f * P:(f + 1) * P],
                                            ident)
                    last.then_inc(psT_full, 1)
                    if l == w == 0 and f >= 2:
                        gate_part(f)
                    if u is not None and f >= 2:
                        products(f - 2)
                if u is not None:
                    products(KD - 2)
                    products(KD - 1)
                norms[0] += 1

            def aside_product(d):
                f = first["attend0"]["B"]
                pe.wait_ge(aside_landed[d % R_SMALL], 16 * (d // R_SMALL + 1))
                if d >= 2:
                    pe.wait_ge(aside_free, d - 1 if d < PREP_ASIDES or d > aside_before(NS) else d)
                pe.wait_ge(psB_free, f + (1 if d >= aside_before(16) else 0))
                for k in range(KD):
                    last = pe.matmul(aside_bank(d), csil[:, :].rearrange("p (c k) -> p k c", c=2)[:, k, :],
                                     aside_raw(d)[:, k, :], start=(k == 0), stop=(k == KD - 1))
                last.then_inc(aside_used, 1)

            def attend(a):
                cfg, f = ATT[a], first[f"attend{a}"]
                for i in range(NS + 2):
                    if i < NS:
                        g = f["A"] + i
                        free_a(g)
                        q, k, _ = cfg["head"](i)
                        pe.matmul(psA[g % 3][:, 0:P * len(keys_of(i // 8))], q, k,
                                  start=True, stop=True).then_inc(psA_full, 1)
                    if 1 <= i <= NS:
                        s = i - 1
                        g = tgroup(a, s)
                        pe.wait_ge(psA_free, f["A"] + s + 1)
                        free_t(g)
                        for k in range(len(keys_of(s // 8))):
                            last = pe.transpose(psT[g % 2][:, k * P:(k + 1) * P],
                                                Pb[:, s % 2, k * P:(k + 1) * P], ident)
                        last.then_inc(psT_full, 1)
                    if i >= 2:
                        s = i - 2
                        g = f["B"] + s // cfg["per"]
                        if s % cfg["per"] == 0:
                            free_b(g)
                            if a == 0 and s > 0:
                                pe.wait_ge(aside_free, aside_before(s))
                        pe.wait_ge(psT_free, tgroup(a, s) + 1)
                        c = s % cfg["per"] * cfg["n"]
                        vs = cfg["head"](s)[2]
                        for k, v in enumerate(vs):
                            last = pe.matmul(psB[g % 3][:, c:c + cfg["n"]], cfg["PT"][:, s % 2, k * P:(k + 1) * P],
                                             v, start=(k == 0), stop=(k == len(vs) - 1))
                        last.then_inc(pv_signal(a, s)[0], 1)
                        if a == 0 and aside_step(s):
                            aside_product(aside_before(s))
                    if i in (otile_at(0), otile_at(1)):
                        o_transpose(a, i // 8 - 1)
                o_transpose(a, NT - 1)

            def o_transpose(a, t):
                g = otgroup(a, t)
                pe.wait_ge(o_ready, NT * a + t + 1)
                free_t(g)
                for k in range(4):
                    last = pe.transpose(psT[g % 2][:, k * P:(k + 1) * P], otok[:, k * P:(k + 1) * P], ident)
                last.then_inc(psT_full, 1)

            def out_projection(l):
                pe.wait_ge(hT_lo, H["att0" if l == 0 else "att2"] + (NT + CT if l == 0 else NT))
                for j in range(YC):
                    unit_b(base["out", l] + j, first["out", l]["B"] + NT * j, (hTh, hTl))

            def ffn(l):
                u0, f = base["ffn", l], first["ffn", l]

                def transposes(j, i):
                    pe.wait_ge(psB_free, f["B"] + NT * (j // 2) + 24 * i)
                    for q in TGROUPS[j]:
                        pe.wait_ge(psT_free, f["T"] + (q if q < 2 else q - 1) + FT * i)
                        for t in range(NT):
                            last = pe.transpose(psT[q % 2][:, t * P:(t + 1) * P],
                                                gt[:, t, q * P:(q + 1) * P], ident)
                        last.then_inc(psT_full, 1)

                with pe.Fori(0, 2) as i:
                    for j in range(3 * FC):
                        u = u0 + j
                        if j == 2 * FC:
                            transposes(j, i)
                            pe.wait_ge(psT_free, f["T"] + FT + FT * i)
                        pe.wait_ge(lo_ready, u + 1 + 12 * i)
                        for t in range(NT):
                            if j < 2 * FC and j % 2 == 0:
                                g = f["A"] + NT * (j // 2) + t
                                free_a(g, i)
                                rows_times(psA[g % 3], u, (hTh, hTl), t).then_inc(psA_full, 1)
                            else:
                                g = f["B"] + NT * (j // 2 if j < 2 * FC else j - FC) + t
                                free_b(g, i)
                                rows_times(psB[g % 3], u, (hTh, hTl) if j < 2 * FC else (gTh, gTl),
                                           t).then_inc(psB_full, 1)
                        if j in TGROUPS and j < 2 * FC:
                            transposes(j, i)

            pe.wait_ge(const_in, 16 * 11)
            pe.transpose(psT[0][:, 0:60], stage[0:60, :], ident[0:60, 0:60]).then_inc(psT_full, 1)
            pe.transpose(psT[1][:, 0:CW * CT], stage_w[0:CW * CT, :],
                         ident[0:CW * CT, 0:CW * CT]).then_inc(psT_full, 1)
            pe.wait_ge(c_ready, 1)
            ada(0)
            mods(0)
            norm(0, 0)
            pe.wait_ge(hT_lo, H["norm0"] + KD)
            for j in range(QKV0):
                unit_b(base["in", 0] + j, first["in0"]["B"] + NT * j, (hTh, hTl))
            for j in range(CT):
                u = base["in", 0] + QKV0 + j
                pe.wait_ge(lo_ready, u + 1)
                wh, wl = by_k(hi_of(u), u), by_k(lo_of(u), u)
                ga, gb = first["in0"]["A"] + j, first["in0"]["B"] + NT * QKV0 + j
                free_a(ga)
                c = slice(P, 2 * P)
                split_products(psA[ga % 3][:, 0:TOK], [
                    (wh[:, k, c], wl[:, k, c], hTh[:, k, :], hTl[:, k, :]) for k in range(KD)
                ]).then_inc(psA_full, 1)
                free_b(gb)
                c = slice(0, P)
                split_products(psB[gb % 3][:, 0:TOK], [
                    (wh[:, k, c], wl[:, k, c], hTh[:, k, :], hTl[:, k, :]) for k in range(KD)
                ]).then_inc(psB_full, 1)
            g0 = first["prep0"]["T"]
            for t in range(NT):
                pe.wait_ge(z_ready, t + 1)
                free_t(g0 + t)
                for j in range(4):
                    last = pe.transpose(psT[(g0 + t) % 2][:, j * P:(j + 1) * P], zq[:, t, j * P:(j + 1) * P], ident)
                last.then_inc(psT_full, 1)
                if t < PREP_ASIDES:
                    aside_product(t)
            pe.wait_ge(cache_in, 64)
            free_t(g0 + 3)
            for t in range(4):
                src = zq[:, t, 512:640] if t < 3 else ck0[:, :]
                last = pe.transpose(psT[(g0 + 3) % 2][:, t * P:(t + 1) * P], src, ident)
            last.then_inc(psT_full, 1)
            pe.wait_ge(psT_free, g0 + 4)
            attend(0)
            for n in range(2):
                g = first["lnorm"]["B"] + n
                pe.wait_ge(ln_in, n + 1)
                free_b(g)
                src = yc if n == 0 else cpad
                if n == 0:
                    pe.wait_ge(aside_free, aside_before(NS))
                    pe.wait_ge(psA_free, first["attend0"]["A"] + NS)
                for c in range(CT):
                    last = pe.matmul(psB[g % 3][:, 0:COUT], avg, src[:, c, 0:COUT], start=(c == 0),
                                     stop=(c == CT - 1))
                last.then_inc(psB_full, 1)
                for d in range(aside_before(NS), aside_before(NS) + 1) if n == 0 else \
                        range(aside_before(NS) + 1, ASIDE):
                    aside_product(d)
            out_projection(0)
            norm(0, 1)
            pe.wait_ge(hT_lo, H["norm1"] + KD)
            ffn(0)

            mods(1)
            norm(1, 0, base["in", 1], first["in1"]["B"])
            for j in range(1, 8):
                unit_b(base["in", 1] + j, first["in1"]["B"] + NT * j, (hTh, hTl))
            pe.wait_ge(cache_in, 96)
            g0 = first["latT"]["T"]
            pe.wait_ge(z_ready, Z_LAT)
            for q in range(3):
                free_t(g0 + q)
                for t in range(3 if q < 2 else 4):
                    src = cckv[:, :] if t == 3 else zm[:, t, q * P:(q + 1) * P]
                    last = pe.transpose(psT[(g0 + q) % 2][:, t * P:(t + 1) * P], src, ident)
                last.then_inc(psT_full, 1)
            g0 = first["prep1"]["T"]
            pe.wait_ge(psT_free, g0)
            for n, (k, t) in enumerate(TURNS1):
                if t < NT:
                    pe.wait_ge(z_ready, Z1 + NT * k + t + 1)
                free_t(g0 + n)
                for j in range(4):
                    if t == NT:
                        src = cdk[:, j * P:(j + 1) * P]
                    else:
                        src = zd[:, t, k * DIFF_W + j * P:k * DIFF_W + (j + 1) * P]
                    last = pe.transpose(psT[(g0 + n) % 2][:, j * P:(j + 1) * P], src, ident)
                last.then_inc(psT_full, 1)
            pe.wait_ge(psT_free, g0 + 7)
            attend(1)
            pe.wait_ge(hT_lo, H["latT"] + 3)
            for j in range(2):
                unit_b(base["lat", 1] + j, first["lat"]["B"] + NT * j, (hTh[:, 4:6, :], hTl[:, 4:6, :]))
            ck = [ckvT(h).rearrange("p (a b) -> p a b", a=1) for h in (hTh, hTl)]
            for j in range(2):
                unit_b(base["lat", 1] + 2 + j, first["lat"]["B"] + 2 * NT + 4 * j, ck, 4)
            g0 = first["prep2"]["T"]
            for n in range(14):
                pe.wait_ge(z_ready, Z2 + n // 2 + 1)
                free_t(g0 + n)
                for j in range(4):
                    h = n % 2 * 4 + j
                    src = qm[:, n // 2 % NT, h * QK:(h + 1) * QK]
                    last = pe.transpose(psT[(g0 + n) % 2][0:QK, j * P:(j + 1) * P], src, ident)
                last.then_inc(psT_full, 1)
            pe.wait_ge(psT_free, g0 + 14)
            attend(2)
            out_projection(1)
            norm(1, 1, base["router"], first["router"]["B"])
            for part, banks, full_sem, free in ((hTh, psA, psA_full, free_a), (hTl, psB, psB_full, free_b)):
                g0 = first["tokens"]["A" if part is hTh else "B"]
                for q in range(2 * NT):
                    if part is hTl and q == 0:
                        g = first["tables"]["B"]
                        pe.wait_ge(mask_ready, 1)
                        pe.wait_ge(jcst_in, 16)
                        free(g)
                        for t in range(NT):
                            for r in range(t + 1):
                                pe.matmul(psB[g % 3][:, t * NE:(t + 1) * NE], jcst[:, P:2 * P] if r < t else
                                          jcst[:, 0:P], mask[:, r, :], start=(r == 0), stop=(r == t))
                        for t in range(NT):
                            last = pe.matmul(psB[g % 3][:, NT * NE:(NT + 1) * NE], jcst[:, P:2 * P], mask[:, t, :],
                                             start=(t == 0), stop=(t == NT - 1))
                        last.then_inc(psB_full, 1)
                    g = g0 + q
                    free(g)
                    for k in range(4):
                        last = pe.transpose(banks[g % 3][:, k * P:(k + 1) * P],
                                            part[:, q % 2 * 4 + k, q // 2 * P:(q // 2 + 1) * P].bitcast(F32), ident)
                    last.then_inc(full_sem, 1)
            f = first["jobs"]
            pe.wait_ge(psA_free, f["A"])
            pe.wait_ge(psB_free, f["B"])
            pe.wait_ge(psT_free, f["T"])

            def gather(m, n, pieces=range(4)):
                if 0 in pieces:
                    pe.wait_ge(pick_ready, m + 1)
                    pe.wait_ge(psA_free, f["A"] + JOB_A * n)
                for q in of_pieces(pieces):
                    if q >= 2:
                        pe.wait_ge(gather_free, q - 1 + KD * m)
                    src = (toks_h, toks_l)[q // 4]
                    for k in range(2):
                        c = (q % 4 * 2 + k) * P
                        for t in range(NT):
                            last = pe.matmul(psAj[q % 2][:, k * 2 * P:(k + 1) * 2 * P], src[:, t, c:c + P],
                                             pick[:, t, :], start=(t == 0), stop=(t == NT - 1))
                    last.then_inc(gather_full, 1)

            def turn(j, n):
                pe.wait_ge(psB_free, f["B"] + j // 2 + JOB_V * n)
                for g, tiles in JT.get(j, ()):
                    pe.wait_ge(psT_free, f["T"] + g - 1 + JOB_T * n)
                    for k, q in enumerate(tiles):
                        last = pe.transpose(psT[g % 2][:, k * P:(k + 1) * P], gj[:, q * P:(q + 1) * P], ident)
                    last.then_inc(psT_full, 1)

            def bank_free(b, n):
                before = next(g % JOB_B for g in range(b - 1 + JOB_B, b - 1, -1) if JOB_BANK[g % JOB_B] == JOB_BANK[b])
                kind, c = JOB_GROUPS[before]
                m = n if before < b else n - 1
                if kind == "b":
                    return back_free, BACKS * m + BACKS + NT * c + (NT if before > ADD_AT[c] else 1)
                return psB_free, f["B"] + JOB_V * m + c + 1 + (FC if kind == "d" else 0)

            def half_products(h, n, bank, free, full_sem, stat):
                k0, k1, cols = half_shape(h)
                wh, wl = (half_of(w, h).rearrange("p (k n) -> p k n", k=k1 - k0) for w in (Wh, Wl))
                pe.wait_ge(half_lo, h + 1 + HALVES * n)
                if h % 2 == 0:
                    pe.wait_ge(*free)
                o = bank[:, 0:cols]
                for k in range(k0, k1):
                    pe.matmul(o, stat[0][:, k, :], wh[:, k - k0, :], start=(k == 0), stop=False)
                    pe.matmul(o, stat[0][:, k, :], wl[:, k - k0, :], start=False, stop=False)
                    last = pe.matmul(o, stat[1][:, k, :], wh[:, k - k0, :], start=False,
                                     stop=(h % 2 == 1 and k == k1 - 1))
                last.then_inc(full_sem if h % 2 else half_used, 1)

            def give_back(c, n):
                pe.wait_ge(psB_free, f["B"] + FC + c + 1 + JOB_V * n)
                for t in range(NT):
                    b = ADD_AT[c] + (t > 0)
                    if t < 2:
                        pe.wait_ge(*bank_free(b, n))
                    o, at = job_bank(b)[:, returned(t)], pickT[:, t * P:(t + 1) * P]
                    pe.matmul(o, at, yh[:, c % 2, :], start=True, stop=False)
                    last = pe.matmul(o, at, yl[:, c % 2, :], start=False, stop=True)
                    if t != 1:
                        last.then_inc(psB_full, 1)

            def job(i, p):
                n, m = job_number(i, p), gather_number(i, p)
                stat = [h[:, :, chosen(p)] for h in picked]
                if p is None:
                    gather(m, n)
                pe.wait_ge(gather_free, KD * m + KD)
                for h in range(HALVES):
                    j = h // 2
                    if j >= 2 * FC:
                        if h <= 4 * FC + 1:
                            pe.wait_ge(psT_free, f["T"] + JOB_T - 1 + h - 4 * FC + JOB_T * n)
                        b = W2_AT[j - 2 * FC]
                        half_products(h, n, job_bank(b), bank_free(b, n), psB_full, (mTh, mTl))
                    elif j % 2:
                        b = j // 2
                        half_products(h, n, job_bank(b), bank_free(b, n), psB_full, stat)
                    else:
                        a = j // 2
                        half_products(h, n, psAj[a % 2], (psA_free, f["A"] + a - 1 + JOB_A * n), psA_full, stat)
                    if h == 1:
                        pe.wait_ge(psT_free, f["T"] - 1 + JOB_T * n)
                        for t in range(NT):
                            last = pe.transpose(psT[0][:, t * P:(t + 1) * P], pick[:, t, chosen(p)].bitcast(F32), ident)
                        last.then_inc(psT_full, 1)
                    if h % 2 and j < 2 * FC and j in JT:
                        turn(j, n)
                    if h == 4 * FC:
                        turn(j, n)
                    if h in GATHER_AT and p == 1:
                        with pe.If(i < NE // 2 - 1):
                            gather(i + 1, n + 1, [GATHER_AT.index(h)])
                    if h % 2 and j > 2 * FC:
                        give_back(j - 2 * FC - 1, n)
                give_back(YC - 1, n)

            gather(0, 0)
            over_jobs(pe, job)

        @block.vector
        def _(dve):
            chain = [0]

            def link(ins):
                chain[0] += 1
                ins.then_inc(dve_chain, 1)
                dve.wait_ge(dve_chain, chain[0])

            def split_lo(u, i=0, per=12):
                dve.wait_ge(hi_ready, u + 1 + per * i)
                dve.tensor_tensor(lo_of(u), raw_of(u), hi_of(u).bitcast(F32), ALU.subtract).then_inc(lo_ready, 1)

            def step(u):
                if u + AHEAD < n_units:
                    split_lo(u + AHEAD)

            asked, lows = [0], [0]

            def ask_root(ins):
                ins.then_inc(ms_ready, 1)
                asked[0] += 1
                dve.wait_ge(root, asked[0])

            def low(dst, src, hi):
                lows[0] += 1
                dve.wait_ge(hT_hi, lows[0])
                dve.tensor_tensor(dst, src, hi.bitcast(F32), ALU.subtract).then_inc(hT_lo, 1)

            def ada(l):
                u0, b0 = base["ada", l], first["ada", l]["B"]

                def rows_out(j, i=0):
                    g = b0 + j
                    dve.wait_ge(psB_full, g + 1 + 6 * i)
                    dve.tensor_copy(mrow[0:4, bass.ds((j + 6 * i) * YN, YN)] if not isinstance(i, int)
                                    else mrow[0:4, (j + 6 * i) * YN:(j + 6 * i + 1) * YN],
                                    psB[g % 3][0:4, 0:YN]).then_inc(psB_free, 1)

                for j in range(6):
                    split_lo(u0 + AHEAD + j)
                    rows_out(j)
                with dve.Fori(1, 3) as i:
                    for j in range(6):
                        split_lo(u0 + AHEAD + j, i, 6)
                        rows_out(j, i)
                for j in range(6):
                    split_lo(u0 + AHEAD + 18 + j)
                    rows_out(j, 3)

            def mods(l):
                f = first["mods", l]
                g = f["T"]
                dve.wait_ge(psT_full, g + 1)
                v = psT[g % 2][:, 0:8 * KD]
                v = (v.rearrange("p (k f c) -> p k f c", k=4, f=KD) if l == 0 else
                     v.rearrange("p (c k f) -> p k f c", c=2, k=4))
                for k in (1, 3):
                    gain = vecs[:, V_N[l, k // 2]:V_N[l, k // 2] + KD]
                    for c in range(2):
                        link(dve.scalar_tensor_tensor(out=mod[:, k, :, c], in0=v[:, k, :, c], scalar=1.0, in1=gain,
                                                      op0=ALU.add, op1=ALU.mult))
                link(dve.tensor_copy(mod[:, 0, :, :], v[:, 0, :, :]))
                dve.tensor_copy(mod[:, 2, :, :], v[:, 2, :, :]).then_inc(psT_free, 1)

            def gate_part(n):
                gate, cond, half = n // 4, n // 2 % 2, n % 2
                g = first["mods", 0]["B"] + n
                dve.wait_ge(psB_full, g + 1)
                dve.tensor_copy(gate_b[:, gate, cond, half * 512:(half + 1) * 512],
                                psB[g % 3][:, :]).then_inc(psB_free, 1)

            norms = [0]

            def norm(l, w):
                n, g0 = norms[0], first["norm", l, w]["T"]
                norms[0] += 1
                if n == 3:
                    dve.wait_ge(state_out, 96)
                for t in range(NT):
                    dve.wait_ge(sumsq, NT * n + t + 1)
                    link(dve.reciprocal(stats[:, 28 + t:29 + t], stats[:, 4 + t:5 + t]))
                    ins = dve.tensor_scalar(xn[:, t, :], x[:, t, :], stats[:, 28 + t:29 + t], None, ALU.mult)
                    if t < NT - 1:
                        link(ins)
                ins.then_inc(xn_ready, 1)
                if w == 0:
                    mods(l)
                for f in range(KD):
                    dve.wait_ge(psT_free, g0 + f + 1)
                    dve.tensor_copy(hTh[:, f, :], hf[:, f % 2, :]).then_inc(hT_hi, 1)
                    low(hTl[:, f, :], hf[:, f % 2, :], hTh[:, f, :])
                    if l == w == 0:
                        gate_part(f)

            def sums_item(prep, m, at=0):
                _, heads, _, sq = heads_of(prep, m)
                dve.wait_ge(squares_made, PREP_AT[prep] + m + 1)
                dve.tensor_reduce(stats[:, SS + at:SS + at + heads], sq, AX.X, ALU.add).then_inc(ms_ready, 1)
                asked[0] += 1
                return asked[0]

            def rms_item(prep, m):
                dve.wait_ge(root, sums_item(prep, m))
                z, heads, _, _ = heads_of(prep, m)
                link(dve.reciprocal(stats[:, RC:RC + heads], stats[:, RT:RT + heads]))
                return z

            def rms_heads(z, heads, hd):
                sq = scr[:, 0:heads * hd].rearrange("p (h d) -> p h d", h=heads)
                link(dve.tensor_tensor(sq, z, z, ALU.mult))
                ask_root(dve.tensor_reduce(stats[:, SS:SS + heads], sq, AX.X, ALU.add))
                link(dve.reciprocal(stats[:, RC:RC + heads], stats[:, RT:RT + heads]))

            def over_rms(z, heads, hd, at, factor=1.0):
                r = stats[:, RC + at:RC + at + heads].unsqueeze(2).to_broadcast([P, heads, hd])
                link(dve.scalar_tensor_tensor(out=z, in0=z, scalar=factor, in1=r, op0=ALU.mult, op1=ALU.mult))

            def scaled(z, heads, hd, at, gain, factor=1.0):
                over_rms(z, heads, hd, at, factor)
                link(dve.tensor_tensor(z, z, gain.unsqueeze(1).to_broadcast([P, heads, hd]), ALU.mult))

            def rope(z, heads, w, t, at_c, at_s):
                cos = cst[:, at_c + (t - 1) * w:at_c + t * w].unsqueeze(1).to_broadcast([P, heads, w])
                sin = cst[:, at_s + (t - 1) * w:at_s + t * w].unsqueeze(1).to_broadcast([P, heads, w])
                rot = scr[:, 0:heads * w].rearrange("p (h d) -> p h d", h=heads)
                h = w // 2
                link(dve.tensor_tensor(rot[:, :, 0:h], z[:, :, h:w], sin[:, :, 0:h], ALU.mult))
                link(dve.tensor_tensor(rot[:, :, h:w], z[:, :, 0:h], sin[:, :, h:w], ALU.mult))
                link(dve.tensor_tensor(z, z, cos, ALU.mult))
                return dve.tensor_tensor(z, z, rot, ALU.add)

            marked = [-1]

            def nothing():
                marked[0] += 1
                return dve.memset(marks[:, marked[0]:marked[0] + 1], 0.0)

            def columns_out(u, g, dst):
                dve.wait_ge(psB_full, g + 1)
                n = units[u][2]
                first_col = n - 160 if u == base["in", 1] + 1 else 0
                dve.tensor_copy(dst, psB[g % 3][:, first_col:n]).then_inc(psB_free, 1)

            taps = [0]

            def tap():
                if taps[0] < CW * CT_V:
                    w, c = divmod(taps[0], CT_V)
                    src, k = cpad[:, c, w:w + COUT], dww[:, w * CT + c:w * CT + c + 1]
                    if w == 0:
                        ins = dve.tensor_scalar(yc[:, c, :], src, k, vecs[:, V_DWB + c:V_DWB + c + 1],
                                                ALU.mult, ALU.add)
                    else:
                        dve.wait_ge(conv_chain, taps[0] - CT_V + 1)
                        ins = dve.scalar_tensor_tensor(out=yc[:, c, :], in0=src, scalar=k, in1=yc[:, c, :],
                                                       op0=ALU.mult, op1=ALU.add)
                    ins.then_inc(conv_chain, 1)
                    taps[0] += 1

            def attend(a):
                cfg, f = ATT[a], first[f"attend{a}"]
                per = cfg["per"]
                for i in range(NS + 2):
                    if i < NS:
                        n = P * len(keys_of(i // 8))
                        g = f["A"] + i
                        dve.wait_ge(psA_full, g + 1)
                        dve.tensor_reduce(stats[:, 32 + i:33 + i], psA[g % 3][:, 0:n], AX.X,
                                          ALU.min).then_inc(bias_ready, 1)
                    if a == 0:
                        for _ in range(3):
                            tap()
                    if 1 <= i <= NS:
                        s = i - 1
                        n = P * len(keys_of(s // 8))
                        g = tgroup(a, s)
                        dve.wait_ge(psT_full, g + 1)
                        if s >= 2:
                            dve.wait_ge(*pv_signal(a, s - 2))
                        dve.tensor_copy(cfg["PT"][:, s % 2, 0:n], psT[g % 2][:, 0:n]).then_inc(psT_free, 1)
                    if i >= 2 and (i - 2) % per == per - 1:
                        rows_ready(a, (i - 2) // per)
                    if i in (otile_at(0), otile_at(1)):
                        o_low(a, i // 8 - 1)
                o_low(a, NT - 1)

            def o_low(a, t):
                k = otgroup(a, t)
                c = slice(cfg_ft(a), cfg_ft(a) + 4)
                lows[0] += 1
                dve.wait_ge(hT_hi, lows[0])
                link(dve.tensor_tensor(hTl[:, c, t * P:(t + 1) * P],
                                       psT[k % 2][:, :].rearrange("p (f n) -> p f n", f=4),
                                       hTh[:, c, t * P:(t + 1) * P].bitcast(F32), ALU.subtract))
                nothing().then_inc(psT_free, 1)
                nothing().then_inc(hT_lo, 1)

            def cfg_ft(a):
                return ATT[a]["ft"]

            def rows_ready(a, m):
                cfg, f = ATT[a], first[f"attend{a}"]
                per, n = cfg["per"], cfg["n"]
                t = m * per // 8
                g = f["B"] + m
                dve.wait_ge(psB_full, g + 1)
                dve.wait_ge(psA_free, f["A"] + (m + 1) * per)
                link(dve.reciprocal(stats[:, 16:16 + per], stats[:, 64 + m * per:64 + (m + 1) * per]))
                r = stats[:, 16:16 + per].unsqueeze(2).to_broadcast([P, per, n])
                src = psB[g % 3][:, :].rearrange("p (h d) -> p h d", h=per)
                if NT * a + t >= 1 and (a != 1 or m % 2 == 0):
                    pa, pt = divmod(NT * a + t - 1, NT)
                    dve.wait_ge(psT_full, otgroup(pa, pt) + 1)
                if a != 1:
                    dve.tensor_tensor(otok.rearrange("p (h d) -> p h d", h=per), src, r, ALU.mult).then_inc(psB_free, 1)
                    dve.wait_ge(psB_free, g + 1)
                    nothing().then_inc(o_ready, 1)
                    return
                o4 = osb.rearrange("p (h j d) -> p h j d", h=2, j=2)
                dve.tensor_tensor(osb.rearrange("p (h d) -> p h d", h=per), src, r, ALU.mult).then_inc(psB_free, 1)
                dve.wait_ge(psB_free, g + 1)
                o2 = od.rearrange("p (h d) -> p h d", h=2)
                link(dve.scalar_tensor_tensor(out=o2, in0=o4[:, :, 1, :], scalar=stats[:, 92:93], in1=o4[:, :, 0, :],
                                              op0=ALU.mult, op1=ALU.add))
                sq = scr[:, 0:256].rearrange("p (h d) -> p h d", h=2)
                link(dve.tensor_tensor(sq, o2, o2, ALU.mult))
                ask_root(dve.tensor_reduce(stats[:, 10:12], sq, AX.X, ALU.add))
                link(dve.reciprocal(stats[:, 14:16], stats[:, 12:14]))
                link(dve.scalar_tensor_tensor(out=o2, in0=o2, scalar=1.0 - LAMBDA_INIT,
                                              in1=stats[:, 14:16].unsqueeze(2).to_broadcast([P, 2, P]),
                                              op0=ALU.mult, op1=ALU.mult))
                half = m % 2
                ins = dve.tensor_tensor(otok[:, half * 256:(half + 1) * 256].rearrange("p (h d) -> p h d", h=2), o2,
                                        G["l1_diff_subln_g"].unsqueeze(1).to_broadcast([P, 2, P]), ALU.mult)
                if half == 1:
                    ins.then_inc(o_ready, 1)
                else:
                    link(ins)

            def gated(g, t, j, gate, y0, i=0):
                n = y0 + NT * j + t
                if n - 2 > 0:
                    dve.wait_ge(x_added, n - 2 + 12 * i)
                dve.wait_ge(psB_full, g + 1 + 24 * i)
                gb = gate_b[:, gate, 0 if t == 0 else 1, j * YN:(j + 1) * YN]
                dve.tensor_tensor(ytmp[:, t, :], psB[g % 3][:, 0:YN], gb, ALU.mult).then_inc(psB_free, 1)

            def out_projection(l, y0):
                for j in range(YC):
                    step(base["out", l] + j)
                    for t in range(NT):
                        gated(first["out", l]["B"] + NT * j + t, t, j, 0, y0)

            def ffn(l, y0, h0):
                u0, f = base["ffn", l], first["ffn", l]

                def gate_tiles(j, i):
                    for q in TGROUPS.get(j, ()):
                        dve.wait_ge(gT_hi, h0 + q + 1 + FT * i)
                        dve.tensor_tensor(gTl[:, q, :], psT[q % 2][:, 0:TOK], gTh[:, q, :].bitcast(F32),
                                          ALU.subtract).then_inc(psT_free, 1)

                with dve.Fori(0, 2) as i:
                    for j in range(3 * FC):
                        if j == 2 * FC:
                            gate_tiles(j, i)
                        split_lo(u0 + j + AHEAD, i)
                        if j < 2 * FC and j % 2:
                            c = j // 2
                            for t in range(NT):
                                g = f["B"] + NT * c + t
                                dve.wait_ge(psA_free, f["A"] + NT * c + t + 1 + 12 * i)
                                dve.wait_ge(psB_full, g + 1 + 24 * i)
                                dst = gt[:, t, c * FN:(c + 1) * FN]
                                dve.tensor_tensor(dst, dst, psB[g % 3][:, 0:FN], ALU.mult).then_inc(psB_free, 1)
                        if j < 2 * FC:
                            gate_tiles(j, i)
                        else:
                            for t in range(NT):
                                gated(f["B"] + 12 + NT * (j - 2 * FC) + t, t, j - 2 * FC, 1, y0, i)

            link(dve.memset(chl[:, :, :].bitcast(F32), 0.0))
            dve.wait_ge(psT_full, 2)
            dve.tensor_copy(vecs[:, :], psT[0][:, 0:60]).then_inc(psT_free, 1)
            dve.tensor_copy(dww[:, :], psT[1][:, 0:CW * CT]).then_inc(psT_free, 1)
            dve.wait_ge(c_silu, 1)
            for c in range(2):
                cs = csil[:, c * KD:(c + 1) * KD]
                link(dve.tensor_copy(chl[:, :, 2 * c], cs))
                ins = dve.tensor_tensor(chl[:, :, 2 * c + 1], cs, chl[:, :, 2 * c].bitcast(F32), ALU.subtract)
                if c == 0:
                    link(ins)
            ins.then_inc(c_ready, 1)
            for u in range(AHEAD):
                split_lo(u)

            ada(0)
            norm(0, 0)
            for j in range(QKV0):
                u = base["in", 0] + j
                step(u)
                for t in range(NT):
                    g = first["in0"]["B"] + NT * j + t
                    if j < 2:
                        dve.wait_ge(psB_full, g + 1)
                        dve.tensor_copy(zq[:, t, 0:512].rearrange("p (h k d) -> p h k d", h=4, k=2)[:, :, j, :],
                                        psB[g % 3][:, 0:256].rearrange("p (h d) -> p h d", h=4)).then_inc(psB_free, 1)
                    else:
                        columns_out(u, g, zq[:, t, 512:768])
            dve.wait_ge(gains_in, 16 * len(G))
            dve.wait_ge(pool_chain, 1)
            for j in range(CT):
                if j < CT - 1:
                    step(base["in", 0] + QKV0 + j)
                if j < NT:
                    dve.wait_ge(psB_free, first["in0"]["B"] + NT * QKV0)
                    z = rms_item(0, j)
                    scaled(z[:, 0:8, :], 8, HD, 0, G["l0_q_norm_g"], -(HD ** -0.5))
                    scaled(z[:, 8:10, :], 2, HD, 8, G["l0_k_norm_g"])
                    (rope(z, 10, HD, j, C_COS, C_SIN) if j else nothing()).then_inc(z_ready, 1)
                    dve.wait_ge(z_ready, j + 1)
                g = first["in0"]["B"] + NT * QKV0 + j
                dve.wait_ge(psA_free, first["in0"]["A"] + j + 1)
                dve.wait_ge(psB_full, g + 1)
                for at, tok, n in CSEG:
                    ins = dve.tensor_tensor(cpad[:, j, at:at + n], psB[g % 3][:, tok:tok + n],
                                            hf[:, j % 2, tok:tok + n], ALU.mult)
                    if tok == 0:
                        link(ins)
                ins.then_inc(psB_free, 1)
            dve.wait_ge(psB_free, first["in0"]["B"] + NT * QKV0 + CT)
            attend(0)
            while taps[0] < CW * CT_V:
                tap()
            dve.wait_ge(conv_chain, CW * CT_V)
            dve.wait_ge(conv_chain_p, (CW - 1) * (CT - CT_V))
            nothing().then_inc(ln_in, 1)
            g = first["lnorm"]["B"]
            dve.wait_ge(psB_full, g + 1)
            for c in range(CT):
                ins = dve.tensor_tensor(yc[:, c, :], yc[:, c, :], psB[g % 3][:, 0:COUT], ALU.subtract)
                if c < CT - 1:
                    link(ins)
            ins.then_inc(psB_free, 1)
            dve.wait_ge(psB_free, g + 1)
            for c in range(CT):
                ins = dve.tensor_tensor(cpad[:, c, 0:COUT], yc[:, c, :], yc[:, c, :], ALU.mult)
                if c < CT - 1:
                    link(ins)
            ins.then_inc(ln_in, 1)
            g += 1
            dve.wait_ge(psB_full, g + 1)
            link(dve.tensor_copy(hf[:, 0, 0:P], psB[g % 3][:, 0:P]))
            dve.tensor_copy(hf[:, 0, P:TOK], psB[g % 3][:, 2 * PAD + P:COUT]).then_inc(psB_free, 1)
            dve.wait_ge(psB_free, g + 1)
            ask_root(nothing())
            link(dve.reciprocal(hf[:, 0, :], hf[:, 1, :]))
            for c in range(CT):
                link(dve.tensor_tensor(yv(c)[:, 0:P], yc[:, c, 0:P], hf[:, 0, 0:P], ALU.mult))
                dve.tensor_tensor(yv(c)[:, P:TOK], yc[:, c, 2 * PAD + P:COUT], hf[:, 0, P:TOK],
                                  ALU.mult).then_inc(ln_out, 1)
            for c in range(CT):
                low(hTl[:, c, :], ysil[:, c, :], hTh[:, c, :])
            step(base["out", 0] - 1)
            for kept in rows_kept:
                dve.wait_ge(kept, 16 * ASIDE // 2)
            out_projection(0, 0)
            norm(0, 1)
            dve.wait_ge(state_out, 32)
            ffn(0, 12, 0)

            dve.wait_ge(x_added, 36)
            for n, (q, k) in enumerate((("l1_lambda_q1", "l1_lambda_k1"), ("l1_lambda_q2", "l1_lambda_k2"))):
                link(dve.tensor_tensor(scr[:, 0:HD], G[q], G[k], ALU.mult))
                ins = dve.tensor_reduce(stats[:, 88 + n:89 + n], scr[:, 0:HD], AX.X, ALU.add)
                if n == 0:
                    link(ins)
            ins.then_inc(lam_in, 1)
            norm(1, 0)

            def item1(m):
                t = m % NT
                z = rms_item(1, m)
                if m < NT:
                    scaled(z, 8, HD, 0, G["l1_diff_q_norm_g"], -(HD ** -0.5))
                else:
                    scaled(z, 8, HD, 0, G["l1_diff_k_norm_g"])
                (rope(z, 8, HD, t, C_COS, C_SIN) if t else nothing()).then_inc(z_ready, 1)
                dve.wait_ge(z_ready, Z1 + m + 1)

            for j in range(8):
                u = base["in", 1] + j
                step(u)
                dve.wait_ge(psB_free, first["in1"]["B"] + NT * j)
                if j in (1, 2):
                    at, n, name = ((0, QR, "l1_mla_q_a_norm_g"), (QR, KVR, "l1_mla_kv_a_norm_g"))[j - 1]
                    z = zm[:, :, at:at + n]
                    rms_heads(z, NT, n)
                    scaled(z, NT, n, 0, G[name])
                    if j == 2:
                        nothing().then_inc(z_ready, 1)
                if j == 3:
                    dve.wait_ge(lam_e, 1)
                    link(dve.tensor_tensor(stats[:, 93:94], stats[:, 91:92], stats[:, 90:91], ALU.subtract))
                    link(dve.tensor_scalar(stats[:, 92:93], stats[:, 93:94], -LAMBDA_INIT, None, ALU.add))
                if j in ITEM_AT:
                    item1(ITEM_AT[j])
                for t in range(NT):
                    dst = zd[:, t, (j - 2) * 256:(j - 1) * 256] if j >= 2 else (
                        zm[:, t, 0:256] if j == 0 else zm[:, t, 256:416])
                    columns_out(u, first["in1"]["B"] + NT * j + t, dst)
            dve.wait_ge(psB_free, first["in1"]["B"] + 24)
            g0 = first["latT"]["T"]
            for q in range(3):
                g = g0 + q
                n = TOK if q < 2 else 4 * P
                dst, hi = ((hTl[:, 4 + q, :], hTh[:, 4 + q, :]) if q < 2 else (ckvT(hTl), ckvT(hTh)))
                lows[0] += 1
                dve.wait_ge(hT_hi, lows[0])
                link(dve.tensor_tensor(dst, psT[g % 2][:, 0:n], hi.bitcast(F32), ALU.subtract))
                nothing().then_inc(psT_free, 1)
                nothing().then_inc(hT_lo, 1)
            item1(4)
            item1(5)
            attend(1)
            dve.wait_ge(state_out, 64)
            b0 = first["lat"]["B"]
            for j in range(4):
                u = base["lat", 1] + j
                step(u)
                for t in range(NT if j < 2 else 4):
                    if j < 2:
                        columns_out(u, b0 + NT * j + t, qm[:, t, j * 384:(j + 1) * 384])
                    else:
                        columns_out(u, b0 + 2 * NT + 4 * (j - 2) + t, kv[:, t, (j - 2) * 512:(j - 1) * 512])
            dve.wait_ge(psB_free, b0 + 14)
            g0 = first["prep2"]["T"]
            request = sums_item(2, 0)
            for m in range(7):
                t = m if m < NT else m - NT
                name, factor = ("l1_mla_q_norm_g", -(QK ** -0.5)) if m < NT else ("l1_mla_k_norm_g", 1.0)
                z, at = heads_of(2, m)[0], MLA_H * (m % 2)
                dve.wait_ge(root, request)
                link(dve.reciprocal(stats[:, RC + at:RC + at + MLA_H], stats[:, RT + at:RT + at + MLA_H]))
                over_rms(z, MLA_H, QK, at, factor)
                if m < 6:
                    request = sums_item(2, m + 1, MLA_H * ((m + 1) % 2))
                link(dve.tensor_tensor(z, z, G[name].unsqueeze(1).to_broadcast([P, MLA_H, QK]), ALU.mult))
                (rope(z[:, :, NOPE:QK], MLA_H, ROPE, t, C_COSR, C_SINR) if t in (1, 2) else nothing()
                 ).then_inc(z_ready, 1)
                dve.wait_ge(z_ready, Z2 + m + 1)
            attend(2)
            dve.wait_ge(gates_back, 16 * 4)
            out_projection(1, 36)
            norm(1, 1)
            step(base["router"])
            g = first["router"]["B"]
            dve.wait_ge(psB_full, g + NT)
            for t in range(NT):
                b = psB[(g + t) % 3][:, 0:NE]
                link(dve.max(mx8[:, t, :], b))
                dve.max_index(ix8[:, t, :], mx8[:, t, :], b).then_inc(psB_free, 1)
            dve.wait_ge(psB_free, g + NT)
            link(dve.tensor_copy(ix8f[:, :, :], ix8[:, :, :]))
            dve.tensor_tensor(rt[:, 0:3], mx8[:, :, 1], mx8[:, :, 0], ALU.subtract).then_inc(router_in, 1)
            dve.wait_ge(logit_e, 1)
            link(dve.tensor_scalar(rt[:, 8:11], rt[:, 4:7], 1.0, None, ALU.add))
            link(dve.reciprocal(rt[:, 12:15], rt[:, 8:11]))
            link(dve.tensor_tensor(rt[:, 16:19], rt[:, 12:15], rt[:, 4:7], ALU.mult))
            iota = cst[:, C_IOTA:C_IOTA + NE]
            for t in range(NT):
                link(dve.tensor_scalar(rt[:, 40:48], iota, ix8f[:, t, 0:1], None, ALU.is_equal))
                link(dve.scalar_tensor_tensor(out=mask[:, t, :], in0=iota, scalar=ix8f[:, t, 1:2], in1=rt[:, 40:48],
                                              op0=ALU.is_equal, op1=ALU.add))
                link(dve.tensor_scalar(rt[:, 24:32], rt[:, 40:48], rt[:, 12 + t:13 + t], None, ALU.mult))
                link(dve.tensor_scalar(rt[:, 32:40], iota, ix8f[:, t, 1:2], rt[:, 16 + t:17 + t],
                                       ALU.is_equal, ALU.mult))
                link(dve.tensor_tensor(comb[:, t, :], rt[:, 24:32], rt[:, 32:40], ALU.add))
            nothing().then_inc(mask_ready, 1)
            g = first["tables"]["B"]
            dve.wait_ge(psB_full, g + 1)
            all_places = slot[:, :, 0:NE]
            link(dve.tensor_tensor(all_places, psB[g % 3][:, 0:NT * NE].rearrange("p (t e) -> p t e", t=NT),
                                   mask[:, :, :], ALU.mult))
            link(dve.tensor_scalar(all_places, all_places, -1.0, None, ALU.add))
            dve.tensor_copy(jobs[:, 0:NE], psB[g % 3][:, NT * NE:(NT + 1) * NE]).then_inc(psB_free, 1)
            dve.wait_ge(psB_free, g + 1)
            f = first["jobs"]

            def choose(e, n, start, p):
                if isinstance(e, int):
                    src = slot[:, :, e]
                else:
                    src = slot[:, :, bass.ds(e, 1)].rearrange("p t e -> p (t e)")
                dve.tensor_scalar(slot_e[:, p or 0, :], src, start, None, ALU.subtract).then_inc(place_ready, 1)
                dve.wait_ge(place_ready, n + 1)
                for t in range(NT):
                    ins = dve.tensor_scalar(pick[:, t, chosen(p)], jcst[:, 2 * P:3 * P], slot_e[:, p or 0, t:t + 1],
                                            None, ALU.is_equal)
                    ins.then_inc(pick_ready if t == NT - 1 and p != 0 else pick_part, 1)

            dve.wait_ge(jcst_in, 16)
            choose(0, 0, 0.0, 0)
            choose(1, 1, 0.0, 1)
            for q in range(2 * NT):
                g = first["tokens"]["B"] + q
                dve.wait_ge(psB_full, g + 1)
                dve.tensor_copy(toks_l[:, q // 2, q % 2 * 512:(q % 2 + 1) * 512], psB[g % 3][:, :]).then_inc(psB_free, 1)

            def split_half(h, n):
                dve.wait_ge(half_hi, h + 1 + HALVES * n)
                dve.tensor_tensor(half_of(Wl, h), half_of(raw, h), half_of(Wh, h).bitcast(F32),
                                  ALU.subtract).then_inc(half_lo, 1)

            def turned(j, n):
                for g, tiles in JT.get(j, ()):
                    k = len(tiles)
                    dve.wait_ge(gT_hi, 2 * FT + g + (JOB_T - 1) * n)
                    c = slice(tiles[0], tiles[-1] + 1)
                    dve.tensor_tensor(mTl[:, c, :], psT[g % 2][:, 0:P * k].rearrange("p (f n) -> p f n", f=k),
                                      mTh[:, c, :].bitcast(F32), ALU.subtract).then_inc(psT_free, 1)

            def job(i, p):
                n = job_number(i, p)
                if p is not None:
                    e = n
                else:
                    e = dve.value_load(jobs_i[0:1, bass.ds(i + 1, 1)], min_val=0, max_val=NE - 1)
                    for h in range(HSLOTS - 1):
                        split_half(h, n)
                    choose(e, n, jobs[:, bass.ds(i + 88, 1)], None)
                for h in range(HALVES):
                    ahead = h + HSLOTS - 1
                    if h in URGENT_V:
                        results(h, n)
                    if ahead < HALVES:
                        split_half(ahead, n)
                    elif p == 0:
                        split_half(ahead - HALVES, n + 1)
                    elif p == 1:
                        with dve.If(i < NE // 2 - 1):
                            split_half(ahead - HALVES, n + 1)
                    if h == 4:
                        dve.wait_ge(back_free, BACKS * n + BACKS)
                        dve.tensor_copy(comb_e[:, :], comb[:, :, bass.ds(e, 1)].rearrange("p t e -> p (t e)")
                                        ).then_inc(comb_ready, 1)
                    if h == 1:
                        dve.wait_ge(psT_full, f["T"] + 1 + JOB_T * n)
                        dve.tensor_copy(pickT[:, :], psT[0][:, 0:TOK]).then_inc(psT_free, 1)
                    if h == 8 and p == 1:
                        with dve.If(i < NE // 2 - 1):
                            choose(n + 1, n + 1, 0.0, 0)
                            choose(n + 2, n + 2, 0.0, 1)
                    if h not in URGENT_V:
                        results(h, n)

            def results(h, n):
                j = h // 2
                if h == 4 * FC:
                    turned(j, n)
                elif h % 2 and j < 2 * FC and j % 2:
                    c = j // 2
                    dve.wait_ge(psA_free, f["A"] + c + 1 + JOB_A * n)
                    dve.wait_ge(psB_full, f["B"] + c + 1 + JOB_B * n)
                    dst = gj[:, c * FN:(c + 1) * FN]
                    dve.tensor_tensor(dst, dst, job_bank(c)[:, 0:FN], ALU.mult).then_inc(psB_free, 1)
                elif h % 2 and j < 2 * FC:
                    turned(j, n)
                elif h % 2:
                    c = j - 2 * FC
                    dve.wait_ge(y_hi, c + 1 + YC * n)
                    dve.tensor_tensor(yl[:, c % 2, :], job_bank(W2_AT[c])[:, 0:YN], yh[:, c % 2, :].bitcast(F32),
                                      ALU.subtract).then_inc(psB_free, 1)

            for h in range(HSLOTS - 1):
                split_half(h, 0)
            link(dve.tensor_scalar(jobs[:, 8:16], jobs[:, 0:8], P + 0.5, None, ALU.is_gt))
            link(dve.scalar_tensor_tensor(out=jobs[:, 16:24], in0=jobs[:, 0:8], scalar=2 * P + 0.5,
                                          in1=jobs[:, 8:16], op0=ALU.is_gt, op1=ALU.add))
            for e in range(1, NE):
                link(dve.tensor_tensor(jobs[:, 16 + e:17 + e], jobs[:, 15 + e:16 + e], jobs[:, 16 + e:17 + e],
                                       ALU.add))
            run = jobs[:, 16:24].unsqueeze(1).to_broadcast([P, EXTRA, NE])
            below = jobs[:, 24:24 + EXTRA * NE].rearrange("p (j e) -> p j e", j=EXTRA)
            link(dve.tensor_tensor(below, run, iota[:, 0:EXTRA].unsqueeze(2).to_broadcast([P, EXTRA, NE]),
                                   ALU.is_le))
            link(dve.tensor_copy(jobs[:, 64:65], jobs[:, 23:24]))
            link(dve.tensor_reduce(jobs[:, 65:65 + EXTRA], below, AX.X, ALU.add))
            link(dve.tensor_scalar(jobs[:, 65:65 + EXTRA], jobs[:, 65:65 + EXTRA], NE - 1.0, None, ALU.min))
            link(dve.tensor_tensor(below, below, run, ALU.mult))
            link(dve.tensor_reduce(jobs[:, 72:72 + EXTRA], below, AX.X, ALU.max))
            link(dve.tensor_tensor(jobs[:, 80:80 + EXTRA], iota[:, 0:EXTRA], jobs[:, 72:72 + EXTRA], ALU.subtract))
            link(dve.tensor_scalar(jobs[:, 88:88 + EXTRA], jobs[:, 80:80 + EXTRA], float(P), float(P),
                                   ALU.mult, ALU.add))
            dve.tensor_copy(jobs_i[:, 0:1 + EXTRA], jobs[:, 64:65 + EXTRA]).then_inc(table_ready, 1)
            more = over_jobs(dve, job)
            for c in range(YC):
                cols = slice(c * YN, (c + 1) * YN)
                dve.wait_ge(y_added, BACKS * (NE - 1) + 6 + NT * c + BACKS * more)
                link(dve.tensor_tensor(yq[:, :, cols], yq[:, :, cols],
                                       gate_b[:, 1, 1, cols].unsqueeze(1).to_broadcast([P, 2, YN]), ALU.mult))
                dve.tensor_tensor(x[:, 1:NT, cols], x[:, 1:NT, cols], yq[:, :, cols], ALU.add).then_inc(x_done_q, 1)


_OUTS = [(1, P, D), (1, 2 * P, D), (1, P, 2, HD), (1, P, 2, HD), (1, P, 4, 2, HD), (1, P, 4, 2 * HD),
         (1, P, KVR), (1, P, ROPE)]


def kernel(**inputs):
    import concourse.bacc as _bacc
    from concourse.bass_utils import run_bass_kernel_spmd as _run

    nc = _bacc.Bacc("TRN2", target_bir_lowering=False, num_devices=1)
    arrays = {f"in_{n}": np.ascontiguousarray(a) for n, a in inputs.items()}
    arrays["in_consts"] = constants()
    arrays["in_job_consts"] = job_constants()
    A = {n[3:]: nc.dram_tensor(n, a.shape, mybir.dt.from_np(a.dtype), kind="ExternalInput").ap()
         for n, a in arrays.items()}
    out = [nc.dram_tensor(f"out_{i}", s, F32, kind="ExternalOutput").ap() for i, s in enumerate(_OUTS)]
    trunk_step(nc, A, out)
    r = _run(nc, [arrays], core_ids=[0])
    return tuple(r.results[0][f"out_{i}"] for i in range(len(_OUTS)))
```
